# Optimizing a Trainium2 kernel written in Bass

```python
import jax, jax.numpy as jnp
from jax import lax
import numpy as np

D_MODEL = 1024
BATCH = 1
SEQ = 512
DEPTH = 2
DEC_BATCH = 8
DEC_SEQ = 4
PAST_LEN = 2048
PAGE_SIZE = 128

D_RNN = D_MODEL // 2
RG_BLOCKS = 8
RG_BLOCK_W = D_RNN // RG_BLOCKS
RG_CONV = 4
RG_C = 8.0
N_HEADS = 8
HEAD_DIM = (D_MODEL // 2) // N_HEADS
N_KV = 2
GROUP = N_HEADS // N_KV
KV_DIM = N_KV * HEAD_DIM
CMP_STRIDE = 16
CMP_BLOCK = 2 * CMP_STRIDE
CMP_HIDDEN = 2 * HEAD_DIM
SLC_BLOCK = 64
N_SELECT = 16
N_LOCAL = 2
WINDOW = 512
Q_BLOCK = 128
D_FF = 3 * D_MODEL
FFN_CONV = 3
ROPE_THETA = 10000.0
EPS = 1e-6
N_IN = 2 * D_RNN + N_HEADS * HEAD_DIM + 6 * KV_DIM + 3 * N_HEADS

kernel_name = 'hymba_rglru_nsa_convffn_step'

def _rms(x, g):
    x32 = x.astype(jnp.float32)
    y = x32 * lax.rsqrt(jnp.mean(x32 * x32, axis=-1, keepdims=True) + EPS)
    return (y * g.astype(jnp.float32)).astype(x.dtype)

def _rope(x, pos):
    half = HEAD_DIM // 2
    freq = ROPE_THETA ** (-jnp.arange(half, dtype=jnp.float32) / half)
    ang = pos.astype(jnp.float32)[:, None] * freq[None, :]
    shape = (1, pos.shape[0]) + (1,) * (x.ndim - 3) + (half,)
    cos, sin = jnp.cos(ang).reshape(shape), jnp.sin(ang).reshape(shape)
    x32 = x.astype(jnp.float32)
    x1, x2 = x32[..., :half], x32[..., half:]
    return jnp.concatenate([x1 * cos - x2 * sin, x2 * cos + x1 * sin], axis=-1).astype(x.dtype)

def _causal_dwconv(x, prefix, w, b):
    width, t = w.shape[0], x.shape[1]
    xp = jnp.concatenate([prefix.astype(x.dtype), x], axis=1)
    y = b
    for k in range(width):
        y = y + xp[:, k:k + t] * w[k]
    return y, xp[:, t:]

def _masked_softmax(s, mask):
    s = jnp.where(mask, s.astype(jnp.float32), -jnp.inf)
    m = jnp.max(s, axis=-1, keepdims=True)
    m = jnp.where(jnp.isfinite(m), m, 0.0)
    e = jnp.where(mask, jnp.exp(s - m), 0.0)
    return e / jnp.maximum(jnp.sum(e, axis=-1, keepdims=True), 1e-30)

def _compress(rows, pe, w1, b1, w2):
    bsz, length = rows.shape[:2]
    n = length // CMP_STRIDE
    ch = rows[:, :n * CMP_STRIDE].reshape(bsz, n, CMP_STRIDE, N_KV, HEAD_DIM)
    ua = jnp.einsum('bnshd,sdf->bnhf', ch + pe[:CMP_STRIDE, None, :], w1[:CMP_STRIDE])
    ub = jnp.einsum('bnshd,sdf->bnhf', ch + pe[CMP_STRIDE:, None, :], w1[CMP_STRIDE:])
    hid = jax.nn.gelu(ua[:, :-1] + ub[:, 1:] + b1)
    return jnp.einsum('bnhf,fd->bnhd', hid, w2)

def _cmp_to_slc(p, n_slc):
    r = SLC_BLOCK // CMP_STRIDE
    c = p.shape[-1]
    pp = jnp.pad(p, [(0, 0)] * (p.ndim - 1) + [(1, r * n_slc - c)])
    return pp[..., :r * n_slc].reshape(p.shape[:-1] + (n_slc, r)).sum(-1) + pp[..., r:r * n_slc + 1:r]

def _slc_blocks(rows):
    bsz, length = rows.shape[:2]
    n = -(-length // SLC_BLOCK)
    rows = jnp.pad(rows, ((0, 0), (0, n * SLC_BLOCK - length), (0, 0), (0, 0)))
    return rows.reshape(bsz, n, SLC_BLOCK, N_KV, HEAD_DIM).transpose(0, 3, 1, 2, 4)

def _nsa_core(q_c, q_r, q_pos, kc, vc, c_end, ks_blk, vs_blk, kw, vw, w_pos, gates):
    bsz, t = q_c.shape[:2]
    n_slc = ks_blk.shape[2]
    scale = HEAD_DIM ** -0.5
    s = jnp.einsum('bthgd,bchd->bthgc', q_c, kc) * scale
    mc = (c_end[None, :] <= q_pos[:, None])[None, :, None, None, :]
    p_cmp = _masked_softmax(s, mc)
    o_cmp = jnp.einsum('bthgc,bchd->bthgd', p_cmp.astype(vc.dtype), vc)
    score = _cmp_to_slc(p_cmp.sum(axis=3), n_slc)
    blk = jnp.arange(n_slc)
    lag = (q_pos // SLC_BLOCK)[:, None] - blk[None, :]
    forced = (blk[None, :] == 0) | ((lag >= 0) & (lag < N_LOCAL))
    score = jnp.where(forced[None, :, None, :], jnp.inf, score)
    score = jnp.where((lag >= 0)[None, :, None, :], score, -jnp.inf)
    k_sel = min(N_SELECT, n_slc)
    _, idx = lax.top_k(score, k_sel)
    idx_h = idx.transpose(0, 2, 1, 3)
    flat = idx_h.reshape(bsz, N_KV, t * k_sel)
    take = jax.vmap(jax.vmap(lambda blocks, ix: blocks[ix]))
    gk = take(ks_blk, flat).reshape(bsz, N_KV, t, k_sel, SLC_BLOCK, HEAD_DIM)
    gv = take(vs_blk, flat).reshape(bsz, N_KV, t, k_sel, SLC_BLOCK, HEAD_DIM)
    tok = idx_h[..., None] * SLC_BLOCK + jnp.arange(SLC_BLOCK)
    ms = (tok <= q_pos[None, None, :, None, None]).transpose(0, 2, 1, 3, 4)
    ms = ms.reshape(bsz, t, N_KV, 1, k_sel * SLC_BLOCK)
    s = jnp.einsum('bthgd,bhtkld->bthgkl', q_r, gk) * scale
    p = _masked_softmax(s.reshape(bsz, t, N_KV, GROUP, k_sel * SLC_BLOCK), ms).reshape(s.shape)
    o_slc = jnp.einsum('bthgkl,bhtkld->bthgd', p.astype(gv.dtype), gv)
    s = jnp.einsum('bthgd,bshd->bthgs', q_r, kw) * scale
    dist = q_pos[:, None] - w_pos[None, :]
    mw = ((dist >= 0) & (dist < WINDOW) & (w_pos[None, :] >= 0))[None, :, None, None, :]
    p = _masked_softmax(s, mw)
    o_win = jnp.einsum('bthgs,bshd->bthgd', p.astype(vw.dtype), vw)
    return gates[..., 0:1] * o_cmp + gates[..., 1:2] * o_slc + gates[..., 2:3] * o_win

def _project(h, w_in):
    sizes = [D_RNN, D_RNN, N_HEADS * HEAD_DIM, 2 * KV_DIM, 2 * KV_DIM, 2 * KV_DIM, 3 * N_HEADS]
    cuts = np.cumsum(sizes)[:-1].tolist()
    xr, gate, q, kvc, kvs, kvw, gl = jnp.split(h @ w_in, cuts, axis=-1)
    bsz, t = h.shape[:2]
    kv = lambda z: z.reshape(bsz, t, 2, N_KV, HEAD_DIM)
    gates = jax.nn.sigmoid(gl.astype(jnp.float32)).astype(h.dtype).reshape(bsz, t, N_KV, GROUP, 3)
    return xr, gate, q.reshape(bsz, t, N_KV, GROUP, HEAD_DIM), kv(kvc), kv(kvs), kv(kvw), gates

def _rglru(xr, gate, conv_prefix, h0, lp):
    xc, conv_state = _causal_dwconv(xr, conv_prefix, lp['rg_conv_w'], lp['rg_conv_b'])
    bsz, t = xc.shape[:2]
    xb = xc.reshape(bsz, t, RG_BLOCKS, RG_BLOCK_W)
    r = jax.nn.sigmoid(jnp.einsum('btnc,ncd->btnd', xb, lp['rg_wa']).reshape(bsz, t, D_RNN) + lp['rg_ba'])
    i = jax.nn.sigmoid(jnp.einsum('btnc,ncd->btnd', xb, lp['rg_wx']).reshape(bsz, t, D_RNN) + lp['rg_bx'])
    log_a = RG_C * r.astype(jnp.float32) * jax.nn.log_sigmoid(lp['rg_lambda'].astype(jnp.float32))
    a = jnp.exp(log_a)
    b = jnp.sqrt(-jnp.expm1(2.0 * log_a)) * (i * xc).astype(jnp.float32)
    b = b.at[:, 0].add(a[:, 0] * h0.astype(jnp.float32))
    comb = lambda e, l: (e[0] * l[0], l[0] * e[1] + l[1])
    _, hseq = lax.associative_scan(comb, (a, b), axis=1)
    y = (hseq * jax.nn.gelu(gate.astype(jnp.float32))).astype(xr.dtype)
    return y, conv_state, hseq[:, -1].astype(h0.dtype)

def _ffn(h, prefix, lp):
    u, g = jnp.split(h @ lp['ffn_w_in'], 2, axis=-1)
    gc, state = _causal_dwconv(g, prefix, lp['ffn_conv_w'], lp['ffn_conv_b'])
    return (jax.nn.gelu(gc) * u) @ lp['ffn_w_down'], state

def _merge(y_rnn, o, lp):
    bsz, t = y_rnn.shape[:2]
    o = o.reshape(bsz, t, N_HEADS * HEAD_DIM).astype(y_rnn.dtype)
    return jnp.concatenate([y_rnn, o], axis=-1) @ lp['w_out']

def _mixer_prompt(h, lp):
    bsz, t = h.shape[:2]
    xr, gate, q, kvc, kvs, kvw, gates = _project(h, lp['w_in'])
    y_rnn, rg_conv, rg_h = _rglru(xr, gate, jnp.zeros((bsz, RG_CONV - 1, D_RNN), h.dtype),
                                  jnp.zeros((bsz, D_RNN), h.dtype), lp)
    pos = jnp.arange(t)
    q_r = _rope(q, pos)
    kc = _compress(kvc[:, :, 0], lp['cmpk_pe'], lp['cmpk_w1'], lp['cmpk_b1'], lp['cmpk_w2'])
    vc = _compress(kvc[:, :, 1], lp['cmpv_pe'], lp['cmpv_w1'], lp['cmpv_b1'], lp['cmpv_w2'])
    c_end = jnp.arange(kc.shape[1]) * CMP_STRIDE + CMP_BLOCK - 1
    kvs_rows = jnp.stack([_rope(kvs[:, :, 0], pos), kvs[:, :, 1]], axis=2)
    ks_blk, vs_blk = _slc_blocks(kvs_rows[:, :, 0]), _slc_blocks(kvs_rows[:, :, 1])
    kvw_rows = jnp.stack([_rope(kvw[:, :, 0], pos), kvw[:, :, 1]], axis=2)
    kvw_pad = jnp.pad(kvw_rows, ((0, 0), (WINDOW, 0), (0, 0), (0, 0), (0, 0)))

    def one_block(start):
        qs = lambda z: lax.dynamic_slice_in_dim(z, start, Q_BLOCK, axis=1)
        win = lax.dynamic_slice_in_dim(kvw_pad, start, WINDOW + Q_BLOCK, axis=1)
        w_pos = start - WINDOW + jnp.arange(WINDOW + Q_BLOCK)
        q_pos = start + jnp.arange(Q_BLOCK)
        return _nsa_core(qs(q), qs(q_r), q_pos, kc, vc, c_end, ks_blk, vs_blk,
                         win[:, :, 0], win[:, :, 1], w_pos, qs(gates))

    o = lax.map(one_block, jnp.arange(t // Q_BLOCK) * Q_BLOCK)
    o = jnp.moveaxis(o, 0, 1)
    win_buf = min(WINDOW, PAST_LEN)
    win_state = jnp.pad(kvw_rows, ((0, 0), (max(win_buf - t, 0), 0), (0, 0), (0, 0), (0, 0)))[:, -win_buf:]
    return _merge(y_rnn, o, lp), (kvc, kvs_rows, win_state, rg_h, rg_conv)

def _mixer_sample(h, lp, cmp_pool, slc_pool, page_table, win_buf, rg_h0, rg_conv0):
    bsz, t = h.shape[:2]
    xr, gate, q, kvc, kvs, kvw, gates = _project(h, lp['w_in'])
    y_rnn, rg_conv, rg_h = _rglru(xr, gate, rg_conv0, rg_h0, lp)
    pos = PAST_LEN + jnp.arange(t)
    q_r = _rope(q, pos)
    past = lambda pool: pool[page_table].reshape(bsz, -1, 2, N_KV, HEAD_DIM)
    cmp_rows = jnp.concatenate([past(cmp_pool), kvc], axis=1)
    kc = _compress(cmp_rows[:, :, 0], lp['cmpk_pe'], lp['cmpk_w1'], lp['cmpk_b1'], lp['cmpk_w2'])
    vc = _compress(cmp_rows[:, :, 1], lp['cmpv_pe'], lp['cmpv_w1'], lp['cmpv_b1'], lp['cmpv_w2'])
    c_end = jnp.arange(kc.shape[1]) * CMP_STRIDE + CMP_BLOCK - 1
    kvs_rows = jnp.stack([_rope(kvs[:, :, 0], pos), kvs[:, :, 1]], axis=2)
    slc_rows = jnp.concatenate([past(slc_pool), kvs_rows], axis=1)
    ks_blk, vs_blk = _slc_blocks(slc_rows[:, :, 0]), _slc_blocks(slc_rows[:, :, 1])
    kvw_rows = jnp.stack([_rope(kvw[:, :, 0], pos), kvw[:, :, 1]], axis=2)
    win_all = jnp.concatenate([win_buf, kvw_rows], axis=1)
    nb = win_buf.shape[1]
    w_pos = PAST_LEN - nb + jnp.arange(nb + t)
    o = _nsa_core(q, q_r, pos, kc, vc, c_end, ks_blk, vs_blk, win_all[:, :, 0], win_all[:, :, 1], w_pos, gates)
    return _merge(y_rnn, o, lp), (kvc, kvs_rows, win_all[:, -nb:], rg_h, rg_conv)

def setup_inputs(seed: int = 0) -> dict:
    key = jax.random.key(seed)
    ks = iter(jax.random.split(key, 48))
    nrm = lambda shape, scale: scale * jax.random.normal(next(ks), shape, jnp.float32)
    n_pages = PAST_LEN // PAGE_SIZE
    n_used = DEC_BATCH * n_pages
    n_pool = n_used + n_used // 4
    win_buf = min(WINDOW, PAST_LEN)
    row = (2, N_KV, HEAD_DIM)
    page_table = jax.random.permutation(next(ks), n_pool)[:n_used].reshape(DEC_BATCH, n_pages).astype(jnp.int32)
    u = jax.random.uniform(next(ks), (DEPTH, D_RNN), jnp.float32, 0.9, 0.999)
    sa = u ** (1.0 / RG_C)
    rg_lambda = jnp.log(sa) - jnp.log1p(-sa)
    gain = lambda: 1.0 + nrm((DEPTH, D_MODEL), 0.02)
    return {
        'x_prompt': nrm((BATCH, SEQ, D_MODEL), 1.0),
        'x_sample': nrm((DEC_BATCH, DEC_SEQ, D_MODEL), 1.0),
        'cache_cmp_kv': nrm((DEPTH, n_pool, PAGE_SIZE) + row, 1.0),
        'cache_slc_kv': nrm((DEPTH, n_pool, PAGE_SIZE) + row, 1.0),
        'cache_win_kv': nrm((DEPTH, DEC_BATCH, win_buf) + row, 1.0),
        'state_rg_h': nrm((DEPTH, DEC_BATCH, D_RNN), 0.5),
        'state_rg_conv': nrm((DEPTH, DEC_BATCH, RG_CONV - 1, D_RNN), 1.0),
        'state_ffn_conv': nrm((DEPTH, DEC_BATCH, FFN_CONV - 1, D_FF), 1.0),
        'page_table': page_table,
        'norm_mix_pre': gain(),
        'norm_mix_post': gain(),
        'norm_ffn_pre': gain(),
        'norm_ffn_post': gain(),
        'w_in': nrm((DEPTH, D_MODEL, N_IN), D_MODEL ** -0.5),
        'rg_conv_w': nrm((DEPTH, RG_CONV, D_RNN), RG_CONV ** -0.5),
        'rg_conv_b': nrm((DEPTH, D_RNN), 0.01),
        'rg_wa': nrm((DEPTH, RG_BLOCKS, RG_BLOCK_W, RG_BLOCK_W), RG_BLOCK_W ** -0.5),
        'rg_ba': nrm((DEPTH, D_RNN), 0.01),
        'rg_wx': nrm((DEPTH, RG_BLOCKS, RG_BLOCK_W, RG_BLOCK_W), RG_BLOCK_W ** -0.5),
        'rg_bx': nrm((DEPTH, D_RNN), 0.01),
        'rg_lambda': rg_lambda,
        'cmpk_pe': nrm((DEPTH, CMP_BLOCK, HEAD_DIM), 0.1),
        'cmpk_w1': nrm((DEPTH, CMP_BLOCK, HEAD_DIM, CMP_HIDDEN), (CMP_BLOCK * HEAD_DIM) ** -0.5),
        'cmpk_b1': nrm((DEPTH, CMP_HIDDEN), 0.01),
        'cmpk_w2': nrm((DEPTH, CMP_HIDDEN, HEAD_DIM), CMP_HIDDEN ** -0.5),
        'cmpv_pe': nrm((DEPTH, CMP_BLOCK, HEAD_DIM), 0.1),
        'cmpv_w1': nrm((DEPTH, CMP_BLOCK, HEAD_DIM, CMP_HIDDEN), (CMP_BLOCK * HEAD_DIM) ** -0.5),
        'cmpv_b1': nrm((DEPTH, CMP_HIDDEN), 0.01),
        'cmpv_w2': nrm((DEPTH, CMP_HIDDEN, HEAD_DIM), CMP_HIDDEN ** -0.5),
        'w_out': nrm((DEPTH, D_MODEL, D_MODEL), D_MODEL ** -0.5),
        'ffn_w_in': nrm((DEPTH, D_MODEL, 2 * D_FF), D_MODEL ** -0.5),
        'ffn_conv_w': nrm((DEPTH, FFN_CONV, D_FF), FFN_CONV ** -0.5),
        'ffn_conv_b': nrm((DEPTH, D_FF), 0.01),
        'ffn_w_down': nrm((DEPTH, D_FF, D_MODEL), D_FF ** -0.5),
    }

def reference(x_prompt, x_sample, cache_cmp_kv, cache_slc_kv, cache_win_kv, state_rg_h, state_rg_conv,
              state_ffn_conv, page_table, norm_mix_pre, norm_mix_post, norm_ffn_pre, norm_ffn_post, w_in,
              rg_conv_w, rg_conv_b, rg_wa, rg_ba, rg_wx, rg_bx, rg_lambda, cmpk_pe, cmpk_w1, cmpk_b1, cmpk_w2,
              cmpv_pe, cmpv_w1, cmpv_b1, cmpv_w2, w_out, ffn_w_in, ffn_conv_w, ffn_conv_b, ffn_w_down):
    hp, hs = x_prompt, x_sample
    states_p, states_s = [], []
    for l in range(DEPTH):
        lp = dict(w_in=w_in[l], rg_conv_w=rg_conv_w[l], rg_conv_b=rg_conv_b[l], rg_wa=rg_wa[l], rg_ba=rg_ba[l],
                  rg_wx=rg_wx[l], rg_bx=rg_bx[l], rg_lambda=rg_lambda[l], cmpk_pe=cmpk_pe[l], cmpk_w1=cmpk_w1[l],
                  cmpk_b1=cmpk_b1[l], cmpk_w2=cmpk_w2[l], cmpv_pe=cmpv_pe[l], cmpv_w1=cmpv_w1[l],
                  cmpv_b1=cmpv_b1[l], cmpv_w2=cmpv_w2[l], w_out=w_out[l], ffn_w_in=ffn_w_in[l],
                  ffn_conv_w=ffn_conv_w[l], ffn_conv_b=ffn_conv_b[l], ffn_w_down=ffn_w_down[l])
        m, st = _mixer_prompt(_rms(hp, norm_mix_pre[l]), lp)
        hp = hp + _rms(m, norm_mix_post[l])
        f, fc = _ffn(_rms(hp, norm_ffn_pre[l]), jnp.zeros((hp.shape[0], FFN_CONV - 1, D_FF), hp.dtype), lp)
        hp = hp + _rms(f, norm_ffn_post[l])
        states_p.append(st + (fc,))
        m, st = _mixer_sample(_rms(hs, norm_mix_pre[l]), lp, cache_cmp_kv[l], cache_slc_kv[l], page_table,
                              cache_win_kv[l], state_rg_h[l], state_rg_conv[l])
        hs = hs + _rms(m, norm_mix_post[l])
        f, fc = _ffn(_rms(hs, norm_ffn_pre[l]), state_ffn_conv[l], lp)
        hs = hs + _rms(f, norm_ffn_post[l])
        states_s.append(st + (fc,))
    p_cmp, p_slc, p_win, p_rgh, p_rgc, p_ffc = [jnp.stack(z) for z in zip(*states_p)]
    s_cmp, s_slc, s_win, s_rgh, s_rgc, s_ffc = [jnp.stack(z) for z in zip(*states_s)]
    return (hp, hs, p_cmp, s_cmp, p_slc, s_slc, p_win, s_win, p_rgh, s_rgh, p_rgc, s_rgc, p_ffc, s_ffc)


_drawn_inputs = setup_inputs


def setup_inputs(seed=0):
    import zlib

    import numpy as np

    out = dict(_drawn_inputs(seed))
    spreads = {}
    factors = {'norm_ffn_post': 3.433,
     'rg_ba': 8.0,
     'rg_bx': 8.0,
     'cmpk_pe': 3.117,
     'cmpk_b1': 26.487,
     'cmpv_b1': 4.606,
     'ffn_conv_b': 6.853}
    for name, (base, spread) in spreads.items():
        noise = np.random.default_rng([zlib.crc32(name.encode()), seed]).standard_normal(out[name].shape)
        drawn = base * np.exp(spread * noise) if base else spread * noise
        out[name] = __import__('jax').numpy.asarray(drawn.astype(out[name].dtype))
    for name, factor in factors.items():
        out[name] = (out[name] * factor).astype(out[name].dtype)
    return out
```

```python
from contextlib import ExitStack

import numpy as np
import concourse.bass as bass
from concourse import mybir

F32 = mybir.dt.float32
I32 = mybir.dt.int32
U32 = mybir.dt.uint32
ALU = mybir.AluOpType
ACT = mybir.ActivationFunctionType
AX = mybir.AxisListType

P = 128
D = 1024
SEQ, DB, DT = 512, 8, 4
NS = DB * DT
T = SEQ + NS
TH = T // 2
DEPTH = 2
PAST, PAGE = 2048, 128
DR = 512
RJ = DR // P
NH, HD, NKV, GR = 8, 64, 2, 4
STRIDE = 16
CPP = PAGE // STRIDE
NCH = PAST // STRIDE
NCP = SEQ // STRIDE
SB = 64
NSB = PAST // SB + 1
WIN = 512
DF = 3072
FT = DF // P
KT = D // P
RND = 3
FR = FT // RND
NIN = 2328
C_GATE, C_Q, C_KVC, C_KVS, C_KVW, C_GL = 512, 1024, 1536, 1792, 2048, 2304
EPS = 1e-6
BIG = 1e30
THETA = 10000.0
TT = [(t * P, min(P, T - t * P)) for t in range(5)]
NPOOL = DB * (PAST // PAGE) * 5 // 4
NW, NA, NTS = 5, 3, 5

K_ID, K_ROT, K_CAUS, K_GSUM, K_HM, K_CMPM, K_NEWM, K_WINM, K_REP, K_PICK, K_CH = \
    0, 128, 256, 384, 512, 640, 768, 832, 836, 1092, 1116
K_COS, K_SIN, K_COSK, K_SINK, K_ALL = 1120, 1120 + T, 1120 + 2 * T, 1120 + 2 * T + 320, 1120 + 2 * T + 640

P_NORM, P_RCW, P_RCB, P_BA, P_BX, P_LAM, P_B1, P_PE, P_N0 = 0, 32, 48, 52, 56, 60, 64, 66, 98
P_FCW, P_FCB = 98, 170
P_H0, P_RC = 194, 226
P_FS = 322
P_ALL = 706

def constants():
    c = np.zeros((P, K_ALL), np.float32)
    c[:, K_ID:K_ID + P] = np.eye(P)
    for m in range(P):
        if m % 64 < 32:
            c[m + 32, K_ROT + m] = -1.0
        else:
            c[m - 32, K_ROT + m] = 1.0
    q = np.arange(P)
    c[:, K_CAUS:K_CAUS + P] = np.where(q[None, :] <= q[:, None], 0.0, -BIG)
    b, h, g, t = q // 32, q // 16 % 2, q // 4 % 4, q % 4
    same = (b[:, None] == b) & (h[:, None] == h) & (t[:, None] == t)
    c[:, K_GSUM:K_GSUM + P] = same
    c[:, K_HM:K_HM + P] = h[:, None] == (q // 64)[None, :]
    ch = np.arange(NCP)
    for i in range(4):
        ok = (ch[None, :] * STRIDE + 2 * STRIDE - 1 <= (i * P + q)[:, None]) & (ch < NCP - 1)[None, :]
        c[:, K_CMPM + i * NCP:K_CMPM + (i + 1) * NCP] = np.where(ok, 0.0, -BIG)
    n = np.arange(NS)
    for G in range(2):
        ok = ((n // DT)[None, :] == (4 * G + b)[:, None]) & ((n % DT)[None, :] <= t[:, None])
        c[:, K_NEWM + G * NS:K_NEWM + (G + 1) * NS] = np.where(ok, 0.0, -BIG)
        c[:NS, K_REP + G * P:K_REP + (G + 1) * P] = ((n // DT)[:, None] == (4 * G + b)[None, :]) & \
            ((n % DT)[:, None] == t[None, :])
    c[:, K_WINM:K_WINM + 4] = np.where(np.arange(4)[None, :] <= t[:, None], -BIG, 0.0)
    for j in range(3):
        c[:, K_PICK + j * 8:K_PICK + j * 8 + 8] = (h * GR + g)[:, None] == np.arange(8)[None, :]
    c[:, K_CH] = q % CPP
    pos = np.concatenate([np.arange(SEQ), PAST + np.arange(NS) % DT]).astype(np.float32)
    half = HD // 2
    freq = (np.float32(THETA) ** (-np.arange(half, dtype=np.float32) / np.float32(half))).astype(np.float32)
    ang = pos[:, None] * freq[None, :]
    cos, sin = np.cos(ang), np.sin(ang)
    c[:, K_COS:K_COS + T] = np.tile(cos.T, (4, 1))
    c[:, K_SIN:K_SIN + T] = np.tile(sin.T, (4, 1))
    for i, (t0, m) in enumerate(TT):
        c[:m, K_COSK + i * 64:K_COSK + i * 64 + 64] = np.tile(cos[t0:t0 + m], (1, 2))
        c[:m, K_SINK + i * 64:K_SINK + i * 64 + 32] = -sin[t0:t0 + m]
        c[:m, K_SINK + i * 64 + 32:K_SINK + i * 64 + 64] = sin[t0:t0 + m]
    return c

class Counts:

    def __init__(self, nc, ctx, known):
        self.nc, self.ctx, self.known = nc, ctx, known
        self.sems, self.count, self.table, self.read = {}, {}, {}, {}
        self.bank_of, self.last_use, self.slot_of, self.bank_key = {}, {}, {}, {}

    def sem(self, name):
        if name not in self.sems:
            self.sems[name] = self.ctx.enter_context(self.nc.semaphore(name))
            self.count[name] = 0
        return self.sems[name]

    def up(self, name, key=None, frees=(), by=1):
        self.count[name] += by
        if key is not None:
            self.table[name, key] = self.count[name]
        for buffer in frees:
            self.read.setdefault(buffer, {})[name] = self.count[name]
        return by

    def now(self, name):
        return self.count[name]

    def after(self, name, key):
        return self.known.table[name, key] if self.known else 1

    def freed(self, buffer):
        if not self.known:
            return []
        return [(self.sem(name), value) for name, value in self.known.read.get(buffer, {}).items()]

def hybrid_step(nc, I, O, known=None):
    ctx = ExitStack()
    with ctx:
        S = Counts(nc, ctx, known)
        sem, up, now, after, freed = S.sem, S.up, S.now, S.after, S.freed
        sb = lambda name, cols, dt=F32: ctx.enter_context(nc.sbuf_tensor(name, [P, cols], dt))
        xT = sb("xT", KT * T)[:].rearrange("p (k t) -> p k t", k=KT)
        hT = sb("hT", KT * T)[:].rearrange("p (k t) -> p k t", k=KT)
        ov = sb("ov", 12256)
        wr = sb("wr", NW * 1024)[:].rearrange("p (s k c) -> p s k c", s=NW, k=8)
        ar = sb("ar", NA * 4096)
        w1 = sb("w1", 4096)[:].rearrange("p (v s f) -> p v s f", v=2, s=16)
        ts = sb("ts", NTS * 512)
        kcT = sb("kcT", DB * 127)[:].rearrange("p (b c) -> p b c", b=DB)
        vc = sb("vc", DB * P)[:].rearrange("p (b c) -> p b c", b=DB)
        par = sb("par", P_ALL)
        cst = sb("cst", K_ALL)
        ov2 = sb("ov2", 1024)
        w2 = sb("w2", 128)[:].rearrange("p (v d) -> p v d", v=2)
        wgl = sb("wgl", 8 * 24)[:].rearrange("p (k c) -> p k c", k=8)
        gates = sb("gates", 120)[:].rearrange("p (t c) -> p t c", t=5)
        gs = sb("gs", 6)[:].rearrange("p (g c) -> p g c", g=2)
        hid = sb("hid", 508)
        ones = sb("ones", P)
        sm = sb("sm", 288)
        outr = sb("outr", 144)
        idi = sb("idi", (1 + DEPTH) * DB, I32)
        pst = ctx.enter_context(nc.psum_tensor("ps", [P, 8, 512], F32))

        ident = cst[:, K_ID:K_ID + P]
        rot = cst[:, K_ROT:K_ROT + P]
        cosT, sinT = cst[:, K_COS:K_COS + T], cst[:, K_SIN:K_SIN + T]
        cosk = cst[:, K_COSK:K_COSK + 320].rearrange("p (t d) -> p t d", t=5)
        sink = cst[:, K_SINK:K_SINK + 320].rearrange("p (t d) -> p t d", t=5)

        o3 = lambda a, n: ov[:, a:a + n * T].rearrange("p (k t) -> p k t", k=n)
        yT = o3(0, 4)
        qcT, qrT = o3(2176, 4), o3(4352, 4)
        sS = ov[:, 6528:8608]
        kvt = {"c": ov[:, 6528:7808], "s": ov[:, 8608:9888], "w": ov[:, 9888:11168]}
        kvt = {n: v.rearrange("p (t c) -> p t c", t=5) for n, v in kvt.items()}
        kT = {"s": ov[:, 11168:11712], "w": ov[:, 11712:12256]}
        mT = o3(2176, 8)
        actT = o3(6528, 8)
        diag = ov[:, 10880:11424]
        gpad = [ov[:, 10880 + 562 * i:10880 + 562 * (i + 1)] for i in range(2)]
        cF, gF, fcb = ov[:, 0:560], ov[:, 560:1104], ov[:, 1104:1536]
        R0 = 6825
        xrp = ov[:, R0:R0 + 571]
        cR = ov[:, R0 + 571:R0 + 1139]
        xc, rt, aR, tR, iR, hR, gR = (ov[:, R0 + 1139 + i * T:R0 + 1139 + (i + 1) * T] for i in range(7))
        recR = cR[:, 0:T]
        wbd = ov2[:, :].rearrange("p (v j c) -> p v j c", v=2, j=RJ)
        qbd = ov2[:, 0:512].rearrange("p (v b r) -> p v b r", v=2, b=DB)
        vbd = ov2[:, 512:1024].rearrange("p (h g d) -> p h g d", h=2, g=4)
        stage = lambda i: hid[:, 0:P] if i == 5 else ov[:, 1536 + i * P:1536 + (i + 1) * P]
        st_out = ov[:, 11424:12192]
        h4 = hT[:, 4:8, :].rearrange("p k t -> p (k t)")
        o_sb, o_tmp, pc_s, pc_p = h4[:, 0:512], h4[:, 512:1024], h4[:, 1024:1280], h4[:, 1280:1536]
        hidrep = h4[:, 512:768].rearrange("p (h c) -> p h c", h=2)
        comb = h4[:, 1536:1792].rearrange("p (g c) -> p g c", g=2)
        xs_slot = lambda n: h4[:, 768 * (n % 2):768 * (n % 2) + 512]
        pp, kcTp = h4[:, 1792:1928], h4[:, 1928:1960]
        idx = h4[:, 0:3 * DB]
        p_slot = lambda m: sS[:, (m % 4) * 512:(m % 4 + 1) * 512]
        mb = lambda G: sm[:, 208 + 36 * G:208 + 36 * G + 33]
        per7 = ov[:, R0 + 571 + 515:R0 + 571 + 515 + 56].rearrange("p (b c) -> p b c", b=DB)[:, :, 0:DT]
        per6 = ov[:, 514:562].rearrange("p (b c) -> p b c", b=DB)[:, :, 0:DT]
        def hid_of(u, v):
            n = 127 if u[1] == "cmp" else NCP
            return hid[:, v * 254:v * 254 + 2 * n].rearrange("p (h c) -> p h c", h=2)

        OUTT = [("rg", 0, 48), ("rgc", 48, 144), ("pf", 0, 48), ("sf0", 48, 176), ("sf1", 176, 304), ("sf2", 304, 432)]
        xin = ov[:, 2176:2176 + 5 * D].rearrange("p (t d) -> p t d", t=5)
        yout = ov[:, 0:5 * D].rearrange("p (t d) -> p t d", t=5)

        halves = lambda ap: ap.rearrange("p (h t) -> p h t", h=2)
        pair = lambda b: pst[:, b:b + 2, 0:TH]
        flat = lambda b, n: pst[:, b:b + 2, :].rearrange("p a c -> p (a c)")[:, 0:n]
        bank = lambda b: pst[:, b, :]
        wv = lambda n: wr[:, n % NW]
        av = lambda n: ar[:, (n % NA) * 4096:(n % NA + 1) * 4096]
        tv = lambda n: ts[:, (n % NTS) * 512:(n % NTS + 1) * 512]

        units = []
        for l in range(DEPTH):
            for j in range(RJ):
                units += [(l, "xr", j), (l, "gate", j)]
            units += [(l, "q", g) for g in range(4)]
            units += [(l, "kv", n) for n in ("s0", "s1", "w0", "w1", "c0", "c1")]
            units += [(l, "out", j) for j in range(KT)]
            for r in range(RND):
                for f in range(r * FR, (r + 1) * FR):
                    units += [(l, "g", f), (l, "u", f)]
                units += [(l, "down", (r, j)) for j in range(KT)]
        unit_no = {u: n for n, u in enumerate(units)}
        loads = []
        for l in range(DEPTH):
            loads += [(l, "cmp", b) for b in range(DB)] + [(l, "cmpp", 0)]
            for G in range(2):
                loads += [(l, "win", G)] + [(l, "slc", 4 * G + b) for b in range(4)]
        load_no = {u: n for n, u in enumerate(loads)}

        block = ctx.enter_context(nc.Block())

        @block.tensor
        def _(pe):
            
            cyc = {"pair": 0, "one": 0, "acc": 0}

            def take(key, kind):
                b = {"pair": (0, 2), "one": (4, 5), "acc": (6, 7), "wide": (0, 2), "six": (0, 1, 2, 3, 4, 5)}[kind]
                c = {"pair": "pair", "wide": "pair", "one": "one", "acc": "acc", "six": "one"}[kind]
                b = b[cyc[c] % len(b)]
                cyc[c] += 1
                for x in range(b, b + (2 if kind in ("pair", "wide") else 1)):
                    if x in S.last_use:
                        for s, n_ in freed(("psum", S.last_use[x])):
                            pe.wait_ge(s, n_)
                    S.last_use[x] = key
                S.bank_of[key] = b
                return b

            mm = lambda o, a, b, st, sp: nc.tensor.matmul(o, a, b, start=st, stop=sp)

            def weights(u):
                n = unit_no[u]
                pe.wait_ge(sem(f"w_loaded{n % NW}"), after(f"w_loaded{n % NW}", n))
                return wv(n)

            def project(u, rhs, key, ready=None):
                w = weights(u)
                b = take(key, "pair")
                for k in range(KT):
                    if ready:
                        ready(k)
                    for h in range(2):
                        i = mm(pst[:, b + h, 0:TH], w[:, k, :], rhs(k)[:, h * TH:(h + 1) * TH], k == 0, k == KT - 1)
                i.then_inc(sem("projected"), up("projected", key, frees=[("w", unit_no[u])]))

            def stats(l, n, sq):
                b = take((l, n, "sum"), "one")
                for k in range(KT):
                    pe.wait_ge(sem("squared"), after("squared", (l, n, k)))
                    for t, (t0, m) in enumerate(TT):
                        i = nc.tensor.matmul(pst[0:m, b, t:t + 1], sq[:, k, t0:t0 + m], ones[:, 0:1],
                                             start=(k == 0 and t == 0), stop=(k == KT - 1 and t == 4),
                                             skip_group_check=True)
                i.then_inc(sem("summed"), up("summed", (l, n)))
                b = take((l, n, "rstd"), "wide")
                pe.wait_ge(sem("diag_built"), after("diag_built", (l, n)))
                for t, (t0, m) in enumerate(TT):
                    i = mm(flat(b, T)[:, t0:t0 + m], ones[0:m, :], diag[0:m, t0:t0 + m], True, True)
                i.then_inc(sem("rstd_spread"), up("rstd_spread", (l, n)))

            def turn_params(l):
                rows = [98, 96, 128, 128, 128, 128]
                for i, r in enumerate(rows):
                    b = take((l, "par", i), "one")
                    pe.wait_ge(sem("params_loaded"), after("params_loaded", l))
                    j = nc.tensor.transpose(pst[:, b, 0:r], stage(i)[0:r, :], ident[0:r, 0:r])
                    j.then_inc(sem("params_turned"), up("params_turned", (l, i)))

            pe.wait_ge(sem("const_loaded"), after("const_loaded", 0))
            pe.wait_ge(sem("ones_set"), after("ones_set", 0))
            pe.wait_ge(sem("x_loaded"), after("x_loaded", 0))
            for k in range(KT):
                b = take(("x", k), "wide")
                for t, (t0, m) in enumerate(TT):
                    i = nc.tensor.transpose(flat(b, T)[:, t0:t0 + m], xin[0:m, t, k * P:(k + 1) * P], ident[0:m, 0:m])
                i.then_inc(sem("x_turned"), up("x_turned", k))

            tsn, xsn = [0], [0]

            def slot(key, bank_key=None):
                S.slot_of[key], S.bank_key[key] = tsn[0], bank_key or key
                tsn[0] += 1
                return tsn[0] - 1

            def compress(l, u):
                nch = NCH if u[1] == "cmp" else NCP
                for v in range(2):
                    hb = take((u, "hid", v), "acc")
                    slots = []

                    def turn(s4):
                        b = take((u, "xt", v, s4), "one")
                        pe.wait_ge(sem("rearranged"), after("rearranged", (u, v, s4)))
                        x = xs_slot(xsn[0])
                        for c in range(4):
                            i = nc.tensor.transpose(pst[:, b, c * nch:(c + 1) * nch], x[0:nch, c * P:(c + 1) * P],
                                                    ident[0:nch, 0:nch])
                        i.then_inc(sem("turned"), up("turned", (u, "xt", v, s4), frees=[("xs", xsn[0])]))
                        xsn[0] += 1
                        slots.append(slot((u, "xt", v, s4)))

                    def product(s4):
                        pe.wait_ge(sem("copied_a" if s4 % 2 else "copied_v"), after("copied_a" if s4 % 2 else "copied_v", (u, "xt", v, s4)))
                        x = tv(slots[s4])[:, 0:4 * nch].rearrange("p (e h c) -> p e h c", e=2, h=2)
                        for e in range(2):
                            sp = 2 * s4 + e
                            o = pst[:, hb, 0:2 * (nch - 1)].rearrange("p (h c) -> p h c", h=2)
                            mm(o, w1[:, v, sp, :], x[:, e, :, 0:nch - 1], sp == 0, False)
                            i = mm(o, w1[:, v, 8 + sp, :], x[:, e, :, 1:nch], False, sp == 7)
                        i.then_inc(sem("compressed"), up("compressed", (u, v, s4), frees=[("ts", slots[s4])]))

                    turn(0)
                    turn(1)
                    for s4 in range(4):
                        product(s4)
                        if s4 < 2:
                            turn(s4 + 2)
                for v in range(2):
                    b = take((u, "c2", v), "one")
                    pe.wait_ge(sem("hidden_rep" if u[1] == "cmpp" and v else "hidden"), after("hidden_rep" if u[1] == "cmpp" and v else "hidden", (u, v)))
                    for h in range(2):
                        if v == 0:
                            m = nch - 1 if u[1] == "cmp" else nch
                            i = mm(pst[h * HD:(h + 1) * HD, b, 0:m], w2[:, 0, :], hid_of(u, 0)[:, h, :], True, True)
                        elif u[1] == "cmp":
                            i = mm(pst[0:nch - 1, b, h * HD:(h + 1) * HD], hid_of(u, 1)[:, h, :], w2[:, 1, :], True, True)
                        else:
                            i = mm(pst[:, b, h * HD:(h + 1) * HD], hidrep[:, h, :], w2[:, 1, :], True, True)
                    i.then_inc(sem("compressed2"), up("compressed2", (u, v)))

            def prompt_attention(l):
                todo = [(i, br, g) for i in range(4) for br in "sw" for g in range(4)]
                st = {}

                def scores(u):
                    i, br, g = u
                    L = (i + 1) * P
                    for h in range(2):
                        b = take((l, u, "S", h), "quad")
                        j = mm(pst[:, b, 0:L], qrT[h * HD:(h + 1) * HD, g, i * P:(i + 1) * P],
                               kT[br][h * HD:(h + 1) * HD, 0:L], True, True)
                        j.then_inc(sem("scored"), up("scored", (l, u, h)))

                def turn(u):
                    i, br, g = u
                    for h in range(2):
                        st[u] = st.get(u, []) + [slot((l, u, h), (l, u, "T", h))]
                        pe.wait_ge(sem("p_exp"), after("p_exp", (l, u, h)))
                        b = take((l, u, "T", h), "one")
                        for c in range(i + 1):
                            j = nc.tensor.transpose(pst[:, b, c * P:(c + 1) * P],
                                                    p_slot(todo.index(u) * 2 + h)[:, c * P:(c + 1) * P], ident)
                        j.then_inc(sem("turned"), up("turned", (l, u, h), frees=[("p", l, todo.index(u) * 2 + h)]))

                def values(u):
                    i, br, g = u
                    if g == 0:
                        take((l, i, br, "O"), "acc")
                    b = S.bank_of[l, i, br, "O"]
                    for h in range(2):
                        pe.wait_ge(sem("copied_a" if h else "copied_v"), after("copied_a" if h else "copied_v", (l, u, h)))
                        x = tv(st[u][h])
                        hd = g * 2 + h
                        for c in range(i + 1):
                            j = mm(pst[:, b, hd * HD:(hd + 1) * HD], x[:, c * P:(c + 1) * P],
                                   kvt[br][:, c, P + h * HD:P + (h + 1) * HD], c == 0, c == i)
                        j.then_inc(sem("summed_values"), up("summed_values", (l, u, h), frees=[("ts", st[u][h])]))

                def cmp_scores(i):
                    for h in range(2):
                        b = take((l, i, "Sc", h), "quad")
                        for g in range(GR):
                            j = mm(pst[:, b, g * NCP:(g + 1) * NCP],
                                   qcT[h * HD:(h + 1) * HD, g, i * P:(i + 1) * P],
                                   kcTp[h * HD:(h + 1) * HD, :], True, True)
                    j.then_inc(sem("scored"), up("scored", (l, i, "c")))

                def cmp_values(i):
                    b = take((l, i, "Tc"), "one")
                    n = slot((l, i, "c"), (l, i, "Tc"))
                    pe.wait_ge(sem("cmp_exp"), after("cmp_exp", (l, i)))
                    for h in range(2):
                        j = nc.tensor.transpose(pst[:, b, h * P:(h + 1) * P], pc_p[:, h * P:(h + 1) * P], ident)
                    j.then_inc(sem("turned"), up("turned", (l, i, "c")))
                    b = take((l, i, "c", "O"), "acc")
                    pe.wait_ge(sem("copied_v"), after("copied_v", (l, i, "c")))
                    for h in range(2):
                        j = mm(pst[:, b, :].rearrange("p (g h d) -> p g h d", g=GR, h=2)[:, :, h, :], tv(n)[:, h * P:(h + 1) * P],
                               vbd[:, h].rearrange("p g d -> p (g d)"), True, True)
                    j.then_inc(sem("summed_values"), up("summed_values", (l, i, "c"), frees=[("ts", n)]))

                def turn_o(i):
                    b = take((l, i, "oT"), "one")
                    pe.wait_ge(sem("o_gated"), after("o_gated", (l, i)))
                    for g in range(GR):
                        j = nc.tensor.transpose(pst[:, b, g * P:(g + 1) * P], o_sb[:, g * P:(g + 1) * P], ident)
                    j.then_inc(sem("o_turned"), up("o_turned", (l, i)))

                N = len(todo)
                for n in range(N + 2):
                    if n < N:
                        scores(todo[n])
                    if 1 <= n <= N:
                        turn(todo[n - 1])
                    if n >= 2:
                        values(todo[n - 2])
                        if (n - 2) % 8 == 7:
                            i = todo[n - 2][0]
                            cmp_scores(i)
                            cmp_values(i)
                            turn_o(i)

            def sample_cmp(l, G):
                b = take((l, G, "Scs"), "one")
                for e in range(4):
                    pe.wait_ge(sem("copied_v"), after("copied_v", ((l, "cmp", 4 * G + e), "kc")))
                    pe.wait_ge(sem("qbd_built"), after("qbd_built", l))
                    i = mm(pst[32 * e:32 * e + 32, b, 0:127], qbd[:, 0, 4 * G + e, :], kcT[:, 4 * G + e, :], True, True)
                i.then_inc(sem("scored"), up("scored", (l, G, "cs")))
                b = take((l, G, "gsum"), "one")
                pe.wait_ge(sem("pn_ready"), after("pn_ready", (l, G)))
                i = mm(pst[:, b, 0:127], cst[:, K_GSUM:K_GSUM + P], sS[:, G * P:G * P + 127], True, True)
                i.then_inc(sem("group_summed"), up("group_summed", (l, G)))
                b = take((l, G, "Tcs"), "one")
                n = slot((l, G, "cs"), (l, G, "Tcs"))
                i = nc.tensor.transpose(pst[0:127, b, 0:P], sS[:, G * P:G * P + 127], ident)
                i.then_inc(sem("turned"), up("turned", (l, G, "cs")))
                b = take((l, G, "Ocs"), "acc")
                pe.wait_ge(sem("copied_v"), after("copied_v", (l, G, "cs")))
                for e in range(4):
                    pe.wait_ge(sem("copied_v"), after("copied_v", ((l, "cmp", 4 * G + e), "vc")))
                    i = mm(pst[32 * e:32 * e + 32, b, 0:P], tv(n)[0:127, 32 * e:32 * e + 32], vc[0:127, 4 * G + e, :], True, True)
                i.then_inc(sem("summed_values"), up("summed_values", (l, G, "cs"), frees=[("ts", n)]))

            def sample_win(l, G):
                u = (l, "win", G)
                n = load_no[u]
                a = av(n).rearrange("p (b s c) -> p b s c", b=4, s=4)
                pe.wait_ge(sem(f"a_loaded{n % NA}"), after(f"a_loaded{n % NA}", n))
                sl = []
                for e in range(4):
                    b = take((u, "kt", e), "one")
                    for s in range(4):
                        i = nc.tensor.transpose(pst[:, b, s * P:(s + 1) * P], a[:, e, s, 0:P], ident)
                    i.then_inc(sem("turned"), up("turned", (u, "kt", e)))
                    sl.append(slot((u, "kt", e)))
                sbk = take((u, "S"), "quad")
                sb2 = take((u, "Sn"), "quad")
                for e in range(4):
                    pe.wait_ge(sem("copied_a" if e % 2 else "copied_v"), after("copied_a" if e % 2 else "copied_v", (u, "kt", e)))
                    q = qbd[:, 1, 4 * G + e, :]
                    mm(pst[32 * e:32 * e + 32, sbk, :], q, tv(sl[e]), True, True)
                    i = mm(pst[32 * e:32 * e + 32, sb2, 0:NS], q, kT["w"][:, SEQ:T], True, True)
                    i.then_inc(sem("scored"), up("scored", (u, e), frees=[("ts", sl[e])]))
                b = take((u, "pt"), "one")
                n1 = slot((u, "pt"))
                pe.wait_ge(sem("p_exp"), after("p_exp", u))
                for s in range(4):
                    i = nc.tensor.transpose(pst[:, b, s * P:(s + 1) * P], sS[:, s * P:(s + 1) * P], ident)
                i.then_inc(sem("turned"), up("turned", (u, "pt")))
                b = take((u, "ptn"), "one")
                n2 = slot((u, "ptn"))
                i = nc.tensor.transpose(pst[0:NS, b, 0:P], sS[:, 2048:2048 + NS], ident)
                i.then_inc(sem("turned"), up("turned", (u, "ptn"), frees=[("sS", u)]))
                b = take((u, "O"), "acc")
                pe.wait_ge(sem("copied_v"), after("copied_v", (u, "ptn")))
                for e in range(4):
                    o = pst[32 * e:32 * e + 32, b, 0:P]
                    for s in range(4):
                        mm(o, tv(n1)[:, s * P + 32 * e:s * P + 32 * e + 32], a[:, e, s, P:2 * P], s == 0, False)
                    i = mm(o, tv(n2)[0:NS, 32 * e:32 * e + 32], kvt["w"][0:NS, 4, P:2 * P], False, True)
                i.then_inc(sem("summed_values"), up("summed_values", (u, 0), frees=[("ts", n1), ("ts", n2), ("a", n)]))

            def sample_slc(l, G):
                ob = None
                for e in range(4):
                    u = (l, "slc", 4 * G + e)
                    n = load_no[u]
                    a = av(n).rearrange("p (s c) -> p s c", s=STRIDE)
                    pe.wait_ge(sem(f"a_loaded{n % NA}"), after(f"a_loaded{n % NA}", n))
                    q = qbd[:, 1, 4 * G + e, :]
                    sl = {}

                    def turn(x):
                        b = take((u, "kt", x), "one")
                        for s in range(4):
                            i = nc.tensor.transpose(pst[:, b, s * P:(s + 1) * P], a[:, 4 * x + s, 0:P], ident)
                        i.then_inc(sem("turned"), up("turned", (u, "kt", x)))
                        sl[x] = slot((u, "kt", x))

                    def score(x):
                        sbk = take((u, "S", x), "quad")
                        pe.wait_ge(sem("copied_a" if x % 2 else "copied_v"), after("copied_a" if x % 2 else "copied_v", (u, "kt", x)))
                        i = mm(pst[32 * e:32 * e + 32, sbk, :], q, tv(sl[x]), True, True)
                        i.then_inc(sem("scored"), up("scored", (u, x), frees=[("ts", sl[x])]))

                    turn(0)
                    turn(1)
                    score(0)
                    turn(2)
                    score(1)
                    turn(3)
                    score(2)
                    score(3)
                    sb2 = take((u, "Sn"), "quad")
                    i = mm(pst[32 * e:32 * e + 32, sb2, 0:NS], q, kT["s"][:, SEQ:T], True, True)
                    i.then_inc(sem("scored"), up("scored", (u, "n")))
                    b = take((u, "pt"), "one")
                    n1 = slot((u, "pt"))
                    pe.wait_ge(sem("p_exp"), after("p_exp", u))
                    idb = ident[32 * e:32 * e + 32, 32 * e:32 * e + 32]
                    for s in range(16):
                        i = nc.tensor.transpose(pst[:, b, 32 * s:32 * s + 32], sS[32 * e:32 * e + 32, s * P:(s + 1) * P], idb)
                    i.then_inc(sem("turned"), up("turned", (u, "pt")))
                    b = take((u, "ptn"), "one")
                    n2 = slot((u, "ptn"))
                    i = nc.tensor.transpose(pst[0:NS, b, 0:32], sS[32 * e:32 * e + 32, 2048:2048 + NS], idb)
                    i.then_inc(sem("turned"), up("turned", (u, "ptn"), frees=[("sS", u)]))
                    if e == 0:
                        ob = take((l, G, "Oslc"), "acc")
                    pe.wait_ge(sem("copied_v"), after("copied_v", (u, "ptn")))
                    o = pst[32 * e:32 * e + 32, ob, 0:P]
                    for s in range(16):
                        mm(o, tv(n1)[:, 32 * s:32 * s + 32], a[:, s, P:2 * P], s == 0, False)
                    i = mm(o, tv(n2)[0:NS, 0:32], kvt["s"][0:NS, 4, P:2 * P], False, True)
                    i.then_inc(sem("summed_values"), up("summed_values", (u, 0), frees=[("ts", n1), ("ts", n2), ("a", n)]))

            def take_quad(key):
                b = (0, 1, 2, 3)[cyc.setdefault("quad", 0) % 4]
                cyc["quad"] += 1
                if b in S.last_use:
                    for s, n_ in freed(("psum", S.last_use[b])):
                        pe.wait_ge(s, n_)
                S.last_use[b] = key
                S.bank_of[key] = b
                return b

            plain_take = take

            def take(key, kind):
                return take_quad(key) if kind == "quad" else plain_take(key, kind)

            for l in range(DEPTH):
                turn_params(l)
                stats(l, 0, actT)
                for j in range(RJ):
                    rd = (lambda k: pe.wait_ge(sem("h_ready"), after("h_ready", (l, 0, k)))) if j == 0 else None
                    project((l, "xr", j), lambda k: hT[:, k, :], (l, "xr", j), rd)
                    project((l, "gate", j), lambda k: hT[:, k, :], (l, "gate", j))
                    pe.wait_ge(sem("wbd_loaded"), after("wbd_loaded", l))
                    pe.wait_ge(sem("conv_done"), after("conv_done", (l, j)))
                    for v in range(2):
                        b = take((l, "rg", j, v), "pair")
                        for h in range(2):
                            i = mm(pst[:, b + h, 0:TH], wbd[:, v, j, :], xc[:, h * TH:(h + 1) * TH], True, True)
                        i.then_inc(sem("projected"), up("projected", (l, "rg", j, v)))
                for g in range(GR):
                    project((l, "q", g), lambda k: hT[:, k, :], (l, "q", g))
                for g in range(GR):
                    b = take((l, "rot", g), "pair")
                    pe.wait_ge(sem("q_copied"), after("q_copied", (l, g)))
                    for h in range(2):
                        i = mm(pst[:, b + h, 0:TH], rot, qcT[:, g, h * TH:(h + 1) * TH], True, True)
                    i.then_inc(sem("projected"), up("projected", (l, "rot", g)))
                for n in ("s0", "s1", "w0", "w1", "c0", "c1"):
                    w = weights((l, "kv", n))
                    b = take((l, "kv", n), "wide")
                    for t, (t0, m) in enumerate(TT):
                        for k in range(KT):
                            i = mm(flat(b, 640)[0:m, t * P:(t + 1) * P], hT[:, k, t0:t0 + m], w[:, k, :], k == 0, k == KT - 1)
                    i.then_inc(sem("projected"), up("projected", (l, "kv", n), frees=[("w", unit_no[l, "kv", n])]))
                b = take((l, "gl"), "one")
                pe.wait_ge(sem("wgl_loaded"), after("wgl_loaded", l))
                for t, (t0, m) in enumerate(TT):
                    for k in range(KT):
                        i = mm(pst[0:m, b, t * 24:(t + 1) * 24], hT[:, k, t0:t0 + m], wgl[:, k, :], k == 0, k == KT - 1)
                i.then_inc(sem("projected"), up("projected", (l, "gl")))
                for n in "sw":
                    b = take((l, "kT", n), "wide")
                    pe.wait_ge(sem("k_roped"), after("k_roped", (l, n)))
                    for t, (t0, m) in enumerate(TT):
                        i = nc.tensor.transpose(flat(b, T)[:, t0:t0 + m], kvt[n][0:m, t, 0:P], ident[0:m, 0:m])
                    i.then_inc(sem("k_turned"), up("k_turned", (l, n)))
                b = take((l, "gsel"), "one")
                pe.wait_ge(sem("gates_ready"), after("gates_ready", l))
                for G in range(2):
                    i = mm(pst[:, b, 24 * G:24 * G + 24], cst[0:NS, K_REP + G * P:K_REP + (G + 1) * P], gates[0:NS, 4, :], True, True)
                i.then_inc(sem("gates_spread"), up("gates_spread", l))
                b = take((l, "pe"), "one")
                pe.wait_ge(sem("w1_loaded"), after("w1_loaded", l))
                for v in range(2):
                    for s in range(16):
                        i = mm(pst[:, b, v:v + 1], w1[:, v, s, :], par[:, P_PE + 16 * v + s:P_PE + 16 * v + s + 1], s == 0, s == 15)
                i.then_inc(sem("pe_summed"), up("pe_summed", l))
                for u in [(l, "cmp", x) for x in range(DB)] + [(l, "cmpp", 0)]:
                    compress(l, u)
                for G in range(2):
                    sample_cmp(l, G)
                pe.wait_ge(sem("kT_copied"), after("kT_copied", (l, "w")))
                pe.wait_ge(sem("q_roped"), after("q_roped", (l, 3)))
                pe.wait_ge(sem("vbd_built"), after("vbd_built", l))
                prompt_attention(l)
                for G in range(2):
                    sample_win(l, G)
                    sample_slc(l, G)
                    b = take((l, G, "oTs"), "one")
                    pe.wait_ge(sem("comb_ready"), after("comb_ready", (l, G)))
                    i = nc.tensor.transpose(pst[:, b, 0:P], comb[:, G, :], ident)
                    i.then_inc(sem("o_turned"), up("o_turned", (l, "s", G)))
                pe.wait_ge(sem("y_ready"), after("y_ready", (l, RJ - 1)))
                pe.wait_ge(sem("oT_copied"), after("oT_copied", (l, "s", 1)))
                for j in range(KT):
                    project((l, "out", j), lambda k: yT[:, k, :] if k < 4 else hT[:, k - 4, :], (l, "out", j))
                stats(l, 1, actT)
                stats(l, 2, actT)
                for r in range(RND):
                    for f in range(r * FR, (r + 1) * FR):
                        rd = (lambda k: pe.wait_ge(sem("h_ready"), after("h_ready", (l, 2, k)))) if f == 0 else None
                        project((l, "g", f), lambda k: hT[:, k, :], (l, "g", f), rd)
                        project((l, "u", f), lambda k: hT[:, k, :], (l, "u", f))
                    for j in range(KT):
                        rd = (lambda k: pe.wait_ge(sem("act_ready"), after("act_ready", (l, r * FR + k)))) if j == 0 else None
                        project((l, "down", (r, j)), lambda k: actT[:, k, :], (l, "down", r, j), rd)
                stats(l, 3, hT)
                pe.wait_ge(sem("states_ready"), after("states_ready", (l, "ffn")))
                for i in range(6):
                    r0, r1 = OUTT[i][1:3]
                    src = outr[:, r0:r1] if i < 2 else fcb[:, r0:r1]
                    b = take((l, "st", i), "one")
                    j = nc.tensor.transpose(pst[0:r1 - r0, b, 0:P], src, ident)
                    j.then_inc(sem("states_turned"), up("states_turned", (l, i)))
            for k in range(KT):
                pe.wait_ge(sem("x_added"), after("x_added", (DEPTH - 1, 3, k)))
                for t, (t0, m) in enumerate(TT):
                    b = take(("y", k, t), "one")
                    i = nc.tensor.transpose(pst[0:m, b, 0:P], xT[:, k, t0:t0 + m], ident)
                    i.then_inc(sem("y_turned"), up("y_turned", (k, t)))

        @block.sync
        def _(sp):

            n_ld = [0]

            sp.dma_start(cst[:, :], I["consts"])\
                .then_inc(sem("const_loaded"), up("const_loaded", 0, by=16))
            xp, xs = I["x_prompt"], I["x_sample"]
            sp.dma_start(xin[:, 0:4, :], xp.rearrange("a (t p) d -> p (a t) d", p=P))\
                .then_inc(sem("x_loaded"), up("x_loaded", 0, by=16))
            sp.dma_start(xin[0:NS, 4, :], xs.rearrange("b t d -> (b t) d"))\
                .then_inc(sem("x_loaded"), up("x_loaded", 0, by=16))

            def small(l):
                if l:
                    sp.wait_ge(sem("projected"), after("projected", (l - 1, "gl")))
                sp.dma_start(wgl, I["w_in"][l][:, C_GL:NIN].rearrange("(k p) c -> p k c", p=P))\
                    .then_inc(sem("wgl_loaded"), up("wgl_loaded", l, by=16))
                sp.wait_ge(sem("wbd_zeroed"), after("wbd_zeroed", l))
                for v, name in enumerate(("rg_wa", "rg_wx")):
                    for e in range(2):
                        src = I[name][l].rearrange("(j e) c d -> e c j d", e=2)[e]
                        sp.dma_start(wbd[64 * e:64 * e + 64, v, :, 64 * e:64 * e + 64], src)\
                            .then_inc(sem("wbd_loaded"), up("wbd_loaded", l, by=16))
                if l:
                    sp.wait_ge(sem("compressed2"), after("compressed2", ((l - 1, "cmpp", 0), 1)))
                for v, name in enumerate(("cmpk", "cmpv")):
                    sp.dma_start(w1[:, v], I[name + "_w1"][l].rearrange("(s e) d f -> (e d) s f", e=2))\
                        .then_inc(sem("w1_loaded"), up("w1_loaded", l, by=16))
                    sp.dma_start(w2[:, v, :], I[name + "_w2"][l])\
                        .then_inc(sem("w1_loaded"), up("w1_loaded", l, by=16))

            for n, (l, kind, x) in enumerate(units):
                if (kind, x) == ("xr", 1):
                    small(l)
                if n >= NW:
                    for s, n_ in freed(("w", n - NW)):
                        sp.wait_ge(s, n_)
                w, name = wv(n), f"w_loaded{n % NW}"
                win = I["w_in"][l].rearrange("(k p) c -> p k c", p=P)
                if kind in ("xr", "gate", "kv"):
                    c = {"xr": 0, "gate": C_GATE}.get(kind)
                    c = c + x * P if c is not None else {"c": C_KVC, "s": C_KVS, "w": C_KVW}[x[0]] + int(x[1]) * P
                    sp.dma_start(w, win[:, :, c:c + P])\
                        .then_inc(sem(name), up(name, n, by=16))
                elif kind == "q":
                    for h in range(2):
                        c = C_Q + h * 256 + x * HD
                        sp.dma_start(w[:, :, h * HD:(h + 1) * HD], win[:, :, c:c + HD])\
                            .then_inc(sem(name), up(name, n, by=16))
                elif kind == "out":
                    c = slice(x * P, (x + 1) * P)
                    sp.dma_start(w[:, 0:4, :], I["w_out"][l][0:DR, c].rearrange("(k p) c -> p k c", p=P))\
                        .then_inc(sem(name), up(name, n, by=16))
                    for h in range(2):
                        src = I["w_out"][l][DR + h * 256:DR + (h + 1) * 256, c].rearrange("(g d) c -> d g c", d=HD)
                        sp.dma_start(w[h * HD:(h + 1) * HD, 4:8, :], src)\
                            .then_inc(sem(name), up(name, n, by=16))
                elif kind in ("g", "u"):
                    c = (DF if kind == "g" else 0) + x * P
                    sp.dma_start(w, I["ffn_w_in"][l].rearrange("(k p) c -> p k c", p=P)[:, :, c:c + P])\
                        .then_inc(sem(name), up(name, n, by=16))
                else:
                    r, j = x
                    src = I["ffn_w_down"][l][r * D:(r + 1) * D, j * P:(j + 1) * P]
                    sp.dma_start(w, src.rearrange("(k p) c -> p k c", p=P))\
                        .then_inc(sem(name), up(name, n, by=16))

        @block.gpsimd
        def _(po):

            def p(ins):
                ins.then_inc(sem("pool_step"), up("pool_step"))
                po.wait_ge(sem("pool_step"), now("pool_step"))

            def params(l):
                if l:
                    po.wait_ge(sem("projected"), after("projected", (l - 1, "out", KT - 1)))
                r = lambda name: I[name][l]
                row = [0]

                def put(src, n, tile):
                    po.dma_start(stage(tile)[row[0]:row[0] + n, :], src)\
                        .then_inc(sem("params_loaded"), up("params_loaded", l, by=16))
                    row[0] += n

                for name in ("norm_mix_pre", "norm_mix_post", "norm_ffn_pre", "norm_ffn_post"):
                    put(r(name).rearrange("(k p) -> k p", p=P), KT, 0)
                put(r("rg_conv_w").rearrange("w (k p) -> (w k) p", p=P), 16, 0)
                for name in ("rg_conv_b", "rg_ba", "rg_bx", "rg_lambda"):
                    put(r(name).rearrange("(k p) -> k p", p=P), RJ, 0)
                for name in ("cmpk_b1", "cmpv_b1"):
                    put(r(name).rearrange("(k p) -> k p", p=P), 1, 0)
                for name in ("cmpk_pe", "cmpv_pe"):
                    put(r(name).rearrange("(s e) d -> s (e d)", e=2), 16, 0)
                row[0] = 0
                put(r("ffn_conv_w").rearrange("w (k p) -> (w k) p", p=P), 72, 1)
                put(r("ffn_conv_b").rearrange("(k p) -> k p", p=P), FT, 1)
                row[0] = 0
                put(r("state_rg_h").rearrange("b (k p) -> (b k) p", p=P), 32, 2)
                put(r("state_rg_conv").rearrange("b w (k p) -> (b w k) p", p=P), 96, 2)
                fs = r("state_ffn_conv").rearrange("b w (k p) -> (b w k) p", p=P)
                for t in range(3):
                    po.dma_start(stage(3 + t), fs[t * P:(t + 1) * P])\
                        .then_inc(sem("params_loaded"), up("params_loaded", l, by=16))

            nc.gpsimd.memset(ones[:, :], 1.0).then_inc(sem("ones_set"), up("ones_set", 0))
            po.wait_ge(sem("ones_set"), now("ones_set"))
            for c in range(CPP):
                po.dma_start(idi[c:P:CPP, 0:DB], I["page_table"].rearrange("b j -> j b"),
                                      allow_slow_non_contiguous=True).then_inc(sem("pages_loaded"), up("pages_loaded", 0, by=16))
            params(0)
            nload, xsn = [0], [0]

            def cache(upto):
                while nload[0] <= upto:
                    n = nload[0]
                    nload[0] += 1
                    l, kind, x = loads[n]
                    if n >= NA:
                        for s, n_ in freed(("a", n - NA)):
                            po.wait_ge(s, n_)
                    name = f"a_loaded{n % NA}"
                    if kind in ("cmp", "slc"):
                        po.wait_ge(sem("index_ready"), after("index_ready", 0))
                        pool = I["cache_cmp_kv" if kind == "cmp" else "cache_slc_kv"]
                        src = pool.rearrange("l n (c s) v h d -> (l n c) (s v h d)", c=CPP)
                        ixc = idi[:, (1 + l) * DB + x:(1 + l) * DB + x + 1].bitcast(U32)
                        po.indirect_dma_start(av(n), None, src, bass.IndirectOffsetOnAxis(ap=ixc, axis=0)).then_inc(sem(name), up(name, n, by=16))
                    elif kind == "cmpp":
                        po.wait_ge(sem("kv_stored_c"), after("kv_stored_c", l))
                        src = O["p_cmp"][l, 0].rearrange("(n s) v h d -> n (s v h d)", s=STRIDE)
                        po.dma_start(av(n)[0:NCP, :], src).then_inc(sem(name), up(name, n, by=16))
                    else:
                        src = I["cache_win_kv"][l, 4 * x:4 * x + 4].rearrange("b (p s) v h d -> p b (s v h d)", s=4)
                        po.dma_start(av(n).rearrange("p (b c) -> p b c", b=4), src).then_inc(sem(name), up(name, n, by=16))

            A0 = len(loads) // DEPTH
            for l in range(DEPTH):
                if l:
                    po.wait_ge(sem("projected"), after("projected", (l - 1, "rg", RJ - 1, 1)))
                    po.wait_ge(sem("comb_ready"), after("comb_ready", (l - 1, 1)))
                    po.wait_ge(sem("summed_values"), after("summed_values", ((l - 1, "slc", 7), 0)))
                nc.gpsimd.memset(ov2[:, :], 0.0).then_inc(sem("wbd_zeroed"), up("wbd_zeroed", l))
                po.wait_ge(sem("wbd_zeroed"), now("wbd_zeroed"))
                if l == 0:
                    cache(2)
                po.wait_ge(sem("projected"), after("projected", (l, "rg", RJ - 1, 1)))
                nc.gpsimd.memset(ov2[:, :], 0.0).then_inc(sem("ov2_zeroed"), up("ov2_zeroed", l))
                po.wait_ge(sem("ov2_zeroed"), now("ov2_zeroed"))
                for n, out in (("s", "slc"), ("w", "win"), ("c", "cmp")):
                    if n != "c":
                        po.wait_ge(sem("k_roped"), after("k_roped", (l, n)))
                    po.wait_ge(sem("kv_copied"), after("kv_copied", (l, n)))
                    kv4 = lambda ap: ap.rearrange("(t p) v h d -> p t (v h d)", p=P)
                    name = f"kv_stored_{n}"
                    po.dma_start(kv4(O["p_" + out][l, 0]), kvt[n][:, 0:4, :])\
                        .then_inc(sem(name), up(name, l, by=16))
                    if n == "w":
                        for b in range(DB):
                            po.dma_start(O["s_win"][l, b, WIN - DT:WIN].rearrange("t v h d -> t (v h d)"), kvt[n][b * DT:(b + 1) * DT, 4, :])\
                                .then_inc(sem(name), up(name, l, by=16))
                        for b in range(DB):
                            po.dma_start(O["s_win"][l, b, 0:WIN - DT].rearrange("(n t) v h d -> n (t v h d)", t=4), I["cache_win_kv"][l, b, DT:WIN].rearrange("(n t) v h d -> n (t v h d)", t=4))\
                                .then_inc(sem("window_moved"), up("window_moved", 0, by=16))
                    else:
                        po.dma_start(O["s_" + out][l].rearrange("b t v h d -> (b t) (v h d)"), kvt[n][0:NS, 4, :])\
                            .then_inc(sem(name), up(name, l, by=16))
                po.wait_ge(sem("projected"), after("projected", (l, "gl")))
                for u in [(l, "cmp", x) for x in range(DB)] + [(l, "cmpp", 0)]:
                    n = load_no[u]
                    cache(n)
                    po.wait_ge(sem(f"a_loaded{n % NA}"), after(f"a_loaded{n % NA}", n))
                    nch = NCH if u[1] == "cmp" else NCP
                    a = av(n).rearrange("p (s c) -> p s c", s=STRIDE)
                    for vv in range(2):
                        for s4 in range(4):
                            for s, n_ in freed(("xs", xsn[0] - 2)):
                                po.wait_ge(s, n_)
                            for e in range(2):
                                r = 4 * s4 + 2 * e
                                src = a[0:nch, r:r + 2, vv * P:(vv + 1) * P].rearrange("p s (h d) -> p h s d", h=2)
                                dst = xs_slot(xsn[0])[0:nch, 256 * e:256 * e + 256].rearrange("p (h s d) -> p h s d", h=2, s=2)
                                nc.gpsimd.tensor_copy(dst, src).then_inc(sem("rearranged" if e else "pool_step"), up("rearranged" if e else "pool_step", (u, vv, s4) if e else None, frees=[("a", n)] if e and vv and s4 == 3 else []))
                                po.wait_ge(sem("rearranged" if e else "pool_step"), now("rearranged" if e else "pool_step"))
                            xsn[0] += 1
                    cache(min(n + NA, l * A0 + A0 - 1))
                cache(l * A0 + A0 - 1)
                if l < DEPTH - 1:
                    cache((l + 1) * A0 + 2)
                    params(l + 1)
                for k in range(KT):
                    po.wait_ge(sem("m_scaled"), after("m_scaled", (l, 1, k)))
                    nc.gpsimd.tensor_tensor(xT[:, k, :], xT[:, k, :], mT[:, k, :], ALU.add).then_inc(sem("x_added"), up("x_added", (l, 1, k)))
                    po.wait_ge(sem("x_added"), now("x_added"))
                po.wait_ge(sem("rstd_spread"), after("rstd_spread", (l, 2)))
                fs = par[:, P_FS:P_FS + 384].rearrange("p (b w f) -> p b w f", b=DB, w=2)
                fo = fcb.rearrange("p (r f) -> p r f", f=FT)
                for f in range(FT):
                    gp = gpad[f % 2]
                    if f < 2:
                        p(nc.gpsimd.memset(gp[:, 0:2], 0.0))
                    else:
                        po.wait_ge(sem("conv_done"), after("conv_done", (l, "f", f - 2)))
                    gps = gp[:, 2 + SEQ:].rearrange("p (b c) -> p b c", b=DB)
                    nc.gpsimd.tensor_copy(gps[:, :, 0:2], fs[:, :, :, f]).then_inc(sem("prefix_copied"), up("prefix_copied", (l, f)))
                    po.wait_ge(sem("prefix_copied"), now("prefix_copied"))
                    po.wait_ge(sem("g_copied"), after("g_copied", (l, f)))
                    p(nc.gpsimd.tensor_copy(fo[:, 0:2, f], gp[:, SEQ:SEQ + 2]))
                    nc.gpsimd.tensor_copy(fo[:, 2:18, f].rearrange("p (b w) -> p b w", b=DB), gps[:, :, 4:6]).then_inc(sem("states_ready"), up("states_ready", (l, f if f < FT - 1 else "ffn"), frees=[("gpad", l, f)]))
                    po.wait_ge(sem("states_ready"), now("states_ready"))
                for k in range(KT):
                    po.wait_ge(sem("m_scaled"), after("m_scaled", (l, 3, k)))
                    nc.gpsimd.tensor_tensor(xT[:, k, :], xT[:, k, :], mT[:, k, :], ALU.add).then_inc(sem("x_added"), up("x_added", (l, 3, k)))
                    po.wait_ge(sem("x_added"), now("x_added"))
                for i, (name, r0, r1) in enumerate(OUTT):
                    po.wait_ge(sem("states_copied"), after("states_copied", (l, i)))
                    src = st_out[0:r1 - r0, i * P:(i + 1) * P]
                    if i == 0:
                        po.dma_start(O["p_rgc"][l].rearrange("b w (k p) -> (b w k) p", p=P), src[0:12])\
                            .then_inc(sem("states_stored"), up("states_stored", l, by=16))
                        po.dma_start(O["p_rgh"][l].rearrange("b (k p) -> (b k) p", p=P), src[12:16])\
                            .then_inc(sem("states_stored"), up("states_stored", l, by=16))
                        po.dma_start(O["s_rgh"][l].rearrange("b (k p) -> (b k) p", p=P), src[16:48])\
                            .then_inc(sem("states_stored"), up("states_stored", l, by=16))
                    elif i == 1:
                        po.dma_start(O["s_rgc"][l].rearrange("b w (k p) -> (b w k) p", p=P), src)\
                            .then_inc(sem("states_stored"), up("states_stored", l, by=16))
                    elif i == 2:
                        po.dma_start(O["p_ffc"][l].rearrange("b w (k p) -> (b w k) p", p=P), src)\
                            .then_inc(sem("states_stored"), up("states_stored", l, by=16))
                    else:
                        dst = O["s_ffc"][l].rearrange("b w (k p) -> (b w k) p", p=P)
                        po.dma_start(dst[(i - 3) * P:(i - 2) * P], src)\
                            .then_inc(sem("states_stored"), up("states_stored", l, by=16))
            for t, (t0, m) in enumerate(TT):
                po.wait_ge(sem("y_copied"), after("y_copied", (KT - 1, t)))
                if t == 4:
                    po.dma_start(O["y_s"].rearrange("b t d -> (b t) d"), yout[0:m, t, :])\
                        .then_inc(sem("y_stored"), up("y_stored", 0, by=16))
                else:
                    po.dma_start(O["y_p"][0, t0:t0 + m, :], yout[0:m, t, :])\
                        .then_inc(sem("y_stored"), up("y_stored", 0, by=16))
            po.wait_ge(sem("y_stored"), after("y_stored", 0))
            po.wait_ge(sem("window_moved"), after("window_moved", 0))
            po.wait_ge(sem("kv_stored_c"), after("kv_stored_c", DEPTH - 1))
            po.wait_ge(sem("states_stored"), after("states_stored", DEPTH - 1))

        @block.scalar
        def _(ac):

            def a(ins):
                ins.then_inc(sem("scalar_step"), up("scalar_step"))
                ac.wait_ge(sem("scalar_step"), now("scalar_step"))

            act = nc.scalar.activation
            psk = lambda key: S.bank_of[key]
            tsa = [0]

            def squares(l, n, src, sq, ready):
                for k in range(KT):
                    ready(k)
                    act(sq[:, k, :], src[:, k, :], ACT.Square).then_inc(sem("squared"), up("squared", (l, n, k)))
                    ac.wait_ge(sem("squared"), now("squared"))

            def root(l, n):
                b = psk((l, n, "sum"))
                ac.wait_ge(sem("summed"), after("summed", (l, n)))
                a(act(sm[:, 0:4], pst[:, b, 0:4], ACT.Sqrt, scale=1.0 / D, bias=sm[:, 150:151]))
                act(sm[0:NS, 4:5], pst[0:NS, b, 4:5], ACT.Sqrt, scale=1.0 / D, bias=sm[0:NS, 150:151]).then_inc(sem("rms_ready"), up("rms_ready", (l, n), frees=[("psum", (l, n, "sum"))]))
                ac.wait_ge(sem("rms_ready"), now("rms_ready"))

            for k in range(KT):
                ac.wait_ge(sem("x_turned"), after("x_turned", k))
                b = psk(("x", k))
                act(xT[:, k, :], flat(b, T), ACT.Copy).then_inc(sem("x_copied"), up("x_copied", k, frees=[("psum", ("x", k))]))
                ac.wait_ge(sem("x_copied"), now("x_copied"))

            def compress(u, prev):
                nch = NCH if u[1] == "cmp" else NCP
                for v in range(2):
                    for s4 in (1, 3):
                        ac.wait_ge(sem("turned"), after("turned", (u, "xt", v, s4)))
                        sl = S.slot_of[u, "xt", v, s4]
                        for s, n_ in freed(("ts", sl - NTS)):
                            ac.wait_ge(s, n_)
                        b = psk((u, "xt", v, s4))
                        act(tv(sl)[:, 0:4 * nch], pst[:, b, 0:4 * nch], ACT.Copy).then_inc(sem("copied_a"), up("copied_a", (u, "xt", v, s4), frees=[("psum", (u, "xt", v, s4))]))
                        ac.wait_ge(sem("copied_a"), now("copied_a"))
                    ac.wait_ge(sem("compressed"), after("compressed", (u, v, 3)))
                    ac.wait_ge(sem("b1_ready"), after("b1_ready", u[0]))
                    b = psk((u, "hid", v))
                    if prev:
                        ac.wait_ge(sem("compressed2"), after("compressed2", (prev, v)))
                    if u[1] == "cmp":
                        act(hid_of(u, v), pst[:, b, 0:2 * (nch - 1)].rearrange("p (h c) -> p h c", h=2),
                              ACT.Gelu_apprx_tanh, bias=sm[:, 140 + v:141 + v]).then_inc(sem("hidden"), up("hidden", (u, v), frees=[("psum", (u, "hid", v))]))
                        ac.wait_ge(sem("hidden"), now("hidden"))
                    else:
                        hv = hid_of(u, v)
                        a(act(hv[:, :, 31:32], cst[:, K_ROT:K_ROT + 2].rearrange("p (h c) -> p h c", h=2), ACT.Copy, scale=0.0))
                        act(hv[:, :, 0:31], pst[:, b, 0:62].rearrange("p (h c) -> p h c", h=2),
                              ACT.Gelu_apprx_tanh, bias=sm[:, 140 + v:141 + v]).then_inc(sem("hidden"), up("hidden", (u, v), frees=[("psum", (u, "hid", v))]))
                        ac.wait_ge(sem("hidden"), now("hidden"))

            for l in range(DEPTH):
                if l == 0:
                    squares(l, 0, xT, actT, lambda k: None)
                else:
                    squares(l, 0, xT, actT, lambda k: ac.wait_ge(sem("x_added"), after("x_added", (l - 1, 3, k))))
                ac.wait_ge(sem("eps_set"), after("eps_set", 0))
                root(l, 0)
                ac.wait_ge(sem("lam_abs"), after("lam_abs", l))
                a(act(sm[:, 108:112], sm[:, 104:108], ACT.Exp))
                act(sm[:, 112:116], sm[:, 108:112], ACT.Ln, bias=1.0).then_inc(sem("lam_exp"), up("lam_exp", l))
                ac.wait_ge(sem("lam_exp"), now("lam_exp"))
                for j in range(RJ):
                    ac.wait_ge(sem("projected"), after("projected", (l, "xr", j)))
                    b = psk((l, "xr", j))
                    if j == 0:
                        ac.wait_ge(sem("h_ready"), after("h_ready", (l, 0, KT - 1)))
                    else:
                        ac.wait_ge(sem("y_ready"), after("y_ready", (l, j - 1)))
                    a(act(xrp[:, 3:3 + TH], pst[:, b, 0:TH], ACT.Copy))
                    a(act(xrp[:, 3 + TH:3 + SEQ], pst[:, b + 1, 0:SEQ - TH], ACT.Copy))
                    xs = xrp[:, 3 + SEQ:].rearrange("p (b c) -> p b c", b=DB)
                    act(xs[:, :, 3:7], pst[:, b + 1, SEQ - TH:TH].rearrange("p (b c) -> p b c", b=DB), ACT.Copy).then_inc(sem("xr_copied"), up("xr_copied", (l, j), frees=[("psum", (l, "xr", j))]))
                    ac.wait_ge(sem("xr_copied"), now("xr_copied"))
                    ac.wait_ge(sem("projected"), after("projected", (l, "gate", j)))
                    b = psk((l, "gate", j))
                    if l:
                        ac.wait_ge(sem("states_stored"), after("states_stored", l - 1))
                    act(halves(gR), pair(b), ACT.Gelu_apprx_tanh).then_inc(sem("gate_ready"), up("gate_ready", (l, j), frees=[("psum", (l, "gate", j))]))
                    ac.wait_ge(sem("gate_ready"), now("gate_ready"))
                    ac.wait_ge(sem("lambda_ready"), after("lambda_ready", l))
                    ac.wait_ge(sem("projected"), after("projected", (l, "rg", j, 0)))
                    b = psk((l, "rg", j, 0))
                    act(halves(rt), pair(b), ACT.Tanh, scale=0.5, bias=sm[:, 20 + j:21 + j]).then_inc(sem("scalar_step"), up("scalar_step", frees=[("psum", (l, "rg", j, 0))]))
                    ac.wait_ge(sem("scalar_step"), now("scalar_step"))
                    ac.wait_ge(sem("projected"), after("projected", (l, "rg", j, 1)))
                    b = psk((l, "rg", j, 1))
                    act(halves(iR), pair(b), ACT.Tanh, scale=0.5, bias=sm[:, 24 + j:25 + j]).then_inc(sem("i_ready"), up("i_ready", (l, j), frees=[("psum", (l, "rg", j, 1))]))
                    ac.wait_ge(sem("i_ready"), now("i_ready"))
                    act(tR, rt, ACT.Tanh, scale=sm[:, 28 + j:29 + j], bias=sm[:, 28 + j:29 + j]).then_inc(sem("t_ready"), up("t_ready", (l, j)))
                    ac.wait_ge(sem("t_ready"), now("t_ready"))
                    act(aR, rt, ACT.Exp, scale=sm[:, 28 + j:29 + j], bias=sm[:, 28 + j:29 + j]).then_inc(sem("a_ready"), up("a_ready", (l, j)))
                    ac.wait_ge(sem("a_ready"), now("a_ready"))
                    ac.wait_ge(sem("f_ready"), after("f_ready", (l, j)))
                    act(rt, tR, ACT.Sqrt, scale=-0.5).then_inc(sem("s_ready"), up("s_ready", (l, j)))
                    ac.wait_ge(sem("s_ready"), now("s_ready"))
                for g in range(GR):
                    ac.wait_ge(sem("projected"), after("projected", (l, "q", g)))
                    b = psk((l, "q", g))
                    act(halves(qcT[:, g, :]), pair(b), ACT.Copy, scale=HD ** -0.5).then_inc(sem("q_copied"), up("q_copied", (l, g), frees=[("psum", (l, "q", g))]))
                    ac.wait_ge(sem("q_copied"), now("q_copied"))
                for n in ("s1", "w1", "c0", "c1"):
                    ac.wait_ge(sem("projected"), after("projected", (l, "kv", n)))
                    b = psk((l, "kv", n))
                    ac.wait_ge(sem("y_ready"), after("y_ready", (l, RJ - 1)))
                    if n[0] == "c":
                        ac.wait_ge(sem("k_roped"), after("k_roped", (l, "w")))
                    v = int(n[1])
                    dst = kvt[n[0]][:, :, v * P:(v + 1) * P]
                    a(act(dst[:, 0:4, :], pst[:, b, :].rearrange("p (t c) -> p t c", t=4), ACT.Copy))
                    act(dst[0:NS, 4, :], pst[0:NS, b + 1, 0:P], ACT.Copy).then_inc(sem("kv_copied"), up("kv_copied", (l, n[0]) if v else None, frees=[("psum", (l, "kv", n))]))
                    ac.wait_ge(sem("kv_copied"), now("kv_copied"))
                ac.wait_ge(sem("projected"), after("projected", (l, "gl")))
                b = psk((l, "gl"))
                a(act(gates[:, 0:4, :], pst[:, b, 0:96].rearrange("p (t c) -> p t c", t=4), ACT.Tanh, scale=0.5))
                act(gates[0:NS, 4, :], pst[0:NS, b, 96:120], ACT.Tanh, scale=0.5).then_inc(sem("gates_tanh"), up("gates_tanh", l, frees=[("psum", (l, "gl"))]))
                ac.wait_ge(sem("gates_tanh"), now("gates_tanh"))
                for n in "sw":
                    ac.wait_ge(sem("k_turned"), after("k_turned", (l, n)))
                    b = psk((l, "kT", n))
                    act(kT[n], flat(b, T), ACT.Copy).then_inc(sem("kT_copied"), up("kT_copied", (l, n), frees=[("psum", (l, "kT", n))]))
                    ac.wait_ge(sem("kT_copied"), now("kT_copied"))
                us = [(l, "cmp", x) for x in range(DB)] + [(l, "cmpp", 0)]
                for i, u in enumerate(us):
                    compress(u, us[i - 1] if i else (l - 1, "cmpp", 0) if l else None)
                for G in range(2):
                    ac.wait_ge(sem("neg_max"), after("neg_max", (l, G, "cs")))
                    b = psk((l, G, "Scs"))
                    act(sS[:, G * P:G * P + 127], pst[:, b, 0:127], ACT.Exp, bias=sm[:, 40 + G:41 + G], accum_out=sm[:, 42 + G:43 + G]).then_inc(sem("p_exp"), up("p_exp", (l, G, "cs"), frees=[("psum", (l, G, "Scs"))]))
                    ac.wait_ge(sem("p_exp"), now("p_exp"))
                todo = [(i, br, g) for i in range(4) for br in "sw" for g in range(4)]

                def p_exp(n):
                    u = todo[n]
                    i, br, g = u
                    for h in range(2):
                        m = 2 * n + h
                        ac.wait_ge(sem("neg_max"), after("neg_max", (l, u, h)))
                        if m >= 4:
                            for s, n_ in freed(("p", l, m - 4)):
                                ac.wait_ge(s, n_)
                        b = psk((l, u, "S", h))
                        L = (i + 1) * P
                        col = 176 + 16 * (i % 2) + (0 if br == "s" else 8) + g * 2 + h
                        act(p_slot(m)[:, 0:L], pst[:, b, 0:L], ACT.Exp, bias=sm[:, 48 + m % 8:49 + m % 8],
                              accum_out=sm[:, col:col + 1]).then_inc(sem("p_exp"), up("p_exp", (l, u, h), frees=[("psum", (l, u, "S", h)), ("nm", l, m)]))
                        ac.wait_ge(sem("p_exp"), now("p_exp"))

                def p_copy(n):
                    u = todo[n]
                    sl = S.slot_of[l, u, 1]
                    ac.wait_ge(sem("turned"), after("turned", (l, u, 1)))
                    for s, n_ in freed(("ts", sl - NTS)):
                        ac.wait_ge(s, n_)
                    L = (u[0] + 1) * P
                    b = psk((l, u, "T", 1))
                    act(tv(sl)[:, 0:L], pst[:, b, 0:L], ACT.Copy).then_inc(sem("copied_a"), up("copied_a", (l, u, 1), frees=[("psum", (l, u, "T", 1))]))
                    ac.wait_ge(sem("copied_a"), now("copied_a"))

                ac.wait_ge(sem("turned"), after("turned", (l, 1, "cs")))
                for n in range(len(todo) + 1):
                    if n < len(todo):
                        if n % 8 == 0 and n >= 16:
                            ac.wait_ge(sem("l_read"), after("l_read", (l, todo[n][0] - 2)))
                        p_exp(n)
                    if n >= 1:
                        p_copy(n - 1)
                    if n and n % 8 == 0:
                        i = todo[n - 1][0]
                        ac.wait_ge(sem("cmp_shifted"), after("cmp_shifted", (l, i)))
                        act(pc_p, pc_s, ACT.Exp).then_inc(sem("cmp_exp"), up("cmp_exp", (l, i)))
                        ac.wait_ge(sem("cmp_exp"), now("cmp_exp"))
                for G in range(2):
                    u = (l, "win", G)
                    for e in (1, 3):
                        ac.wait_ge(sem("turned"), after("turned", (u, "kt", e)))
                        sl = S.slot_of[u, "kt", e]
                        for s, n_ in freed(("ts", sl - NTS)):
                            ac.wait_ge(s, n_)
                        act(tv(sl), bank(psk((u, "kt", e))), ACT.Copy).then_inc(sem("copied_a"), up("copied_a", (u, "kt", e), frees=[("psum", (u, "kt", e))]))
                        ac.wait_ge(sem("copied_a"), now("copied_a"))
                    ac.wait_ge(sem("neg_max"), after("neg_max", u))
                    a(act(sS[:, 0:512], sS[:, 0:512], ACT.Exp, bias=sm[:, 88:89], accum_out=sm[:, 90:91]))
                    act(sS[:, 2048:2080], sS[:, 2048:2080], ACT.Exp, bias=sm[:, 88:89], accum_out=sm[:, 91:92]).then_inc(sem("p_exp"), up("p_exp", u))
                    ac.wait_ge(sem("p_exp"), now("p_exp"))
                    for e in range(4):
                        u = (l, "slc", 4 * G + e)
                        for x in (1, 3):
                            ac.wait_ge(sem("turned"), after("turned", (u, "kt", x)))
                            sl = S.slot_of[u, "kt", x]
                            for s, n_ in freed(("ts", sl - NTS)):
                                ac.wait_ge(s, n_)
                            act(tv(sl), bank(psk((u, "kt", x))), ACT.Copy).then_inc(sem("copied_a"), up("copied_a", (u, "kt", x), frees=[("psum", (u, "kt", x))]))
                            ac.wait_ge(sem("copied_a"), now("copied_a"))
                        ac.wait_ge(sem("neg_max"), after("neg_max", u))
                        r = slice(32 * e, 32 * e + 32)
                        act(sS[r, :], sS[r, :], ACT.Exp, bias=sm[r, 89:90], accum_out=sm[r, 92:93]).then_inc(sem("p_exp"), up("p_exp", u))
                        ac.wait_ge(sem("p_exp"), now("p_exp"))
                ac.wait_ge(sem("kv_stored_s"), after("kv_stored_s", l))
                ac.wait_ge(sem("kv_stored_w"), after("kv_stored_w", l))
                for j in range(KT):
                    ac.wait_ge(sem("projected"), after("projected", (l, "out", j)))
                    b = psk((l, "out", j))
                    ac.wait_ge(sem("summed_values"), after("summed_values", ((l, "slc", 7), 0)))
                    a(act(halves(mT[:, j, :]), pair(b), ACT.Copy))
                    act(halves(actT[:, j, :]), pair(b), ACT.Square).then_inc(sem("squared"), up("squared", (l, 1, j), frees=[("psum", (l, "out", j))]))
                    ac.wait_ge(sem("squared"), now("squared"))
                root(l, 1)
                squares(l, 2, xT, actT, lambda k: ac.wait_ge(sem("x_added"), after("x_added", (l, 1, k))))
                root(l, 2)
                for r in range(RND):
                    for f in range(r * FR, (r + 1) * FR):
                        ac.wait_ge(sem("projected"), after("projected", (l, "g", f)))
                        b = psk((l, "g", f))
                        gp = gpad[f % 2]
                        if f == 0:
                            ac.wait_ge(sem("rstd_spread"), after("rstd_spread", (l, 2)))
                        if f >= 2:
                            ac.wait_ge(sem("conv_done"), after("conv_done", (l, "f", f - 2)))
                            for s, n_ in freed(("gpad", l, f - 2)):
                                ac.wait_ge(s, n_)
                        a(act(gp[:, 2:2 + TH], pst[:, b, 0:TH], ACT.Copy))
                        a(act(gp[:, 2 + TH:2 + SEQ], pst[:, b + 1, 0:SEQ - TH], ACT.Copy))
                        gps = gp[:, 2 + SEQ:].rearrange("p (b c) -> p b c", b=DB)
                        act(gps[:, :, 2:6], pst[:, b + 1, SEQ - TH:TH].rearrange("p (b c) -> p b c", b=DB), ACT.Copy).then_inc(sem("g_copied"), up("g_copied", (l, f), frees=[("psum", (l, "g", f))]))
                        ac.wait_ge(sem("g_copied"), now("g_copied"))
                        ac.wait_ge(sem("conv_done"), after("conv_done", (l, "f", f)))
                        if f:
                            ac.wait_ge(sem("act_ready"), after("act_ready", (l, f - 1)))
                        a(act(gF[:, 0:SEQ], cF[:, 0:SEQ], ACT.Gelu_apprx_tanh))
                        act(gF[:, SEQ:T].rearrange("p (b c) -> p b c", b=DB), per6, ACT.Gelu_apprx_tanh).then_inc(sem("gelu_done"), up("gelu_done", (l, f)))
                        ac.wait_ge(sem("gelu_done"), now("gelu_done"))
                    for j in range(KT):
                        ac.wait_ge(sem("projected"), after("projected", (l, "down", r, j)))
                        b = psk((l, "down", r, j))
                        if r == 0:
                            act(halves(mT[:, j, :]), pair(b), ACT.Copy).then_inc(sem("m_copied"), up("m_copied", (l, j), frees=[("psum", (l, "down", r, j))]))
                            ac.wait_ge(sem("m_copied"), now("m_copied"))
                        if r == RND - 1:
                            ac.wait_ge(sem("m_summed"), after("m_summed", (l, r, j)))
                            act(hT[:, j, :], mT[:, j, :], ACT.Square).then_inc(sem("squared"), up("squared", (l, 3, j)))
                            ac.wait_ge(sem("squared"), now("squared"))
                root(l, 3)
                for i, (name, r0, r1) in enumerate(OUTT):
                    ac.wait_ge(sem("states_turned"), after("states_turned", (l, i)))
                    b = psk((l, "st", i))
                    act(st_out[0:r1 - r0, i * P:(i + 1) * P], pst[0:r1 - r0, b, 0:P], ACT.Copy).then_inc(sem("states_copied"), up("states_copied", (l, i), frees=[("psum", (l, "st", i))]))
                    ac.wait_ge(sem("states_copied"), now("states_copied"))

        @block.vector
        def _(ve):

            def v(ins):
                ins.then_inc(sem("vector_step"), up("vector_step"))
                ve.wait_ge(sem("vector_step"), now("vector_step"))

            V = nc.vector
            tt, tsc, stt, cp = V.tensor_tensor, V.tensor_scalar, V.scalar_tensor_tensor, V.tensor_copy
            psk = lambda key: S.bank_of[key]

            def copy_ts(key, cols, rows=P):
                ve.wait_ge(sem("turned"), after("turned", key))
                sl = S.slot_of[key]
                for s, n_ in freed(("ts", sl - NTS)):
                    ve.wait_ge(s, n_)
                b = S.bank_of[S.bank_key[key]]
                cp(tv(sl)[0:rows, 0:cols], pst[0:rows, b, 0:cols]).then_inc(sem("copied_v"), up("copied_v", key, frees=[("psum", S.bank_key[key])]))
                ve.wait_ge(sem("copied_v"), now("copied_v"))

            def masked(u, x, r, G):
                ve.wait_ge(sem("scored"), after("scored", (u, x)))
                y = lambda ap: ap.rearrange("p (s n c) -> p s n c", s=4, c=4)
                m = mb(G)[r, 0:32].unsqueeze(1).unsqueeze(3).broadcast_to([32, 4, 32, 4])
                tt(y(sS[r, x * 512:(x + 1) * 512]), y(pst[r, S.bank_of[u, "S", x], :]), m, ALU.add).then_inc(sem("vector_step"), up("vector_step", frees=[("psum", (u, "S", x))]))
                ve.wait_ge(sem("vector_step"), now("vector_step"))

            def norm(l, n):
                ve.wait_ge(sem("rms_ready"), after("rms_ready", (l, n)))
                v(V.reciprocal(sm[:, 8:12], sm[:, 0:4]))
                v(V.reciprocal(sm[0:NS, 12:13], sm[0:NS, 4:5]))
                for t, (t0, m) in enumerate(TT):
                    x = tsc(diag[0:m, t0:t0 + m], ident[0:m, 0:m], sm[0:m, 8 + t:9 + t], None, ALU.mult)
                    x.then_inc(sem("diag_built" if t == 4 else "vector_step"), up("diag_built" if t == 4 else "vector_step", (l, n) if t == 4 else None))
                    ve.wait_ge(sem("diag_built" if t == 4 else "vector_step"), now("diag_built" if t == 4 else "vector_step"))
                ve.wait_ge(sem("rstd_spread"), after("rstd_spread", (l, n)))

            def pre(l, n, gain):
                norm(l, n)
                b = psk((l, n, "rstd"))
                for k in range(KT):
                    stt(hT[:, k, :], xT[:, k, :], par[:, gain + k:gain + k + 1], flat(b, T), ALU.mult, ALU.mult).then_inc(sem("h_ready"), up("h_ready", (l, n, k), frees=[("psum", (l, n, "rstd"))]))
                    ve.wait_ge(sem("h_ready"), now("h_ready"))

            def post(l, n, gain):
                norm(l, n)
                b = psk((l, n, "rstd"))
                for k in range(KT):
                    stt(mT[:, k, :], mT[:, k, :], par[:, gain + k:gain + k + 1], flat(b, T), ALU.mult, ALU.mult).then_inc(sem("m_scaled"), up("m_scaled", (l, n, k), frees=[("psum", (l, n, "rstd"))]))
                    ve.wait_ge(sem("m_scaled"), now("m_scaled"))

            v(V.memset(sm[:, :], 0.0))
            V.memset(sm[:, 150:151], EPS).then_inc(sem("eps_set"), up("eps_set", 0))
            ve.wait_ge(sem("eps_set"), now("eps_set"))
            ve.wait_ge(sem("pages_loaded"), after("pages_loaded", 0))
            ve.wait_ge(sem("const_loaded"), after("const_loaded", 0))
            v(cp(idx[:, 0:DB], idi[:, 0:DB]))
            v(tsc(idx[:, DB:2 * DB], idx[:, 0:DB], float(CPP), cst[:, K_CH:K_CH + 1], ALU.mult, ALU.add))

            for l in range(DEPTH):
                v(tsc(idx[:, 2 * DB:3 * DB], idx[:, DB:2 * DB], float(l * NPOOL * CPP), None, ALU.add))
                cp(idi[:, (1 + l) * DB:(2 + l) * DB], idx[:, 2 * DB:3 * DB]).then_inc(sem("index_ready"), up("index_ready", 0))
                ve.wait_ge(sem("index_ready"), now("index_ready"))
            for l in range(DEPTH):
                offs = [0, 98, 194, 322, 450, 578, 706]
                for i in range(6):
                    ve.wait_ge(sem("params_turned"), after("params_turned", (l, i)))
                    b = psk((l, "par", i))
                    cp(par[:, offs[i]:offs[i + 1]], pst[:, b, 0:offs[i + 1] - offs[i]]).then_inc(sem("params_ready"), up("params_ready", (l, i), frees=[("psum", (l, "par", i))]))
                    ve.wait_ge(sem("params_ready"), now("params_ready"))
                pre(l, 0, P_NORM)
                v(tsc(sm[:, 20:28], par[:, P_BA:P_BA + 8], 0.5, None, ALU.mult))
                lam = par[:, P_LAM:P_LAM + 4]
                v(tsc(sm[:, 100:104], lam, -1.0, None, ALU.mult))
                tt(sm[:, 104:108], lam, sm[:, 100:104], ALU.min).then_inc(sem("lam_abs"), up("lam_abs", l))
                ve.wait_ge(sem("lam_abs"), now("lam_abs"))
                ve.wait_ge(sem("lam_exp"), after("lam_exp", l))
                y, w = sm[:, 108:112], sm[:, 112:116]
                v(tsc(sm[:, 116:120], y, 1.0, None, ALU.add))
                v(tsc(sm[:, 120:124], sm[:, 116:120], -1.0, None, ALU.add))
                v(tsc(sm[:, 124:128], sm[:, 120:124], 1e-30, None, ALU.max))
                v(V.reciprocal(sm[:, 128:132], sm[:, 124:128]))
                v(tt(sm[:, 132:136], w, y, ALU.mult))
                v(tt(sm[:, 132:136], sm[:, 132:136], sm[:, 128:132], ALU.mult))
                v(stt(sm[:, 120:124], sm[:, 120:124], 0.0, y, ALU.is_equal, ALU.mult))
                v(tt(sm[:, 132:136], sm[:, 132:136], sm[:, 120:124], ALU.add))
                v(tsc(sm[:, 116:120], lam, 0.0, None, ALU.min))
                v(tt(sm[:, 116:120], sm[:, 116:120], sm[:, 132:136], ALU.subtract))
                tsc(sm[:, 28:32], sm[:, 116:120], 4.0, None, ALU.mult).then_inc(sem("lambda_ready"), up("lambda_ready", l))
                ve.wait_ge(sem("lambda_ready"), now("lambda_ready"))
                rc = par[:, P_RC:P_RC + 96].rearrange("p (b w j) -> p b w j", b=DB, w=3)
                h0 = par[:, P_H0:P_H0 + 32].rearrange("p (b j) -> p b j", b=DB)
                for j in range(RJ):
                    xs = xrp[:, 3 + SEQ:].rearrange("p (b c) -> p b c", b=DB)
                    v(V.memset(xrp[:, 0:3], 0.0))
                    v(cp(xs[:, :, 0:3], rc[:, :, :, j]))
                    ve.wait_ge(sem("xr_copied"), after("xr_copied", (l, j)))
                    cw = lambda k: par[:, P_RCW + 4 * k + j:P_RCW + 4 * k + j + 1]
                    v(tsc(cR, xrp[:, 0:568], cw(0), par[:, P_RCB + j:P_RCB + j + 1], ALU.mult, ALU.add))
                    v(stt(cR, xrp[:, 1:569], cw(1), cR, ALU.mult, ALU.add))
                    v(stt(cR, xrp[:, 2:570], cw(2), cR, ALU.mult, ALU.add))
                    v(stt(xc[:, 0:SEQ], xrp[:, 3:3 + SEQ], cw(3), cR[:, 0:SEQ], ALU.mult, ALU.add))
                    stt(xc[:, SEQ:T].rearrange("p (b c) -> p b c", b=DB), xs[:, :, 3:7], cw(3), per7,
                          ALU.mult, ALU.add).then_inc(sem("conv_done"), up("conv_done", (l, j)))
                    ve.wait_ge(sem("conv_done"), now("conv_done"))
                    oc = outr[:, 0:12].rearrange("p (w j) -> p w j", w=3)
                    if j == 0 and l:
                        ve.wait_ge(sem("states_turned"), after("states_turned", (l - 1, 5)))
                    v(cp(oc[:, :, j], xrp[:, SEQ:SEQ + 3]))
                    oc = outr[:, 48:144].rearrange("p (b w j) -> p b w j", b=DB, w=3)
                    v(cp(oc[:, :, :, j], xs[:, :, 4:7]))
                    ve.wait_ge(sem("t_ready"), after("t_ready", (l, j)))
                    v(tsc(recR, tR, -1.0, 1.0, ALU.mult, ALU.add))
                    v(V.reciprocal(recR, recR))
                    tt(tR, tR, recR, ALU.mult).then_inc(sem("f_ready"), up("f_ready", (l, j)))
                    ve.wait_ge(sem("f_ready"), now("f_ready"))
                    v(stt(iR, iR, 1.0, xc, ALU.add, ALU.mult))
                    ve.wait_ge(sem("s_ready"), after("s_ready", (l, j)))
                    v(tt(iR, iR, rt, ALU.mult))
                    a0 = aR[:, SEQ:T].rearrange("p (b c) -> p b c", b=DB)[:, :, 0]
                    b0 = iR[:, SEQ:T].rearrange("p (b c) -> p b c", b=DB)[:, :, 0]
                    v(tt(sm[:, 100:108], a0, h0[:, :, j], ALU.mult))
                    v(tt(b0, b0, sm[:, 100:108], ALU.add))
                    v(V.memset(a0, 0.0))
                    v(V.tensor_tensor_scan(hR, aR, iR, 0.0, ALU.mult, ALU.add))
                    v(cp(outr[:, 12 + j:13 + j], hR[:, SEQ - 1:SEQ]))
                    oh = outr[:, 16:48].rearrange("p (b j) -> p b j", b=DB)
                    v(cp(oh[:, :, j], hR[:, SEQ:T].rearrange("p (b c) -> p b c", b=DB)[:, :, 3]))
                    ve.wait_ge(sem("gate_ready"), after("gate_ready", (l, j)))
                    tt(yT[:, j, :], hR, gR, ALU.mult).then_inc(sem("y_ready"), up("y_ready", (l, j)))
                    ve.wait_ge(sem("y_ready"), now("y_ready"))
                t1, t2 = sS[:, 0:T], sS[:, T:2 * T]
                for g in range(GR):
                    ve.wait_ge(sem("projected"), after("projected", (l, "rot", g)))
                    b = psk((l, "rot", g))
                    v(tt(t1, qcT[:, g, :], cosT, ALU.mult))
                    tt(halves(t2), pair(b), halves(sinT), ALU.mult).then_inc(sem("vector_step"), up("vector_step", frees=[("psum", (l, "rot", g))]))
                    ve.wait_ge(sem("vector_step"), now("vector_step"))
                    tt(qrT[:, g, :], t1, t2, ALU.add).then_inc(sem("q_roped"), up("q_roped", (l, g)))
                    ve.wait_ge(sem("q_roped"), now("q_roped"))
                ve.wait_ge(sem("ov2_zeroed"), after("ov2_zeroed", l))
                for h in range(2):
                    for c, q in ((0, qcT), (1, qrT)):
                        hr = slice(h * HD, (h + 1) * HD)
                        for g in range(GR):
                            dst = qbd[hr, c, :, h * 16 + 4 * g:h * 16 + 4 * g + 4]
                            cp(dst, q[hr, g, SEQ:T].rearrange("p (b t) -> p b t", b=DB)).then_inc(sem("qbd_built" if (h, c, g) == (1, 1, 3) else "vector_step"), up("qbd_built" if (h, c, g) == (1, 1, 3) else "vector_step", l if (h, c, g) == (1, 1, 3) else None))
                            ve.wait_ge(sem("qbd_built" if (h, c, g) == (1, 1, 3) else "vector_step"), now("qbd_built" if (h, c, g) == (1, 1, 3) else "vector_step"))
                for n in "sw":
                    ve.wait_ge(sem("projected"), after("projected", (l, "kv", n + "0")))
                    b = psk((l, "kv", n + "0"))
                    for m, t0, t1_ in ((P, 0, 4), (NS, 4, 5)):
                        nt = t1_ - t0
                        x = flat(b, 640)[0:m, t0 * P:t1_ * P].rearrange("p (t h d) -> p t h d", t=nt, h=2)
                        A = sS[0:m, 0:nt * P].rearrange("p (t h d) -> p t h d", t=nt, h=2)
                        Bb = sS[0:m, 512:512 + nt * P].rearrange("p (t h d) -> p t h d", t=nt, h=2)
                        for h in range(2):
                            v(tt(A[:, :, h], x[:, :, h], cosk[0:m, t0:t1_, :], ALU.mult))
                            v(tt(Bb[:, :, h, 0:32], x[:, :, h, 32:64], sink[0:m, t0:t1_, 0:32], ALU.mult))
                            v(tt(Bb[:, :, h, 32:64], x[:, :, h, 0:32], sink[0:m, t0:t1_, 32:64], ALU.mult))
                        dst = kvt[n][0:m, t0:t1_, 0:P].rearrange("p t (h d) -> p t h d", h=2)
                        dst = kvt[n][0:m, t0:t1_, 0:P]
                        A2 = sS[0:m, 0:nt * P].rearrange("p (t c) -> p t c", t=nt)
                        B2 = sS[0:m, 512:512 + nt * P].rearrange("p (t c) -> p t c", t=nt)
                        tt(dst, A2, B2, ALU.add).then_inc(sem("k_roped" if nt == 1 else "vector_step"), up("k_roped" if nt == 1 else "vector_step", (l, n) if nt == 1 else None, frees=[("psum", (l, "kv", n + "0"))] if nt == 1 else []))
                        ve.wait_ge(sem("k_roped" if nt == 1 else "vector_step"), now("k_roped" if nt == 1 else "vector_step"))
                ve.wait_ge(sem("gates_tanh"), after("gates_tanh", l))
                v(tsc(gates[:, 0:4, :], gates[:, 0:4, :], 0.5, 0.5, ALU.mult, ALU.add))
                tsc(gates[0:NS, 4, :], gates[0:NS, 4, :], 0.5, 0.5, ALU.mult, ALU.add).then_inc(sem("gates_ready"), up("gates_ready", l))
                ve.wait_ge(sem("gates_ready"), now("gates_ready"))
                ve.wait_ge(sem("gates_spread"), after("gates_spread", l))
                b = psk((l, "gsel"))
                for G in range(2):
                    x = pst[:, b, 24 * G:24 * G + 24].rearrange("p (n c) -> p c n", c=3)
                    tmp = sm[:, 100:124].rearrange("p (c n) -> p c n", c=3)
                    tt(tmp, x, cst[:, K_PICK:K_PICK + 24].rearrange("p (c n) -> p c n", c=3), ALU.mult).then_inc(sem("vector_step"), up("vector_step", frees=[("psum", (l, "gsel"))]))
                    ve.wait_ge(sem("vector_step"), now("vector_step"))
                    v(V.tensor_reduce(gs[:, G, :], tmp, AX.X, ALU.add))
                ve.wait_ge(sem("pe_summed"), after("pe_summed", l))
                b = psk((l, "pe"))
                tt(sm[:, 140:142], pst[:, b, 0:2], par[:, P_B1:P_B1 + 2], ALU.add).then_inc(sem("b1_ready"), up("b1_ready", l, frees=[("psum", (l, "pe"))]))
                ve.wait_ge(sem("b1_ready"), now("b1_ready"))
                for u in [(l, "cmp", x) for x in range(DB)] + [(l, "cmpp", 0)]:
                    nch = NCH if u[1] == "cmp" else NCP
                    for vv in range(2):
                        for s4 in (0, 2):
                            copy_ts((u, "xt", vv, s4), 4 * nch)
                    if u[1] == "cmpp":
                        ve.wait_ge(sem("hidden"), after("hidden", (u, 1)))
                        hv = hid_of(u, 1)
                        for h in range(2):
                            for r in range(4):
                                last = (h, r) == (1, 3)
                                cp(hidrep[:, h, 32 * r:32 * r + 32], hv[:, h, :]).then_inc(sem("hidden_rep" if last else "vector_step"), up("hidden_rep" if last else "vector_step", (u, 1) if last else None))
                                ve.wait_ge(sem("hidden_rep" if last else "vector_step"), now("hidden_rep" if last else "vector_step"))
                    for vv in range(2):
                        ve.wait_ge(sem("compressed2"), after("compressed2", (u, vv)))
                        b = psk((u, "c2", vv))
                        fr = [("psum", (u, "c2", vv))]
                        if u[1] == "cmp":
                            if vv == 0:
                                cp(kcT[:, u[2], :], pst[:, b, 0:127]).then_inc(sem("copied_v"), up("copied_v", (u, "kc"), frees=fr))
                                ve.wait_ge(sem("copied_v"), now("copied_v"))
                            else:
                                cp(vc[0:127, u[2], :], pst[0:127, b, 0:P]).then_inc(sem("copied_v"), up("copied_v", (u, "vc"), frees=fr))
                                ve.wait_ge(sem("copied_v"), now("copied_v"))
                        elif vv == 0:
                            cp(kcTp[:, :], pst[:, b, 0:32]).then_inc(sem("vector_step"), up("vector_step", frees=fr))
                            ve.wait_ge(sem("vector_step"), now("vector_step"))
                        else:
                            for g in range(4):
                                cp(vbd[32 * g:32 * g + 32, :, g, :], pst[32 * g:32 * g + 32, b, 0:P].rearrange("p (h d) -> p h d", h=2)).then_inc(sem("vbd_built" if g == 3 else "vector_step"), up("vbd_built" if g == 3 else "vector_step", l if g == 3 else None, frees=fr if g == 3 else []))
                                ve.wait_ge(sem("vbd_built" if g == 3 else "vector_step"), now("vbd_built" if g == 3 else "vector_step"))
                v(V.memset(pp[:, :], 0.0))
                ve.wait_ge(sem("kv_stored_c"), after("kv_stored_c", l))
                for G in range(2):
                    ve.wait_ge(sem("scored"), after("scored", (l, G, "cs")))
                    b = psk((l, G, "Scs"))
                    V.tensor_reduce(sm[:, 40 + G:41 + G], pst[:, b, 0:127], AX.X, ALU.max, negate=True).then_inc(sem("neg_max"), up("neg_max", (l, G, "cs")))
                    ve.wait_ge(sem("neg_max"), now("neg_max"))
                    ve.wait_ge(sem("p_exp"), after("p_exp", (l, G, "cs")))
                    v(tsc(sm[:, 44:45], sm[:, 42 + G:43 + G], 1e-30, None, ALU.max))
                    v(V.reciprocal(sm[:, 45:46], sm[:, 44:45]))
                    pn = sS[:, G * P:G * P + 127]
                    tsc(pn, pn, sm[:, 45:46], None, ALU.mult).then_inc(sem("pn_ready"), up("pn_ready", (l, G)))
                    ve.wait_ge(sem("pn_ready"), now("pn_ready"))
                    ve.wait_ge(sem("group_summed"), after("group_summed", (l, G)))
                    b = psk((l, G, "gsum"))
                    cp(pp[:, 1:128], pst[:, b, 0:127]).then_inc(sem("vector_step"), up("vector_step", frees=[("psum", (l, G, "gsum"))]))
                    ve.wait_ge(sem("vector_step"), now("vector_step"))
                    sc = sm[:, 100:133]
                    v(V.tensor_reduce(sc, pp[:, 0:132].rearrange("p (n r) -> p n r", r=4), AX.X, ALU.add))
                    v(tt(sc, sc, pp[:, 4:136].rearrange("p (n r) -> p n r", r=4)[:, :, 0], ALU.add))
                    v(V.memset(sm[:, 100:101], BIG))
                    v(V.memset(sm[:, 131:133], BIG))
                    for r in range(2):
                        v(V.max(sm[:, 80:88], sc))
                        v(V.match_replace(sc, sm[:, 80:88], sc, -1.0))
                    tsc(mb(G), sc, 0.0, -BIG, ALU.is_ge, ALU.mult).then_inc(sem("selected"), up("selected", (l, G)))
                    ve.wait_ge(sem("selected"), now("selected"))
                    copy_ts((l, G, "cs"), P, 127)
                    ve.wait_ge(sem("summed_values"), after("summed_values", (l, G, "cs")))
                    b = psk((l, G, "Ocs"))
                    tsc(comb[:, G, :], pst[:, b, 0:P], gs[:, G, 0:1], None, ALU.mult).then_inc(sem("vector_step"), up("vector_step", frees=[("psum", (l, G, "Ocs"))]))
                    ve.wait_ge(sem("vector_step"), now("vector_step"))
                todo = [(i, br, g) for i in range(4) for br in "sw" for g in range(4)]

                def p_max(n):
                    u = todo[n]
                    i = u[0]
                    L = (i + 1) * P
                    for h in range(2):
                        m = 2 * n + h
                        ve.wait_ge(sem("scored"), after("scored", (l, u, h)))
                        b = psk((l, u, "S", h))
                        dg = pst[:, b, L - P:L]
                        v(tt(dg, dg, cst[:, K_CAUS:K_CAUS + P], ALU.add))
                        for s, n_ in freed(("nm", l, m - 8)):
                            ve.wait_ge(s, n_)
                        V.tensor_reduce(sm[:, 48 + m % 8:49 + m % 8], pst[:, b, 0:L], AX.X, ALU.max, negate=True).then_inc(sem("neg_max"), up("neg_max", (l, u, h)))
                        ve.wait_ge(sem("neg_max"), now("neg_max"))

                def gate_o(i):
                    gt = gates[:, i, :].rearrange("p (h g c) -> p g h c", h=2, g=GR)
                    gh = lambda ap: ap.rearrange("p (g h) -> p g h", g=GR)
                    ov3 = o_sb.rearrange("p (n d) -> p n d", n=8)
                    for c, br in ((1, "s"), (2, "w"), (0, "c")):
                        if br == "c":
                            ve.wait_ge(sem("scored"), after("scored", (l, i, "c")))
                            sc3 = pc_s.rearrange("p (n c) -> p n c", n=8)
                            pc3 = pc_p.rearrange("p (n c) -> p n c", n=8)
                            cm = cst[:, K_CMPM + i * NCP:K_CMPM + (i + 1) * NCP]
                            for h in range(2):
                                x = pst[:, psk((l, i, "Sc", h)), 0:P].rearrange("p (n c) -> p n c", n=4)
                                tt(sc3[:, 4 * h:4 * h + 4], x, cm.unsqueeze(1).broadcast_to([P, 4, NCP]), ALU.add).then_inc(sem("vector_step"), up("vector_step", frees=[("psum", (l, i, "Sc", h))]))
                                ve.wait_ge(sem("vector_step"), now("vector_step"))
                            v(V.tensor_reduce(sm[:, 100:108], sc3, AX.X, ALU.max))
                            v(tsc(sm[:, 100:108], sm[:, 100:108], -0.1 * BIG, None, ALU.max))
                            tt(sc3, sc3, sm[:, 100:108].unsqueeze(2).broadcast_to([P, 8, NCP]), ALU.subtract).then_inc(sem("cmp_shifted"), up("cmp_shifted", (l, i)))
                            ve.wait_ge(sem("cmp_shifted"), now("cmp_shifted"))
                            ve.wait_ge(sem("cmp_exp"), after("cmp_exp", (l, i)))
                            copy_ts((l, i, "c"), 256)
                            v(V.tensor_reduce(sm[:, 108:116], pc3, AX.X, ALU.add))
                            v(tsc(sm[:, 108:116], sm[:, 108:116], 1e-30, None, ALU.max))
                            lcol = sm[:, 108:116]
                            ve.wait_ge(sem("summed_values"), after("summed_values", (l, i, "c")))
                        else:
                            lc = 176 + 16 * (i % 2) + (0 if br == "s" else 8)
                            lcol = sm[:, lc:lc + 8]
                            ve.wait_ge(sem("summed_values"), after("summed_values", (l, (i, br, 3), 1)))
                        if br == "c":
                            v(cp(gh(sm[:, 124:132]), lcol.rearrange("p (h g) -> p g h", h=2)))
                            lcol = sm[:, 124:132]
                        V.reciprocal(sm[:, 116:124], lcol).then_inc(sem("l_read" if br == "w" else "vector_step"), up("l_read" if br == "w" else "vector_step", (l, i) if br == "w" else None))
                        ve.wait_ge(sem("l_read" if br == "w" else "vector_step"), now("l_read" if br == "w" else "vector_step"))
                        v(tt(gh(sm[:, 116:124]), gh(sm[:, 116:124]), gt[:, :, :, c], ALU.mult))
                        b = psk((l, i, br, "O"))
                        cf = sm[:, 116:124].unsqueeze(2).broadcast_to([P, 8, HD])
                        dst = ov3 if br == "s" else o_tmp.rearrange("p (n d) -> p n d", n=8)
                        if br == "s" and i:
                            ve.wait_ge(sem("o_turned"), after("o_turned", (l, i - 1)))
                        tt(dst, pst[:, b, :].rearrange("p (n d) -> p n d", n=8), cf, ALU.mult).then_inc(sem("vector_step"), up("vector_step", frees=[("psum", (l, i, br, "O"))]))
                        ve.wait_ge(sem("vector_step"), now("vector_step"))
                        if br != "s":
                            tt(o_sb, o_sb, o_tmp, ALU.add).then_inc(sem("o_gated" if br == "c" else "vector_step"), up("o_gated" if br == "c" else "vector_step", (l, i) if br == "c" else None))
                            ve.wait_ge(sem("o_gated" if br == "c" else "vector_step"), now("o_gated" if br == "c" else "vector_step"))
                    ve.wait_ge(sem("o_turned"), after("o_turned", (l, i)))
                    b = psk((l, i, "oT"))
                    cp(hT[:, 0:4, i * P:(i + 1) * P], pst[:, b, :].rearrange("p (g q) -> p g q", g=4)).then_inc(sem("oT_copied"), up("oT_copied", (l, i), frees=[("psum", (l, i, "oT"))]))
                    ve.wait_ge(sem("oT_copied"), now("oT_copied"))

                ve.wait_ge(sem("gates_spread"), after("gates_spread", l))
                for n in range(len(todo) + 2):
                    if n < len(todo):
                        p_max(n)
                    if 1 <= n <= len(todo):
                        copy_ts((l, todo[n - 1], 0), (todo[n - 1][0] + 1) * P)
                    if n >= 2 and (n - 2) % 8 == 7:
                        gate_o(todo[n - 2][0])
                for G in range(2):
                    u = (l, "win", G)
                    for e in (0, 2):
                        copy_ts((u, "kt", e), 512)
                    ve.wait_ge(sem("scored"), after("scored", (u, 3)))
                    b, b2 = psk((u, "S")), psk((u, "Sn"))
                    if G:
                        ve.wait_ge(sem("turned"), after("turned", ((l, "slc", 3), "ptn")))
                    cp(sS[:, 0:512], bank(b)).then_inc(sem("vector_step"), up("vector_step", frees=[("psum", (u, "S"))]))
                    ve.wait_ge(sem("vector_step"), now("vector_step"))
                    w0 = sS[:, 0:512].rearrange("p (s c) -> p s c", s=4)[:, :, 0]
                    v(tt(w0, w0, cst[:, K_WINM:K_WINM + 4], ALU.add))
                    nm = cst[:, K_NEWM + G * NS:K_NEWM + (G + 1) * NS]
                    tt(sS[:, 2048:2080], pst[:, b2, 0:NS], nm, ALU.add).then_inc(sem("vector_step"), up("vector_step", frees=[("psum", (u, "Sn"))]))
                    ve.wait_ge(sem("vector_step"), now("vector_step"))
                    v(V.tensor_reduce(sm[:, 94:95], sS[:, 0:512], AX.X, ALU.max))
                    v(V.tensor_reduce(sm[:, 95:96], sS[:, 2048:2080], AX.X, ALU.max))
                    V.tensor_reduce(sm[:, 88:89], sm[:, 94:96], AX.X, ALU.max, negate=True).then_inc(sem("neg_max"), up("neg_max", u))
                    ve.wait_ge(sem("neg_max"), now("neg_max"))
                    copy_ts((u, "pt"), 512)
                    copy_ts((u, "ptn"), P, NS)
                    v(tt(sm[:, 96:97], sm[:, 90:91], sm[:, 91:92], ALU.add))
                    v(V.reciprocal(sm[:, 97:98], sm[:, 96:97]))
                    v(tt(sm[:, 97:98], sm[:, 97:98], gs[:, G, 2:3], ALU.mult))
                    ve.wait_ge(sem("summed_values"), after("summed_values", (u, 0)))
                    stt(comb[:, G, :], pst[:, psk((u, "O")), 0:P], sm[:, 97:98], comb[:, G, :], ALU.mult, ALU.add).then_inc(sem("vector_step"), up("vector_step", frees=[("psum", (u, "O"))]))
                    ve.wait_ge(sem("vector_step"), now("vector_step"))
                    for e in range(4):
                        u = (l, "slc", 4 * G + e)
                        r = slice(32 * e, 32 * e + 32)
                        for x in range(4):
                            if x in (0, 2):
                                copy_ts((u, "kt", x), 512)
                            if x:
                                masked(u, x - 1, r, G)
                        masked(u, 3, r, G)
                        ve.wait_ge(sem("scored"), after("scored", (u, "n")))
                        tt(sS[r, 2048:2080], pst[r, psk((u, "Sn")), 0:NS], nm[r, :], ALU.add).then_inc(sem("vector_step"), up("vector_step", frees=[("psum", (u, "Sn"))]))
                        ve.wait_ge(sem("vector_step"), now("vector_step"))
                        V.tensor_reduce(sm[r, 89:90], sS[r, :], AX.X, ALU.max, negate=True).then_inc(sem("neg_max"), up("neg_max", u))
                        ve.wait_ge(sem("neg_max"), now("neg_max"))
                        copy_ts((u, "pt"), 512)
                        copy_ts((u, "ptn"), 32, NS)
                    v(V.reciprocal(sm[:, 98:99], sm[:, 92:93]))
                    v(tt(sm[:, 98:99], sm[:, 98:99], gs[:, G, 1:2], ALU.mult))
                    ve.wait_ge(sem("summed_values"), after("summed_values", (u, 0)))
                    stt(comb[:, G, :], pst[:, psk((l, G, "Oslc")), 0:P], sm[:, 98:99], comb[:, G, :], ALU.mult, ALU.add).then_inc(sem("vector_step"), up("vector_step", frees=[("psum", (l, G, "Oslc"))]))
                    ve.wait_ge(sem("vector_step"), now("vector_step"))
                    tt(comb[:, G, :], comb[:, G, :], cst[:, K_HM:K_HM + P], ALU.mult).then_inc(sem("comb_ready"), up("comb_ready", (l, G)))
                    ve.wait_ge(sem("comb_ready"), now("comb_ready"))
                    ve.wait_ge(sem("o_turned"), after("o_turned", (l, "s", G)))
                    b = psk((l, G, "oTs"))
                    for h in range(2):
                        hr = slice(h * HD, (h + 1) * HD)
                        for g in range(GR):
                            src = pst[hr, b, 0:P].rearrange("p (b h g t) -> p b h g t", b=4, h=2, g=4)[:, :, h, g, :]
                            dst = hT[hr, g, SEQ + 16 * G:SEQ + 16 * G + 16].rearrange("p (b t) -> p b t", b=4)
                            last = (h, g) == (1, 3)
                            cp(dst, src).then_inc(sem("oT_copied" if last else "vector_step"), up("oT_copied" if last else "vector_step", (l, "s", G) if last else None, frees=[("psum", (l, G, "oTs"))] if last else []))
                            ve.wait_ge(sem("oT_copied" if last else "vector_step"), now("oT_copied" if last else "vector_step"))
                post(l, 1, P_NORM + 8)
                pre(l, 2, P_NORM + 16)
                for r in range(RND):
                    for f in range(r * FR, (r + 1) * FR):
                        gp = gpad[f % 2]
                        ve.wait_ge(sem("g_copied"), after("g_copied", (l, f)))
                        ve.wait_ge(sem("prefix_copied"), after("prefix_copied", (l, f)))
                        if f:
                            ve.wait_ge(sem("gelu_done"), after("gelu_done", (l, f - 1)))
                        cw = lambda k: par[:, P_FCW + FT * k + f:P_FCW + FT * k + f + 1]
                        v(tsc(cF, gp[:, 0:560], cw(0), par[:, P_FCB + f:P_FCB + f + 1], ALU.mult, ALU.add))
                        v(stt(cF, gp[:, 1:561], cw(1), cF, ALU.mult, ALU.add))
                        stt(cF, gp[:, 2:562], cw(2), cF, ALU.mult, ALU.add).then_inc(sem("conv_done"), up("conv_done", (l, "f", f)))
                        ve.wait_ge(sem("conv_done"), now("conv_done"))
                        ve.wait_ge(sem("gelu_done"), after("gelu_done", (l, f)))
                        ve.wait_ge(sem("projected"), after("projected", (l, "u", f)))
                        if r:
                            ve.wait_ge(sem("projected"), after("projected", (l, "down", r - 1, KT - 1)))
                        b = psk((l, "u", f))
                        tt(halves(actT[:, f % FR, :]), pair(b), halves(gF), ALU.mult).then_inc(sem("act_ready"), up("act_ready", (l, f), frees=[("psum", (l, "u", f))]))
                        ve.wait_ge(sem("act_ready"), now("act_ready"))
                    if r:
                        for j in range(KT):
                            ve.wait_ge(sem("projected"), after("projected", (l, "down", r, j)))
                            b = psk((l, "down", r, j))
                            if r == 1 and j == 0:
                                ve.wait_ge(sem("m_copied"), after("m_copied", (l, KT - 1)))
                            tt(halves(mT[:, j, :]), pair(b), halves(mT[:, j, :]), ALU.add).then_inc(sem("m_summed"), up("m_summed", (l, r, j), frees=[("psum", (l, "down", r, j))]))
                            ve.wait_ge(sem("m_summed"), now("m_summed"))
                post(l, 3, P_NORM + 24)
            ve.wait_ge(sem("x_added"), after("x_added", (DEPTH - 1, 3, KT - 1)))
            ve.wait_ge(sem("states_copied"), after("states_copied", (DEPTH - 1, 5)))
            for k in range(KT):
                for t, (t0, m) in enumerate(TT):
                    ve.wait_ge(sem("y_turned"), after("y_turned", (k, t)))
                    b = psk(("y", k, t))
                    cp(yout[0:m, t, k * P:(k + 1) * P], pst[0:m, b, 0:P]).then_inc(sem("y_copied"), up("y_copied", (k, t), frees=[("psum", ("y", k, t))]))
                    ve.wait_ge(sem("y_copied"), now("y_copied"))
        return S

_INS = ["x_prompt", "x_sample", "cache_cmp_kv", "cache_slc_kv", "cache_win_kv", "state_rg_h", "state_rg_conv",
        "state_ffn_conv", "page_table", "norm_mix_pre", "norm_mix_post", "norm_ffn_pre", "norm_ffn_post", "w_in",
        "rg_conv_w", "rg_conv_b", "rg_wa", "rg_ba", "rg_wx", "rg_bx", "rg_lambda", "cmpk_pe", "cmpk_w1", "cmpk_b1",
        "cmpk_w2", "cmpv_pe", "cmpv_w1", "cmpv_b1", "cmpv_w2", "w_out", "ffn_w_in", "ffn_conv_w", "ffn_conv_b",
        "ffn_w_down"]
_KV = (2, NKV, HD)
_OUTS = {"y_p": (1, SEQ, D), "y_s": (DB, DT, D), "p_cmp": (DEPTH, 1, SEQ) + _KV, "s_cmp": (DEPTH, DB, DT) + _KV,
         "p_slc": (DEPTH, 1, SEQ) + _KV, "s_slc": (DEPTH, DB, DT) + _KV, "p_win": (DEPTH, 1, WIN) + _KV,
         "s_win": (DEPTH, DB, WIN) + _KV, "p_rgh": (DEPTH, 1, DR), "s_rgh": (DEPTH, DB, DR),
         "p_rgc": (DEPTH, 1, 3, DR), "s_rgc": (DEPTH, DB, 3, DR), "p_ffc": (DEPTH, 1, 2, DF), "s_ffc": (DEPTH, DB, 2, DF)}

def kernel(**inputs):
    import concourse.bacc as bacc
    from concourse.bass_utils import run_bass_kernel_spmd

    arrays = {f"in_{n}": np.ascontiguousarray(inputs[n]) for n in _INS}
    arrays["in_consts"] = constants()

    def build(known):
        nc = bacc.Bacc("TRN2", target_bir_lowering=False, num_devices=1)
        ins = {n[3:]: nc.dram_tensor(n, a.shape, mybir.dt.from_np(a.dtype), kind="ExternalInput").ap()
               for n, a in arrays.items()}
        outs = {n: nc.dram_tensor(f"out_{n}", shape, F32, kind="ExternalOutput").ap() for n, shape in _OUTS.items()}
        return nc, hybrid_step(nc, ins, outs, known)

    _, counts = build(None)
    nc, _ = build(counts)
    r = run_bass_kernel_spmd(nc, [arrays], core_ids=[0])
    return tuple(r.results[0][f"out_{n}"] for n in _OUTS)
```

```python
from contextlib import ExitStack

import numpy as np
import concourse.bass as bass
from concourse import mybir

F32 = mybir.dt.float32
I32 = mybir.dt.int32
U32 = mybir.dt.uint32
ALU = mybir.AluOpType
ACT = mybir.ActivationFunctionType
AX = mybir.AxisListType

P = 128
D = 1024
SEQ, DB, DT = 512, 8, 4
NS = DB * DT
T = SEQ + NS
TH = T // 2
DEPTH = 2
PAST, PAGE = 2048, 128
DR = 512
RJ = DR // P
NH, HD, NKV, GR = 8, 64, 2, 4
STRIDE = 16
CPP = PAGE // STRIDE
NCH = PAST // STRIDE
NCP = SEQ // STRIDE
SB = 64
NSB = PAST // SB + 1
WIN = 512
DF = 3072
FT = DF // P
KT = D // P
RND = 3
FR = FT // RND
NIN = 2328
C_GATE, C_Q, C_KVC, C_KVS, C_KVW, C_GL = 512, 1024, 1536, 1792, 2048, 2304
EPS = 1e-6
BIG = 1e30
THETA = 10000.0
TT = [(t * P, min(P, T - t * P)) for t in range(5)]
NPOOL = DB * (PAST // PAGE) * 5 // 4
NW, NA, NTS, NKS = 5, 3, 5, 3

K_ID, K_ROT, K_CH, K_CAUS, K_GSUM, K_HM, K_CMPM, K_NEWM, K_WINM, K_REP, K_PICK = \
    0, 128, 256, 260, 388, 516, 644, 772, 836, 840, 1096
K_COS, K_SIN, K_COSK, K_SINK, K_ALL = 1120, 1120 + T, 1120 + 2 * T, 1120 + 2 * T + 320, 1120 + 2 * T + 640

P_NORM, P_RCW, P_RCB, P_BA, P_BX, P_LAM, P_B1, P_PE, P_N0 = 0, 32, 48, 52, 56, 60, 64, 66, 98
P_FCW, P_FCB = 98, 170
P_H0, P_RC = 194, 226
P_FS = 322
P_ALL = 706

def constants():
    c = np.zeros((P, K_ALL), np.float32)
    c[:, K_ID:K_ID + P] = np.eye(P)
    for m in range(P):
        if m % 64 < 32:
            c[m + 32, K_ROT + m] = -1.0
        else:
            c[m - 32, K_ROT + m] = 1.0
    q = np.arange(P)
    c[:, K_CAUS:K_CAUS + P] = np.where(q[None, :] <= q[:, None], 0.0, -BIG)
    b, h, g, t = q // 32, q // 16 % 2, q // 4 % 4, q % 4
    same = (b[:, None] == b) & (h[:, None] == h) & (t[:, None] == t)
    c[:, K_GSUM:K_GSUM + P] = same
    c[:, K_HM:K_HM + P] = h[:, None] == (q // 64)[None, :]
    ch = np.arange(NCP)
    for i in range(4):
        ok = (ch[None, :] * STRIDE + 2 * STRIDE - 1 <= (i * P + q)[:, None]) & (ch < NCP - 1)[None, :]
        c[:, K_CMPM + i * NCP:K_CMPM + (i + 1) * NCP] = np.where(ok, 0.0, -BIG)
    n = np.arange(NS)
    for G in range(2):
        ok = ((n // DT)[None, :] == (4 * G + b)[:, None]) & ((n % DT)[None, :] <= t[:, None])
        c[:, K_NEWM + G * NS:K_NEWM + (G + 1) * NS] = np.where(ok, 0.0, -BIG)
        c[:NS, K_REP + G * P:K_REP + (G + 1) * P] = ((n // DT)[:, None] == (4 * G + b)[None, :]) & \
            ((n % DT)[:, None] == t[None, :])
    c[:, K_WINM:K_WINM + 4] = np.where(np.arange(4)[None, :] <= t[:, None], -BIG, 0.0)
    for j in range(3):
        c[:, K_PICK + j * 8:K_PICK + j * 8 + 8] = (h * GR + g)[:, None] == np.arange(8)[None, :]
    c[:, K_CH] = q % CPP
    pos = np.concatenate([np.arange(SEQ), PAST + np.arange(NS) % DT]).astype(np.float32)
    half = HD // 2
    freq = (np.float32(THETA) ** (-np.arange(half, dtype=np.float32) / np.float32(half))).astype(np.float32)
    ang = pos[:, None] * freq[None, :]
    cos, sin = np.cos(ang), np.sin(ang)
    c[:, K_COS:K_COS + T] = np.tile(cos.T, (4, 1))
    c[:, K_SIN:K_SIN + T] = np.tile(sin.T, (4, 1))
    for i, (t0, m) in enumerate(TT):
        c[:m, K_COSK + i * 64:K_COSK + i * 64 + 64] = np.tile(cos[t0:t0 + m], (1, 2))
        c[:m, K_SINK + i * 64:K_SINK + i * 64 + 32] = -sin[t0:t0 + m]
        c[:m, K_SINK + i * 64 + 32:K_SINK + i * 64 + 64] = sin[t0:t0 + m]
    return c

class Counts:

    def __init__(self, nc, ctx, known):
        self.nc, self.ctx, self.known = nc, ctx, known
        self.sems, self.count, self.table, self.read = {}, {}, {}, {}
        self.bank_of, self.last_use, self.slot_of, self.bank_key = {}, {}, {}, {}

    def sem(self, name):
        if name not in self.sems:
            self.sems[name] = self.ctx.enter_context(self.nc.semaphore(name))
            self.count[name] = 0
        return self.sems[name]

    def up(self, name, key=None, frees=(), by=1):
        self.count[name] += by
        if key is not None:
            self.table[name, key] = self.count[name]
        for buffer in frees:
            self.read.setdefault(buffer, {})[name] = self.count[name]
        return by

    def now(self, name):
        return self.count[name]

    def after(self, name, key):
        return self.known.table[name, key] if self.known else 1

    def freed(self, buffer):
        if not self.known:
            return []
        return [(self.sem(name), value) for name, value in self.known.read.get(buffer, {}).items()]

def hybrid_step(nc, I, O, known=None):
    ctx = ExitStack()
    with ctx:
        S = Counts(nc, ctx, known)
        sem, up, now, after, freed = S.sem, S.up, S.now, S.after, S.freed
        sb = lambda name, cols, dt=F32: ctx.enter_context(nc.sbuf_tensor(name, [P, cols], dt))
        xT = sb("xT", KT * T)[:].rearrange("p (k t) -> p k t", k=KT)
        hT = sb("hT", KT * T)[:].rearrange("p (k t) -> p k t", k=KT)
        ov = sb("ov", 12256)
        wr = sb("wr", NW * 1024)[:].rearrange("p (s k c) -> p s k c", s=NW, k=8)
        ar = sb("ar", NA * 4096)
        w1 = sb("w1", 4096)[:].rearrange("p (v s f) -> p v s f", v=2, s=16)
        ts = sb("ts", NTS * 512)
        kcT = sb("kcT", DB * 127)[:].rearrange("p (b c) -> p b c", b=DB)
        vc = sb("vc", DB * P)[:].rearrange("p (b c) -> p b c", b=DB)
        par = sb("par", P_ALL)
        cst = sb("cst", K_ALL)
        ov2 = sb("ov2", 1024)
        free1, freek, freev = (x.rearrange(r) for x, r in ((w1, "p v s f -> p (v s f)"), (kcT, "p b c -> p (b c)"),
                                                           (vc, "p b c -> p (b c)")))
        sQ, sW = free1[:, 0:2080], free1[:, 2080:2624]
        key_slot = lambda n: (free1[:, 2624:3136], free1[:, 3136:3648], freev[:, 0:512])[n % NKS]
        prob_slot = lambda n: (freek[:, 0:512], freev[:, 512:1024])[n % 2]
        new_slot = lambda n: freek[:, 512 + P * (n % 2):512 + P * (n % 2) + P]
        w2 = sb("w2", 128)[:].rearrange("p (v d) -> p v d", v=2)
        wgl = sb("wgl", 8 * 24)[:].rearrange("p (k c) -> p k c", k=8)
        gates = sb("gates", 120)[:].rearrange("p (t c) -> p t c", t=5)
        gs = sb("gs", 6)[:].rearrange("p (g c) -> p g c", g=2)
        hid = sb("hid", 508)
        ones = sb("ones", P)
        sm = sb("sm", 288)
        outr = sb("outr", 144)
        idi = sb("idi", (1 + DEPTH) * DB, I32)
        pst = ctx.enter_context(nc.psum_tensor("ps", [P, 8, 512], F32))

        ident = cst[:, K_ID:K_ID + P]
        rot = cst[:, K_ROT:K_ROT + P]
        cosT, sinT = cst[:, K_COS:K_COS + T], cst[:, K_SIN:K_SIN + T]
        cosk = cst[:, K_COSK:K_COSK + 320].rearrange("p (t d) -> p t d", t=5)
        sink = cst[:, K_SINK:K_SINK + 320].rearrange("p (t d) -> p t d", t=5)

        o3 = lambda a, n: ov[:, a:a + n * T].rearrange("p (k t) -> p k t", k=n)
        yT = o3(0, 4)
        qcT, qrT = o3(2176, 4), o3(4352, 4)
        sS = ov[:, 6528:8608]
        kvt = {"c": ov[:, 6528:7808], "s": ov[:, 8608:9888], "w": ov[:, 9888:11168]}
        kvt = {n: v.rearrange("p (t c) -> p t c", t=5) for n, v in kvt.items()}
        kT = {"s": ov[:, 11168:11712], "w": ov[:, 11712:12256]}
        mT = o3(2176, 8)
        actT = o3(6528, 8)
        diag = ov[:, 10880:11424]
        gpad = [ov[:, 10880 + 562 * i:10880 + 562 * (i + 1)] for i in range(2)]
        cF, gF, fcb = ov[:, 0:560], ov[:, 560:1104], ov[:, 1104:1536]
        R0 = 6825
        xrp = ov[:, R0:R0 + 571]
        cR = ov[:, R0 + 571:R0 + 1139]
        xc, rt, aR, tR, iR, hR, gR = (ov[:, R0 + 1139 + i * T:R0 + 1139 + (i + 1) * T] for i in range(7))
        recR = cR[:, 0:T]
        wbd = ov2[:, :].rearrange("p (v j c) -> p v j c", v=2, j=RJ)
        qbd = ov2[:, 0:512].rearrange("p (v b r) -> p v b r", v=2, b=DB)
        vbd = ov2[:, 512:1024].rearrange("p (h g d) -> p h g d", h=2, g=4)
        stage = lambda i: hid[:, 0:P] if i == 5 else ov[:, 1536 + i * P:1536 + (i + 1) * P]
        st_out = ov[:, 11424:12192]
        h4 = hT[:, 4:8, :].rearrange("p k t -> p (k t)")
        o_sb, o_tmp, pc_s, pc_p = h4[:, 0:512], h4[:, 512:1024], h4[:, 1024:1280], h4[:, 1280:1536]
        hidrep = h4[:, 512:768].rearrange("p (h c) -> p h c", h=2)
        comb = h4[:, 1536:1792].rearrange("p (g c) -> p g c", g=2)
        xs_slot = lambda n: h4[:, 768 * (n % 2):768 * (n % 2) + 512]
        pp, kcTp = h4[:, 1792:1928], h4[:, 1928:1960]
        cmp_p = h4[:, 1960:2087]
        idx = h4[:, 0:3 * DB]
        p_slot = lambda m: sS[:, (m % 4) * 512:(m % 4 + 1) * 512]
        mb = lambda G: sm[:, 208 + 36 * G:208 + 36 * G + 33]
        per7 = ov[:, R0 + 571 + 515:R0 + 571 + 515 + 56].rearrange("p (b c) -> p b c", b=DB)[:, :, 0:DT]
        per6 = ov[:, 514:562].rearrange("p (b c) -> p b c", b=DB)[:, :, 0:DT]
        def hid_of(u, v):
            n = 127 if u[1] == "cmp" else NCP
            return hid[:, v * 254:v * 254 + 2 * n].rearrange("p (h c) -> p h c", h=2)

        OUTT = [("rg", 0, 48), ("rgc", 48, 144), ("pf", 0, 48), ("sf0", 48, 176), ("sf1", 176, 304), ("sf2", 304, 432)]
        xin = ov[:, 2176:2176 + 5 * D].rearrange("p (t d) -> p t d", t=5)
        yout = hT.rearrange("p k t -> p (k t)")[:, 0:4 * D].rearrange("p (t d) -> p t d", t=4)
        youts = ov[0:NS, 0:D]

        halves = lambda ap: ap.rearrange("p (h t) -> p h t", h=2)
        pair = lambda b: pst[:, b:b + 2, 0:TH]
        flat = lambda b, n: pst[:, b:b + 2, :].rearrange("p a c -> p (a c)")[:, 0:n]
        bank = lambda b: pst[:, b, :]
        wv = lambda n: wr[:, n % NW]
        av = lambda n: ar[:, (n % NA) * 4096:(n % NA + 1) * 4096]
        tv = lambda n: ts[:, (n % NTS) * 512:(n % NTS + 1) * 512]

        units = []
        for l in range(DEPTH):
            for j in range(RJ):
                units += [(l, "xr", j), (l, "gate", j)]
            units += [(l, "q", g) for g in range(4)]
            units += [(l, "kv", n) for n in ("s0", "s1", "w0", "w1", "c0", "c1")]
            units += [(l, "out", j) for j in range(KT)]
            for r in range(RND):
                for f in range(r * FR, (r + 1) * FR):
                    units += [(l, "g", f), (l, "u", f)]
                units += [(l, "down", (r, j)) for j in range(KT)]
        unit_no = {u: n for n, u in enumerate(units)}
        loads = []
        for l in range(DEPTH):
            loads += [(l, "cmp", b) for b in range(DB)] + [(l, "cmpp", 0)]
            for G in range(2):
                loads += [(l, "win", G)] + [(l, "slc", 4 * G + b) for b in range(4)]
        load_no = {u: n for n, u in enumerate(loads)}

        todo = [(i, br, g) for i in range(4) for br in "sw" for g in range(GR)]
        sample_units = [(G, e) for G in range(2) for e in (None, 0, 1, 2, 3)]
        PARTS = {"keys0": 0, "keys1": 1, "keys2": 2, "keys3": 3, "exp": 4, "turn": 8, "values": 10, "output": 12}
        START = (1, 4, 7, 10, 13, 16, 19, 22, 25, 28)
        CMP_PARTS = {4: ("scores", 0), 5: ("group", 0), 6: ("values", 0), 8: ("scores", 1)}
        plan = []
        for n in range(len(todo) + 3):
            for s, what in enumerate(("scores", "turn", "values")):
                if 0 <= n - s < len(todo):
                    plan.append(("prompt", what, n - s))
                for i in range(4):
                    for part, at in (("scores", (2, 2)), ("exp", (3, 0)), ("turn", (3, 2)), ("values", (4, 0)), ("output", (10, 1))):
                        if (n - 8 * i, s) == at:
                            plan.append(("tile", part, i))
                if 3 * n + s in (1, 4):
                    plan.append(("sample_cmp", "group" if n == 0 else "values", 1))
                for k, (G, e) in enumerate(sample_units):
                    for part, at in PARTS.items():
                        if 3 * n + s == 3 * START[k] + 2 + at and (part != "output" or e == 3):
                            plan.append(("sample", part, (k, G, e)))

        block = ctx.enter_context(nc.Block())

        @block.tensor
        def _(pe):
            
            cyc = {"pair": 0, "one": 0, "acc": 0, "quad": 0}

            def take(key, kind):
                banks, c, width = {"pair": ((0, 2), "pair", 2), "wide": ((0, 2), "pair", 2), "one": ((4, 5), "one", 1),
                                   "acc": ((6, 7), "acc", 1), "quad": ((0, 1, 2, 3), "quad", 1),
                                   "two": ((0, 1, 2, 3), "quad", 2)}[kind]
                if kind == "two":
                    cyc[c] += cyc[c] % 2
                b = banks[cyc[c] % len(banks)]
                cyc[c] += 2 if kind == "two" else 1
                for x in range(b, b + width):
                    if x in S.last_use:
                        for s, n_ in freed(("psum", S.last_use[x])):
                            pe.wait_ge(s, n_)
                    S.last_use[x] = key
                S.bank_of[key] = b
                return b

            mm = lambda o, a, b, st, sp: nc.tensor.matmul(o, a, b, start=st, stop=sp)

            def weights(u):
                n = unit_no[u]
                pe.wait_ge(sem(f"w_loaded{n % NW}"), after(f"w_loaded{n % NW}", n))
                return wv(n)

            def project(u, rhs, key, ready=None):
                w = weights(u)
                b = take(key, "pair")
                for k in range(KT):
                    if ready:
                        ready(k)
                    for h in range(2):
                        i = mm(pst[:, b + h, 0:TH], w[:, k, :], rhs(k)[:, h * TH:(h + 1) * TH], k == 0, k == KT - 1)
                i.then_inc(sem("projected"), up("projected", key, frees=[("w", unit_no[u])]))

            def stats(l, n, sq):
                b = take((l, n, "sum"), "one")
                for k in range(KT):
                    pe.wait_ge(sem("squared"), after("squared", (l, n, k)))
                    for t, (t0, m) in enumerate(TT):
                        i = nc.tensor.matmul(pst[0:m, b, t:t + 1], sq[:, k, t0:t0 + m], ones[:, 0:1],
                                             start=(k == 0 and t == 0), stop=(k == KT - 1 and t == 4),
                                             skip_group_check=True)
                i.then_inc(sem("summed"), up("summed", (l, n)))
                b = take((l, n, "rstd"), "wide")
                pe.wait_ge(sem("diag_built"), after("diag_built", (l, n)))
                for t, (t0, m) in enumerate(TT):
                    i = mm(flat(b, T)[:, t0:t0 + m], ones[0:m, :], diag[0:m, t0:t0 + m], True, True)
                i.then_inc(sem("rstd_spread"), up("rstd_spread", (l, n)))

            def turn_params(l):
                rows = [98, 96, 128, 128, 128, 128]
                for i, r in enumerate(rows):
                    b = take((l, "par", i), "one")
                    pe.wait_ge(sem("params_loaded"), after("params_loaded", l))
                    j = nc.tensor.transpose(pst[:, b, 0:r], stage(i)[0:r, :], ident[0:r, 0:r])
                    j.then_inc(sem("params_turned"), up("params_turned", (l, i)))

            pe.wait_ge(sem("const_loaded"), after("const_loaded", 0))
            pe.wait_ge(sem("ones_set"), after("ones_set", 0))
            pe.wait_ge(sem("x_loaded"), after("x_loaded", 0))
            for k in range(KT):
                b = take(("x", k), "wide")
                for t, (t0, m) in enumerate(TT):
                    i = nc.tensor.transpose(flat(b, T)[:, t0:t0 + m], xin[0:m, t, k * P:(k + 1) * P], ident[0:m, 0:m])
                i.then_inc(sem("x_turned"), up("x_turned", k))

            tsn, xsn = [0], [0]

            def slot(key, bank_key=None):
                S.slot_of[key], S.bank_key[key] = tsn[0], bank_key or key
                tsn[0] += 1
                return tsn[0] - 1

            def compress(l, u):
                nch = NCH if u[1] == "cmp" else NCP
                for v in range(2):
                    hb = take((u, "hid", v), "acc")
                    slots = []

                    def turn(s4):
                        b = take((u, "xt", v, s4), "one")
                        pe.wait_ge(sem("rearranged"), after("rearranged", (u, v, s4)))
                        x = xs_slot(xsn[0])
                        for c in range(4):
                            i = nc.tensor.transpose(pst[:, b, c * nch:(c + 1) * nch], x[0:nch, c * P:(c + 1) * P],
                                                    ident[0:nch, 0:nch])
                        i.then_inc(sem("turned"), up("turned", (u, "xt", v, s4), frees=[("xs", xsn[0])]))
                        xsn[0] += 1
                        slots.append(slot((u, "xt", v, s4)))

                    def product(s4):
                        pe.wait_ge(sem("copied_a" if s4 % 2 else "copied_v"), after("copied_a" if s4 % 2 else "copied_v", (u, "xt", v, s4)))
                        x = tv(slots[s4])[:, 0:4 * nch].rearrange("p (e h c) -> p e h c", e=2, h=2)
                        for e in range(2):
                            sp = 2 * s4 + e
                            o = pst[:, hb, 0:2 * (nch - 1)].rearrange("p (h c) -> p h c", h=2)
                            mm(o, w1[:, v, sp, :], x[:, e, :, 0:nch - 1], sp == 0, False)
                            i = mm(o, w1[:, v, 8 + sp, :], x[:, e, :, 1:nch], False, sp == 7)
                        i.then_inc(sem("compressed"), up("compressed", (u, v, s4), frees=[("ts", slots[s4])]))

                    turn(0)
                    turn(1)
                    for s4 in range(4):
                        product(s4)
                        if s4 < 2:
                            turn(s4 + 2)
                for v in range(2):
                    b = take((u, "c2", v), "one")
                    pe.wait_ge(sem("hidden_rep" if u[1] == "cmpp" and v else "hidden"), after("hidden_rep" if u[1] == "cmpp" and v else "hidden", (u, v)))
                    for h in range(2):
                        if v == 0:
                            m = nch - 1 if u[1] == "cmp" else nch
                            i = mm(pst[h * HD:(h + 1) * HD, b, 0:m], w2[:, 0, :], hid_of(u, 0)[:, h, :], True, True)
                        elif u[1] == "cmp":
                            i = mm(pst[0:nch - 1, b, h * HD:(h + 1) * HD], hid_of(u, 1)[:, h, :], w2[:, 1, :], True, True)
                        else:
                            i = mm(pst[:, b, h * HD:(h + 1) * HD], hidrep[:, h, :], w2[:, 1, :], True, True)
                    i.then_inc(sem("compressed2"), up("compressed2", (u, v)))

            def prompt_attention(l):
                st = {}

                def scores(u):
                    i, br, g = u
                    L = (i + 1) * P
                    b = take((l, u, "S"), "two")
                    for h in range(2):
                        j = mm(pst[:, b + h, 0:L], qrT[h * HD:(h + 1) * HD, g, i * P:(i + 1) * P],
                               kT[br][h * HD:(h + 1) * HD, 0:L], True, True)
                    j.then_inc(sem("scored"), up("scored", (l, u)))

                def turn(u):
                    i, br, g = u
                    for h in range(2):
                        st[u] = st.get(u, []) + [slot((l, u, h), (l, u, "T", h))]
                        pe.wait_ge(sem("p_exp"), after("p_exp", (l, u, h)))
                        b = take((l, u, "T", h), "one")
                        for c in range(i + 1):
                            j = nc.tensor.transpose(pst[:, b, c * P:(c + 1) * P],
                                                    p_slot(todo.index(u) * 2 + h)[:, c * P:(c + 1) * P], ident)
                        j.then_inc(sem("turned"), up("turned", (l, u, h), frees=[("p", l, todo.index(u) * 2 + h)]))

                def values(u):
                    i, br, g = u
                    if g == 0:
                        take((l, i, br, "O"), "acc")
                    b = S.bank_of[l, i, br, "O"]
                    for h in range(2):
                        pe.wait_ge(sem("copied_a" if h else "copied_v"), after("copied_a" if h else "copied_v", (l, u, h)))
                        x = tv(st[u][h])
                        hd = g * 2 + h
                        for c in range(i + 1):
                            j = mm(pst[:, b, hd * HD:(hd + 1) * HD], x[:, c * P:(c + 1) * P],
                                   kvt[br][:, c, P + h * HD:P + (h + 1) * HD], c == 0, c == i)
                        j.then_inc(sem("summed_values"), up("summed_values", (l, u, h), frees=[("ts", st[u][h])]))

                def cmp_scores(i):
                    b = take((l, i, "Sc"), "two")
                    for h in range(2):
                        for g in range(GR):
                            j = mm(pst[:, b + h, g * NCP:(g + 1) * NCP],
                                   qcT[h * HD:(h + 1) * HD, g, i * P:(i + 1) * P],
                                   kcTp[h * HD:(h + 1) * HD, :], True, True)
                    j.then_inc(sem("scored"), up("scored", (l, i, "c")))

                def cmp_turn(i):
                    b = take((l, i, "Tc"), "one")
                    n = slot((l, i, "c"), (l, i, "Tc"))
                    pe.wait_ge(sem("cmp_exp"), after("cmp_exp", (l, i)))
                    for h in range(2):
                        j = nc.tensor.transpose(pst[:, b, h * P:(h + 1) * P], pc_p[:, h * P:(h + 1) * P], ident)
                    j.then_inc(sem("turned"), up("turned", (l, i, "c")))

                def cmp_values(i):
                    n = S.slot_of[l, i, "c"]
                    b = take((l, i, "c", "O"), "one")
                    pe.wait_ge(sem("copied_v"), after("copied_v", (l, i, "c")))
                    for h in range(2):
                        j = mm(pst[:, b, :].rearrange("p (g h d) -> p g h d", g=GR, h=2)[:, :, h, :], tv(n)[:, h * P:(h + 1) * P],
                               vbd[:, h].rearrange("p g d -> p (g d)"), True, True)
                    j.then_inc(sem("summed_values"), up("summed_values", (l, i, "c"), frees=[("ts", n)]))

                def turn_o(i):
                    b = take((l, i, "oT"), "one")
                    pe.wait_ge(sem("o_gated"), after("o_gated", (l, i)))
                    for g in range(GR):
                        j = nc.tensor.transpose(pst[:, b, g * P:(g + 1) * P], o_sb[:, g * P:(g + 1) * P], ident)
                    j.then_inc(sem("o_turned"), up("o_turned", (l, i)))

                for who_, what, n in plan:
                    if who_ == "sample":
                        sample_part(l, what, *n)
                    elif who_ == "sample_cmp":
                        sample_cmp(l, what, n)
                    elif who_ == "tile":
                        if what == "scores":
                            cmp_scores(n)
                        elif what == "turn":
                            cmp_turn(n)
                        elif what == "values":
                            cmp_values(n)
                        elif what == "output":
                            turn_o(n)
                    elif what == "scores":
                        scores(todo[n])
                    elif what == "turn":
                        turn(todo[n])
                    else:
                        values(todo[n])

            def sample_cmp(l, part, G):
                if part == "scores":
                    b = take((l, G, "Scs"), "one")
                    for e in range(4):
                        pe.wait_ge(sem("copied_v"), after("copied_v", ((l, "cmp", 4 * G + e), "kc")))
                        pe.wait_ge(sem("qbd_built"), after("qbd_built", l))
                        i = mm(pst[32 * e:32 * e + 32, b, 0:127], qbd[:, 0, 4 * G + e, :], kcT[:, 4 * G + e, :], True, True)
                    i.then_inc(sem("scored"), up("scored", (l, G, "cs")))
                elif part == "group":
                    b = take((l, G, "gsum"), "one")
                    pe.wait_ge(sem("pn_ready"), after("pn_ready", (l, G)))
                    i = mm(pst[:, b, 0:127], cst[:, K_GSUM:K_GSUM + P], cmp_p, True, True)
                    i.then_inc(sem("group_summed"), up("group_summed", (l, G)))
                else:
                    b = take((l, G, "Tcs"), "one")
                    n = slot((l, G, "cs"), (l, G, "Tcs"))
                    i = nc.tensor.transpose(pst[0:127, b, 0:P], cmp_p, ident)
                    i.then_inc(sem("turned"), up("turned", (l, G, "cs")))
                    b = take((l, G, "Ocs"), "one")
                    pe.wait_ge(sem("copied_v"), after("copied_v", (l, G, "cs")))
                    for e in range(4):
                        pe.wait_ge(sem("copied_v"), after("copied_v", ((l, "cmp", 4 * G + e), "vc")))
                        i = mm(pst[32 * e:32 * e + 32, b, 0:P], tv(n)[0:127, 32 * e:32 * e + 32], vc[0:127, 4 * G + e, :], True, True)
                    i.then_inc(sem("summed_values"), up("summed_values", (l, G, "cs"), frees=[("ts", n)]))

            def sample_part(l, part, k, G, e):
                u = (l, "win", G) if e is None else (l, "slc", 4 * G + e)
                n = load_no[u]
                if e is None:
                    a = av(n).rearrange("p (b s c) -> p b s c", b=4, s=4)
                    key_tile = lambda x, s: a[:, x, s, 0:P]
                else:
                    a = av(n).rearrange("p (s c) -> p s c", s=STRIDE)
                    key_tile = lambda x, s: a[:, 4 * x + s, 0:P]
                kn = 4 * (10 * l + k)
                pn = 10 * l + k

                def turn(x):
                    b = take((u, "kt", x), "one")
                    for s in range(4):
                        i = nc.tensor.transpose(pst[:, b, s * P:(s + 1) * P], key_tile(x, s), ident)
                    i.then_inc(sem("turned"), up("turned", (u, "kt", x)))

                def score(x):
                    r = x if e is None else e
                    q = qbd[:, 1, 4 * G + r, :]
                    r = slice(32 * r, 32 * r + 32)
                    if e is not None and x % 2 == 0:
                        take((u, "S", x), "two")
                    if e is None and x == 0:
                        take((u, "S", 0), "quad")
                        take((u, "Sn"), "quad")
                    sbk = S.bank_of[u, "S", 0] if e is None else S.bank_of[u, "S", x - x % 2] + x % 2
                    pe.wait_ge(sem("copied_a" if x % 2 else "copied_v"), after("copied_a" if x % 2 else "copied_v", (u, "kt", x)))
                    i = mm(pst[r, sbk, :], q, key_slot(kn + x), True, True)
                    i.then_inc(sem("scored"), up("scored", (u, x), frees=[("ks", kn + x)]))
                    if e is None:
                        i = mm(pst[r, S.bank_of[u, "Sn"], 0:NS], q, kT["w"][:, SEQ:T], True, True)
                        i.then_inc(sem("scored"), up("scored", (u, x, "n")))

                if part == "keys0":
                    pe.wait_ge(sem(f"a_loaded{n % NA}"), after(f"a_loaded{n % NA}", n))
                    turn(0)
                    turn(1)
                elif part == "keys1":
                    score(0)
                    turn(2)
                elif part == "keys2":
                    score(1)
                    turn(3)
                elif part == "keys3":
                    score(2)
                    score(3)
                    if e is not None:
                        sb2 = take((u, "Sn"), "one")
                        i = mm(pst[32 * e:32 * e + 32, sb2, 0:NS], qbd[:, 1, 4 * G + e, :], kT["s"][:, SEQ:T], True, True)
                        i.then_inc(sem("scored"), up("scored", (u, "n")))
                elif part == "turn" and e is None:
                    b = take((u, "pt"), "one")
                    pe.wait_ge(sem("p_exp"), after("p_exp", u))
                    for s in range(4):
                        i = nc.tensor.transpose(pst[:, b, s * P:(s + 1) * P], sW[:, s * P:(s + 1) * P], ident)
                    i.then_inc(sem("turned"), up("turned", (u, "pt")))
                    b = take((u, "ptn"), "one")
                    i = nc.tensor.transpose(pst[0:NS, b, 0:P], sW[:, 512:512 + NS], ident)
                    i.then_inc(sem("turned"), up("turned", (u, "ptn"), frees=[("sS", u)]))
                elif part == "turn":
                    b = take((u, "pt"), "one")
                    pe.wait_ge(sem("p_exp"), after("p_exp", u))
                    idb = ident[32 * e:32 * e + 32, 32 * e:32 * e + 32]
                    for s in range(16):
                        i = nc.tensor.transpose(pst[:, b, 32 * s:32 * s + 32], sQ[32 * e:32 * e + 32, s * P:(s + 1) * P], idb)
                    i.then_inc(sem("turned"), up("turned", (u, "pt")))
                    b = take((u, "ptn"), "one")
                    i = nc.tensor.transpose(pst[0:NS, b, 0:32], sQ[32 * e:32 * e + 32, 2048:2048 + NS], idb)
                    i.then_inc(sem("turned"), up("turned", (u, "ptn"), frees=[("sS", u)]))
                elif part == "values":
                    b = take((u, "O"), "one")
                    pe.wait_ge(sem("copied_v"), after("copied_v", (u, "ptn")))
                    for x in range(4) if e is None else [e]:
                        o = pst[32 * x:32 * x + 32, b, 0:P]
                        if e is None:
                            for s in range(4):
                                mm(o, prob_slot(pn)[:, s * P + 32 * x:s * P + 32 * x + 32], a[:, x, s, P:2 * P], s == 0, False)
                            i = mm(o, new_slot(pn)[0:NS, 32 * x:32 * x + 32], kvt["w"][0:NS, 4, P:2 * P], False, True)
                        else:
                            for s in range(16):
                                mm(o, prob_slot(pn)[:, 32 * s:32 * s + 32], a[:, s, P:2 * P], s == 0, False)
                            i = mm(o, new_slot(pn)[0:NS, 0:32], kvt["s"][0:NS, 4, P:2 * P], False, True)
                    i.then_inc(sem("summed_values"), up("summed_values", (u, 0), frees=[("pt", pn), ("a", n)]))
                elif part == "output":
                    b = take((l, G, "oTs"), "one")
                    pe.wait_ge(sem("comb_ready"), after("comb_ready", (l, G)))
                    i = nc.tensor.transpose(pst[:, b, 0:P], comb[:, G, :], ident)
                    i.then_inc(sem("o_turned"), up("o_turned", (l, "s", G)))

            for l in range(DEPTH):
                turn_params(l)
                stats(l, 0, actT)
                for j in range(RJ):
                    rd = (lambda k: pe.wait_ge(sem("h_ready"), after("h_ready", (l, 0, k)))) if j == 0 else None
                    project((l, "xr", j), lambda k: hT[:, k, :], (l, "xr", j), rd)
                    project((l, "gate", j), lambda k: hT[:, k, :], (l, "gate", j))
                    pe.wait_ge(sem("wbd_loaded"), after("wbd_loaded", l))
                    pe.wait_ge(sem("conv_done"), after("conv_done", (l, j)))
                    for v in range(2):
                        b = take((l, "rg", j, v), "pair")
                        for h in range(2):
                            i = mm(pst[:, b + h, 0:TH], wbd[:, v, j, :], xc[:, h * TH:(h + 1) * TH], True, True)
                        i.then_inc(sem("projected"), up("projected", (l, "rg", j, v)))
                for g in range(GR):
                    project((l, "q", g), lambda k: hT[:, k, :], (l, "q", g))
                for g in range(GR):
                    b = take((l, "rot", g), "pair")
                    pe.wait_ge(sem("q_copied"), after("q_copied", (l, g)))
                    for h in range(2):
                        i = mm(pst[:, b + h, 0:TH], rot, qcT[:, g, h * TH:(h + 1) * TH], True, True)
                    i.then_inc(sem("projected"), up("projected", (l, "rot", g)))
                for n in ("s0", "s1", "w0", "w1", "c0", "c1"):
                    w = weights((l, "kv", n))
                    b = take((l, "kv", n), "wide")
                    for t, (t0, m) in enumerate(TT):
                        for k in range(KT):
                            i = mm(flat(b, 640)[0:m, t * P:(t + 1) * P], hT[:, k, t0:t0 + m], w[:, k, :], k == 0, k == KT - 1)
                    i.then_inc(sem("projected"), up("projected", (l, "kv", n), frees=[("w", unit_no[l, "kv", n])]))
                b = take((l, "gl"), "one")
                pe.wait_ge(sem("wgl_loaded"), after("wgl_loaded", l))
                for t, (t0, m) in enumerate(TT):
                    for k in range(KT):
                        i = mm(pst[0:m, b, t * 24:(t + 1) * 24], hT[:, k, t0:t0 + m], wgl[:, k, :], k == 0, k == KT - 1)
                i.then_inc(sem("projected"), up("projected", (l, "gl")))
                for n in "sw":
                    b = take((l, "kT", n), "wide")
                    pe.wait_ge(sem("k_roped"), after("k_roped", (l, n)))
                    for t, (t0, m) in enumerate(TT):
                        i = nc.tensor.transpose(flat(b, T)[:, t0:t0 + m], kvt[n][0:m, t, 0:P], ident[0:m, 0:m])
                    i.then_inc(sem("k_turned"), up("k_turned", (l, n)))
                b = take((l, "gsel"), "one")
                pe.wait_ge(sem("gates_ready"), after("gates_ready", l))
                for G in range(2):
                    i = mm(pst[:, b, 24 * G:24 * G + 24], cst[0:NS, K_REP + G * P:K_REP + (G + 1) * P], gates[0:NS, 4, :], True, True)
                i.then_inc(sem("gates_spread"), up("gates_spread", l))
                b = take((l, "pe"), "one")
                pe.wait_ge(sem("w1_loaded"), after("w1_loaded", l))
                for v in range(2):
                    for s in range(16):
                        i = mm(pst[:, b, v:v + 1], w1[:, v, s, :], par[:, P_PE + 16 * v + s:P_PE + 16 * v + s + 1], s == 0, s == 15)
                i.then_inc(sem("pe_summed"), up("pe_summed", l))
                for x, u in enumerate([(l, "cmp", x) for x in range(DB)] + [(l, "cmpp", 0)]):
                    compress(l, u)
                    if x in CMP_PARTS:
                        sample_cmp(l, *CMP_PARTS[x])
                pe.wait_ge(sem("kT_copied"), after("kT_copied", (l, "w")))
                pe.wait_ge(sem("q_roped"), after("q_roped", (l, 3)))
                pe.wait_ge(sem("vbd_built"), after("vbd_built", l))
                prompt_attention(l)
                pe.wait_ge(sem("y_ready"), after("y_ready", (l, RJ - 1)))
                pe.wait_ge(sem("oT_copied"), after("oT_copied", (l, "s", 1)))
                pe.wait_ge(sem("oT_copied"), after("oT_copied", (l, 3)))
                for j in range(KT):
                    project((l, "out", j), lambda k: yT[:, k, :] if k < 4 else hT[:, k - 4, :], (l, "out", j))
                stats(l, 1, actT)
                stats(l, 2, actT)
                for r in range(RND):
                    for f in range(r * FR, (r + 1) * FR):
                        rd = (lambda k: pe.wait_ge(sem("h_ready"), after("h_ready", (l, 2, k)))) if f == 0 else None
                        project((l, "g", f), lambda k: hT[:, k, :], (l, "g", f), rd)
                        project((l, "u", f), lambda k: hT[:, k, :], (l, "u", f))
                    for j in range(KT):
                        rd = (lambda k: pe.wait_ge(sem("act_ready"), after("act_ready", (l, r * FR + k)))) if j == 0 else None
                        project((l, "down", (r, j)), lambda k: actT[:, k, :], (l, "down", r, j), rd)
                stats(l, 3, hT)
                pe.wait_ge(sem("states_ready"), after("states_ready", (l, "ffn")))
                for i in range(6):
                    r0, r1 = OUTT[i][1:3]
                    src = outr[:, r0:r1] if i < 2 else fcb[:, r0:r1]
                    b = take((l, "st", i), "one")
                    j = nc.tensor.transpose(pst[0:r1 - r0, b, 0:P], src, ident)
                    j.then_inc(sem("states_turned"), up("states_turned", (l, i)))
            for k in range(KT):
                pe.wait_ge(sem("x_added_p" if k % 2 else "x_added_v"), after("x_added_p" if k % 2 else "x_added_v", (DEPTH - 1, 3, k)))
                b = take(("y", k), "wide")
                for t, (t0, m) in enumerate(TT):
                    i = nc.tensor.transpose(flat(b, 640)[0:m, t * P:(t + 1) * P], xT[:, k, t0:t0 + m], ident)
                i.then_inc(sem("y_turned"), up("y_turned", k))

        @block.sync
        def _(sp):

            n_ld = [0]

            sp.dma_start(cst[:, 0:K_CAUS], I["consts"][:, 0:K_CAUS])\
                .then_inc(sem("const_loaded"), up("const_loaded", 0, by=16))
            xp, xs = I["x_prompt"], I["x_sample"]
            sp.dma_start(xin[:, 0:4, :], xp.rearrange("a (t p) d -> p (a t) d", p=P))\
                .then_inc(sem("x_loaded"), up("x_loaded", 0, by=16))
            sp.dma_start(xin[0:NS, 4, :], xs.rearrange("b t d -> (b t) d"))\
                .then_inc(sem("x_loaded"), up("x_loaded", 0, by=16))
            sp.dma_start(cst[:, K_CAUS:], I["consts"][:, K_CAUS:])\
                .then_inc(sem("tables_loaded"), up("tables_loaded", 0, by=16))

            def small(l):
                if l:
                    sp.wait_ge(sem("projected"), after("projected", (l - 1, "gl")))
                sp.dma_start(wgl, I["w_in"][l][:, C_GL:NIN].rearrange("(k p) c -> p k c", p=P))\
                    .then_inc(sem("wgl_loaded"), up("wgl_loaded", l, by=16))
                sp.wait_ge(sem("wbd_zeroed"), after("wbd_zeroed", l))
                for v, name in enumerate(("rg_wa", "rg_wx")):
                    for e in range(2):
                        src = I[name][l].rearrange("(j e) c d -> e c j d", e=2)[e]
                        sp.dma_start(wbd[64 * e:64 * e + 64, v, :, 64 * e:64 * e + 64], src)\
                            .then_inc(sem("wbd_loaded"), up("wbd_loaded", l, by=16))
                if l:
                    sp.wait_ge(sem("summed_values"), after("summed_values", ((l - 1, "slc", 7), 0)))
                for v, name in enumerate(("cmpk", "cmpv")):
                    sp.dma_start(w1[:, v], I[name + "_w1"][l].rearrange("(s e) d f -> (e d) s f", e=2))\
                        .then_inc(sem("w1_loaded"), up("w1_loaded", l, by=16))
                    sp.dma_start(w2[:, v, :], I[name + "_w2"][l])\
                        .then_inc(sem("w1_loaded"), up("w1_loaded", l, by=16))

            def params(l):
                if l:
                    sp.wait_ge(sem("projected"), after("projected", (l - 1, "out", KT - 1)))
                r = lambda name: I[name][l]
                row = [0]

                def put(src, n, tile):
                    sp.dma_start(stage(tile)[row[0]:row[0] + n, :], src)\
                        .then_inc(sem("params_loaded"), up("params_loaded", l, by=16))
                    row[0] += n

                for name in ("norm_mix_pre", "norm_mix_post", "norm_ffn_pre", "norm_ffn_post"):
                    put(r(name).rearrange("(k p) -> k p", p=P), KT, 0)
                put(r("rg_conv_w").rearrange("w (k p) -> (w k) p", p=P), 16, 0)
                for name in ("rg_conv_b", "rg_ba", "rg_bx", "rg_lambda"):
                    put(r(name).rearrange("(k p) -> k p", p=P), RJ, 0)
                for name in ("cmpk_b1", "cmpv_b1"):
                    put(r(name).rearrange("(k p) -> k p", p=P), 1, 0)
                for name in ("cmpk_pe", "cmpv_pe"):
                    put(r(name).rearrange("(s e) d -> s (e d)", e=2), 16, 0)
                row[0] = 0
                put(r("ffn_conv_w").rearrange("w (k p) -> (w k) p", p=P), 72, 1)
                put(r("ffn_conv_b").rearrange("(k p) -> k p", p=P), FT, 1)
                row[0] = 0
                put(r("state_rg_h").rearrange("b (k p) -> (b k) p", p=P), 32, 2)
                put(r("state_rg_conv").rearrange("b w (k p) -> (b w k) p", p=P), 96, 2)
                fs = r("state_ffn_conv").rearrange("b w (k p) -> (b w k) p", p=P)
                for t in range(3):
                    sp.dma_start(stage(3 + t), fs[t * P:(t + 1) * P])\
                        .then_inc(sem("params_loaded"), up("params_loaded", l, by=16))

            def new_rows(l):
                for n, out in (("s", "slc"), ("w", "win"), ("c", "cmp")):
                    if n != "c":
                        sp.wait_ge(sem("k_roped"), after("k_roped", (l, n)))
                    sp.wait_ge(sem("kv_copied"), after("kv_copied", (l, n)))
                    kv4 = lambda ap: ap.rearrange("(t p) v h d -> p t (v h d)", p=P)
                    name = f"kv_stored_{n}"
                    sp.dma_start(kv4(O["p_" + out][l, 0]), kvt[n][:, 0:4, :])\
                        .then_inc(sem(name), up(name, l, by=16))
                    if n == "w":
                        for b in range(DB):
                            sp.dma_start(O["s_win"][l, b, WIN - DT:WIN].rearrange("t v h d -> t (v h d)"), kvt[n][b * DT:(b + 1) * DT, 4, :])\
                                .then_inc(sem(name), up(name, l, by=16))
                        for b in range(DB):
                            sp.dma_start(O["s_win"][l, b, 0:WIN - DT].rearrange("(n t) v h d -> n (t v h d)", t=4), I["cache_win_kv"][l, b, DT:WIN].rearrange("(n t) v h d -> n (t v h d)", t=4))\
                                .then_inc(sem("window_moved"), up("window_moved", 0, by=16))
                    else:
                        sp.dma_start(O["s_" + out][l].rearrange("b t v h d -> (b t) (v h d)"), kvt[n][0:NS, 4, :])\
                            .then_inc(sem(name), up(name, l, by=16))

            params(0)
            for n, (l, kind, x) in enumerate(units):
                if (kind, x) == ("xr", 1):
                    small(l)
                if (kind, x) == ("out", 0):
                    new_rows(l)
                if l < DEPTH - 1 and n == unit_no[l, "out", KT - 1] + NW:
                    params(l + 1)
                if n >= NW:
                    for s, n_ in freed(("w", n - NW)):
                        sp.wait_ge(s, n_)
                w, name = wv(n), f"w_loaded{n % NW}"
                win = I["w_in"][l].rearrange("(k p) c -> p k c", p=P)
                if kind in ("xr", "gate", "kv"):
                    c = {"xr": 0, "gate": C_GATE}.get(kind)
                    c = c + x * P if c is not None else {"c": C_KVC, "s": C_KVS, "w": C_KVW}[x[0]] + int(x[1]) * P
                    sp.dma_start(w, win[:, :, c:c + P])\
                        .then_inc(sem(name), up(name, n, by=16))
                elif kind == "q":
                    for h in range(2):
                        c = C_Q + h * 256 + x * HD
                        sp.dma_start(w[:, :, h * HD:(h + 1) * HD], win[:, :, c:c + HD])\
                            .then_inc(sem(name), up(name, n, by=16))
                elif kind == "out":
                    c = slice(x * P, (x + 1) * P)
                    sp.dma_start(w[:, 0:4, :], I["w_out"][l][0:DR, c].rearrange("(k p) c -> p k c", p=P))\
                        .then_inc(sem(name), up(name, n, by=16))
                    for h in range(2):
                        src = I["w_out"][l][DR + h * 256:DR + (h + 1) * 256, c].rearrange("(g d) c -> d g c", d=HD)
                        sp.dma_start(w[h * HD:(h + 1) * HD, 4:8, :], src)\
                            .then_inc(sem(name), up(name, n, by=16))
                elif kind in ("g", "u"):
                    c = (DF if kind == "g" else 0) + x * P
                    sp.dma_start(w, I["ffn_w_in"][l].rearrange("(k p) c -> p k c", p=P)[:, :, c:c + P])\
                        .then_inc(sem(name), up(name, n, by=16))
                else:
                    r, j = x
                    src = I["ffn_w_down"][l][r * D:(r + 1) * D, j * P:(j + 1) * P]
                    sp.dma_start(w, src.rearrange("(k p) c -> p k c", p=P))\
                        .then_inc(sem(name), up(name, n, by=16))
            for n in "swc":
                sp.wait_ge(sem("kv_stored_" + n), after("kv_stored_" + n, DEPTH - 1))
            sp.wait_ge(sem("window_moved"), after("window_moved", 0))

        @block.gpsimd
        def _(po):

            def p(ins):
                ins.then_inc(sem("pool_step"), up("pool_step"))
                po.wait_ge(sem("pool_step"), now("pool_step"))

            nc.gpsimd.memset(ones[:, :], 1.0).then_inc(sem("ones_set"), up("ones_set", 0))
            po.wait_ge(sem("ones_set"), now("ones_set"))
            for c in range(CPP):
                po.dma_start(idi[c:P:CPP, 0:DB], I["page_table"].rearrange("b j -> j b"),
                                      allow_slow_non_contiguous=True).then_inc(sem("pages_loaded"), up("pages_loaded", 0, by=16))
            nload, xsn = [0], [0]

            def cache(upto):
                while nload[0] <= upto:
                    n = nload[0]
                    nload[0] += 1
                    l, kind, x = loads[n]
                    if n >= NA:
                        for s, n_ in freed(("a", n - NA)):
                            po.wait_ge(s, n_)
                    name = f"a_loaded{n % NA}"
                    if kind in ("cmp", "slc"):
                        po.wait_ge(sem("index_ready"), after("index_ready", 0))
                        pool = I["cache_cmp_kv" if kind == "cmp" else "cache_slc_kv"]
                        src = pool.rearrange("l n (c s) v h d -> (l n c) (s v h d)", c=CPP)
                        ixc = idi[:, (1 + l) * DB + x:(1 + l) * DB + x + 1].bitcast(U32)
                        po.indirect_dma_start(av(n), None, src, bass.IndirectOffsetOnAxis(ap=ixc, axis=0)).then_inc(sem(name), up(name, n, by=16))
                    elif kind == "cmpp":
                        po.wait_ge(sem("kv_stored_c"), after("kv_stored_c", l))
                        src = O["p_cmp"][l, 0].rearrange("(n s) v h d -> n (s v h d)", s=STRIDE)
                        po.dma_start(av(n)[0:NCP, :], src).then_inc(sem(name), up(name, n, by=16))
                    else:
                        src = I["cache_win_kv"][l, 4 * x:4 * x + 4].rearrange("b (p s) v h d -> p b (s v h d)", s=4)
                        po.dma_start(av(n).rearrange("p (b c) -> p b c", b=4), src).then_inc(sem(name), up(name, n, by=16))

            A0 = len(loads) // DEPTH
            for l in range(DEPTH):
                if l:
                    po.wait_ge(sem("projected"), after("projected", (l - 1, "rg", RJ - 1, 1)))
                    po.wait_ge(sem("comb_ready"), after("comb_ready", (l - 1, 1)))
                    po.wait_ge(sem("summed_values"), after("summed_values", ((l - 1, "slc", 7), 0)))
                nc.gpsimd.memset(ov2[:, :], 0.0).then_inc(sem("wbd_zeroed"), up("wbd_zeroed", l))
                po.wait_ge(sem("wbd_zeroed"), now("wbd_zeroed"))
                if l == 0:
                    cache(2)
                po.wait_ge(sem("projected"), after("projected", (l, "rg", RJ - 1, 1)))
                nc.gpsimd.memset(ov2[:, :], 0.0).then_inc(sem("ov2_zeroed"), up("ov2_zeroed", l))
                po.wait_ge(sem("ov2_zeroed"), now("ov2_zeroed"))
                po.wait_ge(sem("projected"), after("projected", (l, "gl")))
                for u in [(l, "cmp", x) for x in range(DB)] + [(l, "cmpp", 0)]:
                    n = load_no[u]
                    cache(n)
                    po.wait_ge(sem(f"a_loaded{n % NA}"), after(f"a_loaded{n % NA}", n))
                    nch = NCH if u[1] == "cmp" else NCP
                    a = av(n).rearrange("p (s c) -> p s c", s=STRIDE)
                    for vv in range(2):
                        for s4 in range(4):
                            for s, n_ in freed(("xs", xsn[0] - 2)):
                                po.wait_ge(s, n_)
                            for e in range(2):
                                r = 4 * s4 + 2 * e
                                src = a[0:nch, r:r + 2, vv * P:(vv + 1) * P].rearrange("p s (h d) -> p h s d", h=2)
                                dst = xs_slot(xsn[0])[0:nch, 256 * e:256 * e + 256].rearrange("p (h s d) -> p h s d", h=2, s=2)
                                nc.gpsimd.tensor_copy(dst, src).then_inc(sem("rearranged" if e else "pool_step"), up("rearranged" if e else "pool_step", (u, vv, s4) if e else None, frees=[("a", n)] if e and vv and s4 == 3 else []))
                                po.wait_ge(sem("rearranged" if e else "pool_step"), now("rearranged" if e else "pool_step"))
                            xsn[0] += 1
                    cache(min(n + NA, l * A0 + A0 - 1))
                cache(l * A0 + A0 - 1)
                if l < DEPTH - 1:
                    cache((l + 1) * A0 + 2)
                for k in range(1, KT, 2):
                    po.wait_ge(sem("m_scaled"), after("m_scaled", (l, 1, k)))
                    nc.gpsimd.tensor_tensor(xT[:, k, :], xT[:, k, :], mT[:, k, :], ALU.add).then_inc(sem("x_added_p"), up("x_added_p", (l, 1, k)))
                    po.wait_ge(sem("x_added_p"), now("x_added_p"))
                po.wait_ge(sem("rstd_spread"), after("rstd_spread", (l, 2)))
                fs = par[:, P_FS:P_FS + 384].rearrange("p (b w f) -> p b w f", b=DB, w=2)
                fo = fcb.rearrange("p (r f) -> p r f", f=FT)
                for f in range(FT):
                    gp = gpad[f % 2]
                    if f < 2:
                        p(nc.gpsimd.memset(gp[:, 0:2], 0.0))
                    else:
                        po.wait_ge(sem("conv_done"), after("conv_done", (l, "f", f - 2)))
                    gps = gp[:, 2 + SEQ:].rearrange("p (b c) -> p b c", b=DB)
                    nc.gpsimd.tensor_copy(gps[:, :, 0:2], fs[:, :, :, f]).then_inc(sem("prefix_copied"), up("prefix_copied", (l, f)))
                    po.wait_ge(sem("prefix_copied"), now("prefix_copied"))
                    po.wait_ge(sem("g_copied"), after("g_copied", (l, f)))
                    p(nc.gpsimd.tensor_copy(fo[:, 0:2, f], gp[:, SEQ:SEQ + 2]))
                    nc.gpsimd.tensor_copy(fo[:, 2:18, f].rearrange("p (b w) -> p b w", b=DB), gps[:, :, 4:6]).then_inc(sem("states_ready"), up("states_ready", (l, f if f < FT - 1 else "ffn"), frees=[("gpad", l, f)]))
                    po.wait_ge(sem("states_ready"), now("states_ready"))
                for k in range(1, KT, 2):
                    po.wait_ge(sem("m_scaled"), after("m_scaled", (l, 3, k)))
                    nc.gpsimd.tensor_tensor(xT[:, k, :], xT[:, k, :], mT[:, k, :], ALU.add).then_inc(sem("x_added_p"), up("x_added_p", (l, 3, k)))
                    po.wait_ge(sem("x_added_p"), now("x_added_p"))
                for i, (name, r0, r1) in enumerate(OUTT):
                    po.wait_ge(sem("states_copied"), after("states_copied", (l, i)))
                    src = st_out[0:r1 - r0, i * P:(i + 1) * P]
                    if i == 0:
                        po.dma_start(O["p_rgc"][l].rearrange("b w (k p) -> (b w k) p", p=P), src[0:12])\
                            .then_inc(sem("states_stored"), up("states_stored", l, by=16))
                        po.dma_start(O["p_rgh"][l].rearrange("b (k p) -> (b k) p", p=P), src[12:16])\
                            .then_inc(sem("states_stored"), up("states_stored", l, by=16))
                        po.dma_start(O["s_rgh"][l].rearrange("b (k p) -> (b k) p", p=P), src[16:48])\
                            .then_inc(sem("states_stored"), up("states_stored", l, by=16))
                    elif i == 1:
                        po.dma_start(O["s_rgc"][l].rearrange("b w (k p) -> (b w k) p", p=P), src)\
                            .then_inc(sem("states_stored"), up("states_stored", l, by=16))
                    elif i == 2:
                        po.dma_start(O["p_ffc"][l].rearrange("b w (k p) -> (b w k) p", p=P), src)\
                            .then_inc(sem("states_stored"), up("states_stored", l, by=16))
                    else:
                        dst = O["s_ffc"][l].rearrange("b w (k p) -> (b w k) p", p=P)
                        po.dma_start(dst[(i - 3) * P:(i - 2) * P], src)\
                            .then_inc(sem("states_stored"), up("states_stored", l, by=16))
            for k in (3, 7):
                po.wait_ge(sem("y_copied_v"), after("y_copied_v", k - 1))
                po.wait_ge(sem("y_copied_a"), after("y_copied_a", k))
                c = slice((k - 3) * P, (k + 1) * P)
                po.dma_start(O["y_p"][0].rearrange("(t p) d -> p t d", p=P)[:, :, c], yout[:, :, c])\
                    .then_inc(sem("y_stored"), up("y_stored", 0, by=16))
                po.dma_start(O["y_s"].rearrange("b t d -> (b t) d")[:, c], youts[:, c])\
                    .then_inc(sem("y_stored"), up("y_stored", 0, by=16))
            po.wait_ge(sem("y_stored"), after("y_stored", 0))
            po.wait_ge(sem("states_stored"), after("states_stored", DEPTH - 1))

        @block.scalar
        def _(ac):

            def a(ins):
                ins.then_inc(sem("scalar_step"), up("scalar_step"))
                ac.wait_ge(sem("scalar_step"), now("scalar_step"))

            act = nc.scalar.activation
            psk = lambda key: S.bank_of[key]
            tsa = [0]

            def squares(l, n, src, sq, ready):
                for k in range(KT):
                    ready(k)
                    act(sq[:, k, :], src[:, k, :], ACT.Square).then_inc(sem("squared"), up("squared", (l, n, k)))
                    ac.wait_ge(sem("squared"), now("squared"))

            def root(l, n):
                b = psk((l, n, "sum"))
                ac.wait_ge(sem("summed"), after("summed", (l, n)))
                a(act(sm[:, 0:4], pst[:, b, 0:4], ACT.Sqrt, scale=1.0 / D, bias=sm[:, 150:151]))
                act(sm[0:NS, 4:5], pst[0:NS, b, 4:5], ACT.Sqrt, scale=1.0 / D, bias=sm[0:NS, 150:151]).then_inc(sem("rms_ready"), up("rms_ready", (l, n), frees=[("psum", (l, n, "sum"))]))
                ac.wait_ge(sem("rms_ready"), now("rms_ready"))

            for k in range(KT):
                ac.wait_ge(sem("x_turned"), after("x_turned", k))
                b = psk(("x", k))
                act(xT[:, k, :], flat(b, T), ACT.Copy).then_inc(sem("x_copied"), up("x_copied", k, frees=[("psum", ("x", k))]))
                ac.wait_ge(sem("x_copied"), now("x_copied"))

            def compress(u, prev):
                nch = NCH if u[1] == "cmp" else NCP
                for v in range(2):
                    for s4 in (1, 3):
                        ac.wait_ge(sem("turned"), after("turned", (u, "xt", v, s4)))
                        sl = S.slot_of[u, "xt", v, s4]
                        for s, n_ in freed(("ts", sl - NTS)):
                            ac.wait_ge(s, n_)
                        b = psk((u, "xt", v, s4))
                        act(tv(sl)[:, 0:4 * nch], pst[:, b, 0:4 * nch], ACT.Copy).then_inc(sem("copied_a"), up("copied_a", (u, "xt", v, s4), frees=[("psum", (u, "xt", v, s4))]))
                        ac.wait_ge(sem("copied_a"), now("copied_a"))
                    ac.wait_ge(sem("compressed"), after("compressed", (u, v, 3)))
                    ac.wait_ge(sem("b1_ready"), after("b1_ready", u[0]))
                    b = psk((u, "hid", v))
                    if prev:
                        ac.wait_ge(sem("compressed2"), after("compressed2", (prev, v)))
                    if u[1] == "cmp":
                        act(hid_of(u, v), pst[:, b, 0:2 * (nch - 1)].rearrange("p (h c) -> p h c", h=2),
                              ACT.Gelu_apprx_tanh, bias=sm[:, 140 + v:141 + v]).then_inc(sem("hidden"), up("hidden", (u, v), frees=[("psum", (u, "hid", v))]))
                        ac.wait_ge(sem("hidden"), now("hidden"))
                    else:
                        hv = hid_of(u, v)
                        a(act(hv[:, :, 31:32], cst[:, K_ROT:K_ROT + 2].rearrange("p (h c) -> p h c", h=2), ACT.Copy, scale=0.0))
                        act(hv[:, :, 0:31], pst[:, b, 0:62].rearrange("p (h c) -> p h c", h=2),
                              ACT.Gelu_apprx_tanh, bias=sm[:, 140 + v:141 + v]).then_inc(sem("hidden"), up("hidden", (u, v), frees=[("psum", (u, "hid", v))]))
                        ac.wait_ge(sem("hidden"), now("hidden"))

            for l in range(DEPTH):
                if l == 0:
                    squares(l, 0, xT, actT, lambda k: None)
                else:
                    squares(l, 0, xT, actT, lambda k: ac.wait_ge(sem("x_added_p" if k % 2 else "x_added_v"), after("x_added_p" if k % 2 else "x_added_v", (l - 1, 3, k))))
                ac.wait_ge(sem("eps_set"), after("eps_set", 0))
                root(l, 0)
                ac.wait_ge(sem("lam_abs"), after("lam_abs", l))
                a(act(sm[:, 108:112], sm[:, 104:108], ACT.Exp))
                act(sm[:, 112:116], sm[:, 108:112], ACT.Ln, bias=1.0).then_inc(sem("lam_exp"), up("lam_exp", l))
                ac.wait_ge(sem("lam_exp"), now("lam_exp"))
                for j in range(RJ):
                    ac.wait_ge(sem("projected"), after("projected", (l, "xr", j)))
                    b = psk((l, "xr", j))
                    if j == 0:
                        ac.wait_ge(sem("h_ready"), after("h_ready", (l, 0, KT - 1)))
                    else:
                        ac.wait_ge(sem("y_ready"), after("y_ready", (l, j - 1)))
                    a(act(xrp[:, 3:3 + TH], pst[:, b, 0:TH], ACT.Copy))
                    a(act(xrp[:, 3 + TH:3 + SEQ], pst[:, b + 1, 0:SEQ - TH], ACT.Copy))
                    xs = xrp[:, 3 + SEQ:].rearrange("p (b c) -> p b c", b=DB)
                    act(xs[:, :, 3:7], pst[:, b + 1, SEQ - TH:TH].rearrange("p (b c) -> p b c", b=DB), ACT.Copy).then_inc(sem("xr_copied"), up("xr_copied", (l, j), frees=[("psum", (l, "xr", j))]))
                    ac.wait_ge(sem("xr_copied"), now("xr_copied"))
                    ac.wait_ge(sem("projected"), after("projected", (l, "gate", j)))
                    b = psk((l, "gate", j))
                    if l:
                        ac.wait_ge(sem("states_stored"), after("states_stored", l - 1))
                    act(halves(gR), pair(b), ACT.Gelu_apprx_tanh).then_inc(sem("gate_ready"), up("gate_ready", (l, j), frees=[("psum", (l, "gate", j))]))
                    ac.wait_ge(sem("gate_ready"), now("gate_ready"))
                    ac.wait_ge(sem("lambda_ready"), after("lambda_ready", l))
                    ac.wait_ge(sem("projected"), after("projected", (l, "rg", j, 0)))
                    b = psk((l, "rg", j, 0))
                    act(halves(rt), pair(b), ACT.Tanh, scale=0.5, bias=sm[:, 20 + j:21 + j]).then_inc(sem("scalar_step"), up("scalar_step", frees=[("psum", (l, "rg", j, 0))]))
                    ac.wait_ge(sem("scalar_step"), now("scalar_step"))
                    ac.wait_ge(sem("projected"), after("projected", (l, "rg", j, 1)))
                    b = psk((l, "rg", j, 1))
                    act(halves(iR), pair(b), ACT.Tanh, scale=0.5, bias=sm[:, 24 + j:25 + j]).then_inc(sem("i_ready"), up("i_ready", (l, j), frees=[("psum", (l, "rg", j, 1))]))
                    ac.wait_ge(sem("i_ready"), now("i_ready"))
                    act(tR, rt, ACT.Tanh, scale=sm[:, 28 + j:29 + j], bias=sm[:, 28 + j:29 + j]).then_inc(sem("t_ready"), up("t_ready", (l, j)))
                    ac.wait_ge(sem("t_ready"), now("t_ready"))
                    act(aR, rt, ACT.Exp, scale=sm[:, 28 + j:29 + j], bias=sm[:, 28 + j:29 + j]).then_inc(sem("a_ready"), up("a_ready", (l, j)))
                    ac.wait_ge(sem("a_ready"), now("a_ready"))
                    ac.wait_ge(sem("f_ready"), after("f_ready", (l, j)))
                    act(rt, tR, ACT.Sqrt, scale=-0.5).then_inc(sem("s_ready"), up("s_ready", (l, j)))
                    ac.wait_ge(sem("s_ready"), now("s_ready"))
                for g in range(GR):
                    ac.wait_ge(sem("projected"), after("projected", (l, "q", g)))
                    b = psk((l, "q", g))
                    act(halves(qcT[:, g, :]), pair(b), ACT.Copy, scale=HD ** -0.5).then_inc(sem("q_copied"), up("q_copied", (l, g), frees=[("psum", (l, "q", g))]))
                    ac.wait_ge(sem("q_copied"), now("q_copied"))
                for n in ("s1", "w1", "c0", "c1"):
                    ac.wait_ge(sem("projected"), after("projected", (l, "kv", n)))
                    b = psk((l, "kv", n))
                    ac.wait_ge(sem("y_ready"), after("y_ready", (l, RJ - 1)))
                    if n[0] == "c":
                        ac.wait_ge(sem("k_roped"), after("k_roped", (l, "w")))
                    v = int(n[1])
                    dst = kvt[n[0]][:, :, v * P:(v + 1) * P]
                    a(act(dst[:, 0:4, :], pst[:, b, :].rearrange("p (t c) -> p t c", t=4), ACT.Copy))
                    act(dst[0:NS, 4, :], pst[0:NS, b + 1, 0:P], ACT.Copy).then_inc(sem("kv_copied"), up("kv_copied", (l, n[0]) if v else None, frees=[("psum", (l, "kv", n))]))
                    ac.wait_ge(sem("kv_copied"), now("kv_copied"))
                ac.wait_ge(sem("projected"), after("projected", (l, "gl")))
                b = psk((l, "gl"))
                a(act(gates[:, 0:4, :], pst[:, b, 0:96].rearrange("p (t c) -> p t c", t=4), ACT.Tanh, scale=0.5))
                act(gates[0:NS, 4, :], pst[0:NS, b, 96:120], ACT.Tanh, scale=0.5).then_inc(sem("gates_tanh"), up("gates_tanh", l, frees=[("psum", (l, "gl"))]))
                ac.wait_ge(sem("gates_tanh"), now("gates_tanh"))
                for n in "sw":
                    ac.wait_ge(sem("k_turned"), after("k_turned", (l, n)))
                    b = psk((l, "kT", n))
                    act(kT[n], flat(b, T), ACT.Copy).then_inc(sem("kT_copied"), up("kT_copied", (l, n), frees=[("psum", (l, "kT", n))]))
                    ac.wait_ge(sem("kT_copied"), now("kT_copied"))
                us = [(l, "cmp", x) for x in range(DB)] + [(l, "cmpp", 0)]
                for i, u in enumerate(us):
                    compress(u, us[i - 1] if i else (l - 1, "cmpp", 0) if l else None)
                    if CMP_PARTS.get(i, ("", 0))[0] != "scores":
                        continue
                    G = CMP_PARTS[i][1]
                    ac.wait_ge(sem("neg_max"), after("neg_max", (l, G, "cs")))
                    if G:
                        ac.wait_ge(sem("turned"), after("turned", (l, 0, "cs")))
                    b = psk((l, G, "Scs"))
                    act(cmp_p, pst[:, b, 0:127], ACT.Exp, bias=sm[:, 40 + G:41 + G], accum_out=sm[:, 42 + G:43 + G]).then_inc(sem("p_exp"), up("p_exp", (l, G, "cs"), frees=[("psum", (l, G, "Scs"))]))
                    ac.wait_ge(sem("p_exp"), now("p_exp"))
                def p_exp(n):
                    u = todo[n]
                    i, br, g = u
                    for h in range(2):
                        m = 2 * n + h
                        if h == 0:
                            ac.wait_ge(sem("neg_max"), after("neg_max", (l, u)))
                        if m >= 4:
                            for s, n_ in freed(("p", l, m - 4)):
                                ac.wait_ge(s, n_)
                        b = psk((l, u, "S")) + h
                        L = (i + 1) * P
                        col = 176 + 16 * (i % 2) + (0 if br == "s" else 8) + g * 2 + h
                        act(p_slot(m)[:, 0:L], pst[:, b, 0:L], ACT.Exp, bias=sm[:, 48 + m % 8:49 + m % 8],
                              accum_out=sm[:, col:col + 1]).then_inc(sem("p_exp"), up("p_exp", (l, u, h), frees=[("psum", (l, u, "S")), ("nm", l, n)]))
                        ac.wait_ge(sem("p_exp"), now("p_exp"))

                def p_copy(n):
                    u = todo[n]
                    sl = S.slot_of[l, u, 1]
                    ac.wait_ge(sem("turned"), after("turned", (l, u, 1)))
                    for s, n_ in freed(("ts", sl - NTS)):
                        ac.wait_ge(s, n_)
                    L = (u[0] + 1) * P
                    b = psk((l, u, "T", 1))
                    act(tv(sl)[:, 0:L], pst[:, b, 0:L], ACT.Copy).then_inc(sem("copied_a"), up("copied_a", (l, u, 1), frees=[("psum", (l, u, "T", 1))]))
                    ac.wait_ge(sem("copied_a"), now("copied_a"))

                def sample_part(part, k, G, e):
                    u = (l, "win", G) if e is None else (l, "slc", 4 * G + e)
                    if part in ("keys0", "keys2"):
                        x = 1 if part == "keys0" else 3
                        n = 4 * (10 * l + k) + x
                        ac.wait_ge(sem("turned"), after("turned", (u, "kt", x)))
                        if n >= NKS:
                            for s, n_ in freed(("ks", n - NKS)):
                                ac.wait_ge(s, n_)
                        act(key_slot(n), bank(psk((u, "kt", x))), ACT.Copy).then_inc(sem("copied_a"), up("copied_a", (u, "kt", x), frees=[("psum", (u, "kt", x))]))
                        ac.wait_ge(sem("copied_a"), now("copied_a"))
                    elif part == "exp":
                        ac.wait_ge(sem("neg_max"), after("neg_max", u))
                        if e is None:
                            a(act(sW[:, 0:512], sW[:, 0:512], ACT.Exp, bias=sm[:, 88:89], accum_out=sm[:, 90:91]))
                            act(sW[:, 512:544], sW[:, 512:544], ACT.Exp, bias=sm[:, 88:89], accum_out=sm[:, 91:92]).then_inc(sem("p_exp"), up("p_exp", u))
                            ac.wait_ge(sem("p_exp"), now("p_exp"))
                        else:
                            r = slice(32 * e, 32 * e + 32)
                            act(sQ[r, :], sQ[r, :], ACT.Exp, bias=sm[r, 89:90], accum_out=sm[r, 92:93]).then_inc(sem("p_exp"), up("p_exp", u))
                            ac.wait_ge(sem("p_exp"), now("p_exp"))

                ac.wait_ge(sem("kv_stored_c"), after("kv_stored_c", l))
                for who_, what, n in plan:
                    if who_ == "sample":
                        if what == "keys0":
                            ac.wait_ge(sem("summed_values"), after("summed_values", (l, 1, "cs")))
                        sample_part(what, *n)
                    elif (who_, what) == ("tile", "exp"):
                        ac.wait_ge(sem("cmp_shifted"), after("cmp_shifted", (l, n)))
                        act(pc_p, pc_s, ACT.Exp).then_inc(sem("cmp_exp"), up("cmp_exp", (l, n)))
                        ac.wait_ge(sem("cmp_exp"), now("cmp_exp"))
                    elif who_ != "prompt":
                        continue
                    elif what == "scores":
                        if n % 8 == 0 and n >= 16:
                            ac.wait_ge(sem("l_read"), after("l_read", (l, todo[n][0] - 2)))
                        p_exp(n)
                    elif what == "turn":
                        p_copy(n)
                ac.wait_ge(sem("kv_stored_s"), after("kv_stored_s", l))
                ac.wait_ge(sem("kv_stored_w"), after("kv_stored_w", l))
                for j in range(KT):
                    ac.wait_ge(sem("projected"), after("projected", (l, "out", j)))
                    b = psk((l, "out", j))
                    ac.wait_ge(sem("summed_values"), after("summed_values", ((l, "slc", 7), 0)))
                    a(act(halves(mT[:, j, :]), pair(b), ACT.Copy))
                    act(halves(actT[:, j, :]), pair(b), ACT.Square).then_inc(sem("squared"), up("squared", (l, 1, j), frees=[("psum", (l, "out", j))]))
                    ac.wait_ge(sem("squared"), now("squared"))
                root(l, 1)
                squares(l, 2, xT, actT, lambda k: ac.wait_ge(sem("x_added_p" if k % 2 else "x_added_v"), after("x_added_p" if k % 2 else "x_added_v", (l, 1, k))))
                root(l, 2)
                for r in range(RND):
                    for f in range(r * FR, (r + 1) * FR):
                        ac.wait_ge(sem("projected"), after("projected", (l, "g", f)))
                        b = psk((l, "g", f))
                        gp = gpad[f % 2]
                        if f == 0:
                            ac.wait_ge(sem("rstd_spread"), after("rstd_spread", (l, 2)))
                        if f >= 2:
                            ac.wait_ge(sem("conv_done"), after("conv_done", (l, "f", f - 2)))
                            for s, n_ in freed(("gpad", l, f - 2)):
                                ac.wait_ge(s, n_)
                        a(act(gp[:, 2:2 + TH], pst[:, b, 0:TH], ACT.Copy))
                        a(act(gp[:, 2 + TH:2 + SEQ], pst[:, b + 1, 0:SEQ - TH], ACT.Copy))
                        gps = gp[:, 2 + SEQ:].rearrange("p (b c) -> p b c", b=DB)
                        act(gps[:, :, 2:6], pst[:, b + 1, SEQ - TH:TH].rearrange("p (b c) -> p b c", b=DB), ACT.Copy).then_inc(sem("g_copied"), up("g_copied", (l, f), frees=[("psum", (l, "g", f))]))
                        ac.wait_ge(sem("g_copied"), now("g_copied"))
                        ac.wait_ge(sem("conv_done"), after("conv_done", (l, "f", f)))
                        if f:
                            ac.wait_ge(sem("act_ready"), after("act_ready", (l, f - 1)))
                        a(act(gF[:, 0:SEQ], cF[:, 0:SEQ], ACT.Gelu_apprx_tanh))
                        act(gF[:, SEQ:T].rearrange("p (b c) -> p b c", b=DB), per6, ACT.Gelu_apprx_tanh).then_inc(sem("gelu_done"), up("gelu_done", (l, f)))
                        ac.wait_ge(sem("gelu_done"), now("gelu_done"))
                    for j in range(KT):
                        ac.wait_ge(sem("projected"), after("projected", (l, "down", r, j)))
                        b = psk((l, "down", r, j))
                        if r == 0:
                            act(halves(mT[:, j, :]), pair(b), ACT.Copy).then_inc(sem("m_copied"), up("m_copied", (l, j), frees=[("psum", (l, "down", r, j))]))
                            ac.wait_ge(sem("m_copied"), now("m_copied"))
                        if r == RND - 1:
                            ac.wait_ge(sem("m_summed"), after("m_summed", (l, r, j)))
                            act(hT[:, j, :], mT[:, j, :], ACT.Square).then_inc(sem("squared"), up("squared", (l, 3, j)))
                            ac.wait_ge(sem("squared"), now("squared"))
                root(l, 3)
                for i, (name, r0, r1) in enumerate(OUTT):
                    ac.wait_ge(sem("states_turned"), after("states_turned", (l, i)))
                    b = psk((l, "st", i))
                    act(st_out[0:r1 - r0, i * P:(i + 1) * P], pst[0:r1 - r0, b, 0:P], ACT.Copy).then_inc(sem("states_copied"), up("states_copied", (l, i), frees=[("psum", (l, "st", i))]))
                    ac.wait_ge(sem("states_copied"), now("states_copied"))
            ac.wait_ge(sem("x_added_v"), after("x_added_v", (DEPTH - 1, 3, KT - 2)))
            for k in range(1, KT, 2):
                ac.wait_ge(sem("y_turned"), after("y_turned", k))
                b = psk(("y", k))
                a(act(yout[:, :, k * P:(k + 1) * P], bank(b).rearrange("p (t c) -> p t c", t=4), ACT.Copy))
                act(youts[:, k * P:(k + 1) * P], pst[0:NS, b + 1, 0:P], ACT.Copy).then_inc(sem("y_copied_a"), up("y_copied_a", k, frees=[("psum", ("y", k))]))
                ac.wait_ge(sem("y_copied_a"), now("y_copied_a"))

        @block.vector
        def _(ve):

            def v(ins):
                ins.then_inc(sem("vector_step"), up("vector_step"))
                ve.wait_ge(sem("vector_step"), now("vector_step"))

            V = nc.vector
            tt, tsc, stt, cp = V.tensor_tensor, V.tensor_scalar, V.scalar_tensor_tensor, V.tensor_copy
            psk = lambda key: S.bank_of[key]

            def copy_ts(key, cols, rows=P):
                ve.wait_ge(sem("turned"), after("turned", key))
                sl = S.slot_of[key]
                for s, n_ in freed(("ts", sl - NTS)):
                    ve.wait_ge(s, n_)
                b = S.bank_of[S.bank_key[key]]
                cp(tv(sl)[0:rows, 0:cols], pst[0:rows, b, 0:cols]).then_inc(sem("copied_v"), up("copied_v", key, frees=[("psum", S.bank_key[key])]))
                ve.wait_ge(sem("copied_v"), now("copied_v"))

            def masked(u, x, r, G):
                ve.wait_ge(sem("scored"), after("scored", (u, x + 1)))
                b = S.bank_of[u, "S", x]
                y = lambda ap: ap.rearrange("p (s n c) -> p s n c", n=32, c=4)
                m = mb(G)[r, 0:32].unsqueeze(1).unsqueeze(3).broadcast_to([32, 8, 32, 4])
                tt(y(sQ[r, x * 512:(x + 2) * 512]), y(pst[r, b:b + 2, :].rearrange("p b c -> p (b c)")), m, ALU.add).then_inc(sem("vector_step"), up("vector_step", frees=[("psum", (u, "S", x))]))
                ve.wait_ge(sem("vector_step"), now("vector_step"))

            def norm(l, n):
                ve.wait_ge(sem("rms_ready"), after("rms_ready", (l, n)))
                v(V.reciprocal(sm[:, 8:12], sm[:, 0:4]))
                v(V.reciprocal(sm[0:NS, 12:13], sm[0:NS, 4:5]))
                for t, (t0, m) in enumerate(TT):
                    x = tsc(diag[0:m, t0:t0 + m], ident[0:m, 0:m], sm[0:m, 8 + t:9 + t], None, ALU.mult)
                    x.then_inc(sem("diag_built" if t == 4 else "vector_step"), up("diag_built" if t == 4 else "vector_step", (l, n) if t == 4 else None))
                    ve.wait_ge(sem("diag_built" if t == 4 else "vector_step"), now("diag_built" if t == 4 else "vector_step"))
                ve.wait_ge(sem("rstd_spread"), after("rstd_spread", (l, n)))

            def pre(l, n, gain):
                norm(l, n)
                b = psk((l, n, "rstd"))
                for k in range(KT):
                    stt(hT[:, k, :], xT[:, k, :], par[:, gain + k:gain + k + 1], flat(b, T), ALU.mult, ALU.mult).then_inc(sem("h_ready"), up("h_ready", (l, n, k), frees=[("psum", (l, n, "rstd"))]))
                    ve.wait_ge(sem("h_ready"), now("h_ready"))

            def post(l, n, gain):
                norm(l, n)
                b = psk((l, n, "rstd"))
                for k in range(KT):
                    stt(mT[:, k, :], mT[:, k, :], par[:, gain + k:gain + k + 1], flat(b, T), ALU.mult, ALU.mult).then_inc(sem("m_scaled"), up("m_scaled", (l, n, k), frees=[("psum", (l, n, "rstd"))]))
                    ve.wait_ge(sem("m_scaled"), now("m_scaled"))
                    if k % 2 == 0:
                        tt(xT[:, k, :], xT[:, k, :], mT[:, k, :], ALU.add).then_inc(sem("x_added_v"), up("x_added_v", (l, n, k)))
                        ve.wait_ge(sem("x_added_v"), now("x_added_v"))

            v(V.memset(sm[:, :], 0.0))
            V.memset(sm[:, 150:151], EPS).then_inc(sem("eps_set"), up("eps_set", 0))
            ve.wait_ge(sem("eps_set"), now("eps_set"))
            ve.wait_ge(sem("pages_loaded"), after("pages_loaded", 0))
            ve.wait_ge(sem("const_loaded"), after("const_loaded", 0))
            v(cp(idx[:, 0:DB], idi[:, 0:DB]))
            v(tsc(idx[:, DB:2 * DB], idx[:, 0:DB], float(CPP), cst[:, K_CH:K_CH + 1], ALU.mult, ALU.add))

            for l in range(DEPTH):
                v(tsc(idx[:, 2 * DB:3 * DB], idx[:, DB:2 * DB], float(l * NPOOL * CPP), None, ALU.add))
                cp(idi[:, (1 + l) * DB:(2 + l) * DB], idx[:, 2 * DB:3 * DB]).then_inc(sem("index_ready"), up("index_ready", 0))
                ve.wait_ge(sem("index_ready"), now("index_ready"))
            for l in range(DEPTH):
                offs = [0, 98, 194, 322, 450, 578, 706]
                for i in range(6):
                    ve.wait_ge(sem("params_turned"), after("params_turned", (l, i)))
                    b = psk((l, "par", i))
                    cp(par[:, offs[i]:offs[i + 1]], pst[:, b, 0:offs[i + 1] - offs[i]]).then_inc(sem("params_ready"), up("params_ready", (l, i), frees=[("psum", (l, "par", i))]))
                    ve.wait_ge(sem("params_ready"), now("params_ready"))
                pre(l, 0, P_NORM)
                v(tsc(sm[:, 20:28], par[:, P_BA:P_BA + 8], 0.5, None, ALU.mult))
                lam = par[:, P_LAM:P_LAM + 4]
                v(tsc(sm[:, 100:104], lam, -1.0, None, ALU.mult))
                tt(sm[:, 104:108], lam, sm[:, 100:104], ALU.min).then_inc(sem("lam_abs"), up("lam_abs", l))
                ve.wait_ge(sem("lam_abs"), now("lam_abs"))
                ve.wait_ge(sem("lam_exp"), after("lam_exp", l))
                y, w = sm[:, 108:112], sm[:, 112:116]
                v(tsc(sm[:, 116:120], y, 1.0, None, ALU.add))
                v(tsc(sm[:, 120:124], sm[:, 116:120], -1.0, None, ALU.add))
                v(tsc(sm[:, 124:128], sm[:, 120:124], 1e-30, None, ALU.max))
                v(V.reciprocal(sm[:, 128:132], sm[:, 124:128]))
                v(tt(sm[:, 132:136], w, y, ALU.mult))
                v(tt(sm[:, 132:136], sm[:, 132:136], sm[:, 128:132], ALU.mult))
                v(stt(sm[:, 120:124], sm[:, 120:124], 0.0, y, ALU.is_equal, ALU.mult))
                v(tt(sm[:, 132:136], sm[:, 132:136], sm[:, 120:124], ALU.add))
                v(tsc(sm[:, 116:120], lam, 0.0, None, ALU.min))
                v(tt(sm[:, 116:120], sm[:, 116:120], sm[:, 132:136], ALU.subtract))
                tsc(sm[:, 28:32], sm[:, 116:120], 4.0, None, ALU.mult).then_inc(sem("lambda_ready"), up("lambda_ready", l))
                ve.wait_ge(sem("lambda_ready"), now("lambda_ready"))
                rc = par[:, P_RC:P_RC + 96].rearrange("p (b w j) -> p b w j", b=DB, w=3)
                h0 = par[:, P_H0:P_H0 + 32].rearrange("p (b j) -> p b j", b=DB)
                for j in range(RJ):
                    xs = xrp[:, 3 + SEQ:].rearrange("p (b c) -> p b c", b=DB)
                    v(V.memset(xrp[:, 0:3], 0.0))
                    v(cp(xs[:, :, 0:3], rc[:, :, :, j]))
                    ve.wait_ge(sem("xr_copied"), after("xr_copied", (l, j)))
                    cw = lambda k: par[:, P_RCW + 4 * k + j:P_RCW + 4 * k + j + 1]
                    v(tsc(cR, xrp[:, 0:568], cw(0), par[:, P_RCB + j:P_RCB + j + 1], ALU.mult, ALU.add))
                    v(stt(cR, xrp[:, 1:569], cw(1), cR, ALU.mult, ALU.add))
                    v(stt(cR, xrp[:, 2:570], cw(2), cR, ALU.mult, ALU.add))
                    v(stt(xc[:, 0:SEQ], xrp[:, 3:3 + SEQ], cw(3), cR[:, 0:SEQ], ALU.mult, ALU.add))
                    stt(xc[:, SEQ:T].rearrange("p (b c) -> p b c", b=DB), xs[:, :, 3:7], cw(3), per7,
                          ALU.mult, ALU.add).then_inc(sem("conv_done"), up("conv_done", (l, j)))
                    ve.wait_ge(sem("conv_done"), now("conv_done"))
                    oc = outr[:, 0:12].rearrange("p (w j) -> p w j", w=3)
                    if j == 0 and l:
                        ve.wait_ge(sem("states_turned"), after("states_turned", (l - 1, 5)))
                    v(cp(oc[:, :, j], xrp[:, SEQ:SEQ + 3]))
                    oc = outr[:, 48:144].rearrange("p (b w j) -> p b w j", b=DB, w=3)
                    v(cp(oc[:, :, :, j], xs[:, :, 4:7]))
                    ve.wait_ge(sem("t_ready"), after("t_ready", (l, j)))
                    v(tsc(recR, tR, -1.0, 1.0, ALU.mult, ALU.add))
                    v(V.reciprocal(recR, recR))
                    tt(tR, tR, recR, ALU.mult).then_inc(sem("f_ready"), up("f_ready", (l, j)))
                    ve.wait_ge(sem("f_ready"), now("f_ready"))
                    v(stt(iR, iR, 1.0, xc, ALU.add, ALU.mult))
                    ve.wait_ge(sem("s_ready"), after("s_ready", (l, j)))
                    v(tt(iR, iR, rt, ALU.mult))
                    a0 = aR[:, SEQ:T].rearrange("p (b c) -> p b c", b=DB)[:, :, 0]
                    b0 = iR[:, SEQ:T].rearrange("p (b c) -> p b c", b=DB)[:, :, 0]
                    v(tt(sm[:, 100:108], a0, h0[:, :, j], ALU.mult))
                    v(tt(b0, b0, sm[:, 100:108], ALU.add))
                    v(V.memset(a0, 0.0))
                    v(V.tensor_tensor_scan(hR, aR, iR, 0.0, ALU.mult, ALU.add))
                    v(cp(outr[:, 12 + j:13 + j], hR[:, SEQ - 1:SEQ]))
                    oh = outr[:, 16:48].rearrange("p (b j) -> p b j", b=DB)
                    v(cp(oh[:, :, j], hR[:, SEQ:T].rearrange("p (b c) -> p b c", b=DB)[:, :, 3]))
                    ve.wait_ge(sem("gate_ready"), after("gate_ready", (l, j)))
                    tt(yT[:, j, :], hR, gR, ALU.mult).then_inc(sem("y_ready"), up("y_ready", (l, j)))
                    ve.wait_ge(sem("y_ready"), now("y_ready"))
                ve.wait_ge(sem("tables_loaded"), after("tables_loaded", 0))
                t1, t2 = sS[:, 0:T], sS[:, T:2 * T]
                for g in range(GR):
                    ve.wait_ge(sem("projected"), after("projected", (l, "rot", g)))
                    b = psk((l, "rot", g))
                    v(tt(t1, qcT[:, g, :], cosT, ALU.mult))
                    tt(halves(t2), pair(b), halves(sinT), ALU.mult).then_inc(sem("vector_step"), up("vector_step", frees=[("psum", (l, "rot", g))]))
                    ve.wait_ge(sem("vector_step"), now("vector_step"))
                    tt(qrT[:, g, :], t1, t2, ALU.add).then_inc(sem("q_roped"), up("q_roped", (l, g)))
                    ve.wait_ge(sem("q_roped"), now("q_roped"))
                ve.wait_ge(sem("ov2_zeroed"), after("ov2_zeroed", l))
                for h in range(2):
                    for c, q in ((0, qcT), (1, qrT)):
                        hr = slice(h * HD, (h + 1) * HD)
                        for g in range(GR):
                            dst = qbd[hr, c, :, h * 16 + 4 * g:h * 16 + 4 * g + 4]
                            cp(dst, q[hr, g, SEQ:T].rearrange("p (b t) -> p b t", b=DB)).then_inc(sem("qbd_built" if (h, c, g) == (1, 1, 3) else "vector_step"), up("qbd_built" if (h, c, g) == (1, 1, 3) else "vector_step", l if (h, c, g) == (1, 1, 3) else None))
                            ve.wait_ge(sem("qbd_built" if (h, c, g) == (1, 1, 3) else "vector_step"), now("qbd_built" if (h, c, g) == (1, 1, 3) else "vector_step"))
                for n in "sw":
                    ve.wait_ge(sem("projected"), after("projected", (l, "kv", n + "0")))
                    b = psk((l, "kv", n + "0"))
                    for m, t0, t1_ in ((P, 0, 4), (NS, 4, 5)):
                        nt = t1_ - t0
                        x = flat(b, 640)[0:m, t0 * P:t1_ * P].rearrange("p (t h d) -> p t h d", t=nt, h=2)
                        A = sS[0:m, 0:nt * P].rearrange("p (t h d) -> p t h d", t=nt, h=2)
                        Bb = sS[0:m, 512:512 + nt * P].rearrange("p (t h d) -> p t h d", t=nt, h=2)
                        for h in range(2):
                            v(tt(A[:, :, h], x[:, :, h], cosk[0:m, t0:t1_, :], ALU.mult))
                            v(tt(Bb[:, :, h, 0:32], x[:, :, h, 32:64], sink[0:m, t0:t1_, 0:32], ALU.mult))
                            v(tt(Bb[:, :, h, 32:64], x[:, :, h, 0:32], sink[0:m, t0:t1_, 32:64], ALU.mult))
                        dst = kvt[n][0:m, t0:t1_, 0:P].rearrange("p t (h d) -> p t h d", h=2)
                        dst = kvt[n][0:m, t0:t1_, 0:P]
                        A2 = sS[0:m, 0:nt * P].rearrange("p (t c) -> p t c", t=nt)
                        B2 = sS[0:m, 512:512 + nt * P].rearrange("p (t c) -> p t c", t=nt)
                        tt(dst, A2, B2, ALU.add).then_inc(sem("k_roped" if nt == 1 else "vector_step"), up("k_roped" if nt == 1 else "vector_step", (l, n) if nt == 1 else None, frees=[("psum", (l, "kv", n + "0"))] if nt == 1 else []))
                        ve.wait_ge(sem("k_roped" if nt == 1 else "vector_step"), now("k_roped" if nt == 1 else "vector_step"))
                ve.wait_ge(sem("gates_tanh"), after("gates_tanh", l))
                v(tsc(gates[:, 0:4, :], gates[:, 0:4, :], 0.5, 0.5, ALU.mult, ALU.add))
                tsc(gates[0:NS, 4, :], gates[0:NS, 4, :], 0.5, 0.5, ALU.mult, ALU.add).then_inc(sem("gates_ready"), up("gates_ready", l))
                ve.wait_ge(sem("gates_ready"), now("gates_ready"))
                ve.wait_ge(sem("gates_spread"), after("gates_spread", l))
                b = psk((l, "gsel"))
                for G in range(2):
                    x = pst[:, b, 24 * G:24 * G + 24].rearrange("p (n c) -> p c n", c=3)
                    tmp = sm[:, 100:124].rearrange("p (c n) -> p c n", c=3)
                    tt(tmp, x, cst[:, K_PICK:K_PICK + 24].rearrange("p (c n) -> p c n", c=3), ALU.mult).then_inc(sem("vector_step"), up("vector_step", frees=[("psum", (l, "gsel"))]))
                    ve.wait_ge(sem("vector_step"), now("vector_step"))
                    v(V.tensor_reduce(gs[:, G, :], tmp, AX.X, ALU.add))
                ve.wait_ge(sem("pe_summed"), after("pe_summed", l))
                b = psk((l, "pe"))
                tt(sm[:, 140:142], pst[:, b, 0:2], par[:, P_B1:P_B1 + 2], ALU.add).then_inc(sem("b1_ready"), up("b1_ready", l, frees=[("psum", (l, "pe"))]))
                ve.wait_ge(sem("b1_ready"), now("b1_ready"))

                def sample_cmp(part, G):
                    if part == "scores":
                        ve.wait_ge(sem("scored"), after("scored", (l, G, "cs")))
                        b = psk((l, G, "Scs"))
                        V.tensor_reduce(sm[:, 40 + G:41 + G], pst[:, b, 0:127], AX.X, ALU.max, negate=True).then_inc(sem("neg_max"), up("neg_max", (l, G, "cs")))
                        ve.wait_ge(sem("neg_max"), now("neg_max"))
                    elif part == "group":
                        ve.wait_ge(sem("p_exp"), after("p_exp", (l, G, "cs")))
                        v(tsc(sm[:, 44:45], sm[:, 42 + G:43 + G], 1e-30, None, ALU.max))
                        v(V.reciprocal(sm[:, 45:46], sm[:, 44:45]))
                        tsc(cmp_p, cmp_p, sm[:, 45:46], None, ALU.mult).then_inc(sem("pn_ready"), up("pn_ready", (l, G)))
                        ve.wait_ge(sem("pn_ready"), now("pn_ready"))
                        ve.wait_ge(sem("group_summed"), after("group_summed", (l, G)))
                        b = psk((l, G, "gsum"))
                        cp(pp[:, 1:128], pst[:, b, 0:127]).then_inc(sem("vector_step"), up("vector_step", frees=[("psum", (l, G, "gsum"))]))
                        ve.wait_ge(sem("vector_step"), now("vector_step"))
                        sc = sm[:, 100:133]
                        v(V.tensor_reduce(sc, pp[:, 0:132].rearrange("p (n r) -> p n r", r=4), AX.X, ALU.add))
                        v(tt(sc, sc, pp[:, 4:136].rearrange("p (n r) -> p n r", r=4)[:, :, 0], ALU.add))
                        v(V.memset(sm[:, 100:101], BIG))
                        v(V.memset(sm[:, 131:133], BIG))
                        for r in range(2):
                            v(V.max(sm[:, 80:88], sc))
                            v(V.match_replace(sc, sm[:, 80:88], sc, -1.0))
                        tsc(mb(G), sc, 0.0, -BIG, ALU.is_ge, ALU.mult).then_inc(sem("selected"), up("selected", (l, G)))
                        ve.wait_ge(sem("selected"), now("selected"))
                    else:
                        copy_ts((l, G, "cs"), P, 127)
                        ve.wait_ge(sem("summed_values"), after("summed_values", (l, G, "cs")))
                        b = psk((l, G, "Ocs"))
                        tsc(comb[:, G, :], pst[:, b, 0:P], gs[:, G, 0:1], None, ALU.mult).then_inc(sem("vector_step"), up("vector_step", frees=[("psum", (l, G, "Ocs"))]))
                        ve.wait_ge(sem("vector_step"), now("vector_step"))

                v(V.memset(pp[:, :], 0.0))
                for x, u in enumerate([(l, "cmp", x) for x in range(DB)] + [(l, "cmpp", 0)]):
                    nch = NCH if u[1] == "cmp" else NCP
                    for vv in range(2):
                        for s4 in (0, 2):
                            copy_ts((u, "xt", vv, s4), 4 * nch)
                    if u[1] == "cmpp":
                        ve.wait_ge(sem("hidden"), after("hidden", (u, 1)))
                        hv = hid_of(u, 1)
                        for h in range(2):
                            for r in range(4):
                                last = (h, r) == (1, 3)
                                cp(hidrep[:, h, 32 * r:32 * r + 32], hv[:, h, :]).then_inc(sem("hidden_rep" if last else "vector_step"), up("hidden_rep" if last else "vector_step", (u, 1) if last else None))
                                ve.wait_ge(sem("hidden_rep" if last else "vector_step"), now("hidden_rep" if last else "vector_step"))
                    for vv in range(2):
                        ve.wait_ge(sem("compressed2"), after("compressed2", (u, vv)))
                        b = psk((u, "c2", vv))
                        fr = [("psum", (u, "c2", vv))]
                        if u[1] == "cmp":
                            if vv == 0:
                                cp(kcT[:, u[2], :], pst[:, b, 0:127]).then_inc(sem("copied_v"), up("copied_v", (u, "kc"), frees=fr))
                                ve.wait_ge(sem("copied_v"), now("copied_v"))
                            else:
                                cp(vc[0:127, u[2], :], pst[0:127, b, 0:P]).then_inc(sem("copied_v"), up("copied_v", (u, "vc"), frees=fr))
                                ve.wait_ge(sem("copied_v"), now("copied_v"))
                        elif vv == 0:
                            cp(kcTp[:, :], pst[:, b, 0:32]).then_inc(sem("vector_step"), up("vector_step", frees=fr))
                            ve.wait_ge(sem("vector_step"), now("vector_step"))
                        else:
                            for g in range(4):
                                cp(vbd[32 * g:32 * g + 32, :, g, :], pst[32 * g:32 * g + 32, b, 0:P].rearrange("p (h d) -> p h d", h=2)).then_inc(sem("vbd_built" if g == 3 else "vector_step"), up("vbd_built" if g == 3 else "vector_step", l if g == 3 else None, frees=fr if g == 3 else []))
                                ve.wait_ge(sem("vbd_built" if g == 3 else "vector_step"), now("vbd_built" if g == 3 else "vector_step"))
                    if x in CMP_PARTS:
                        sample_cmp(*CMP_PARTS[x])
                def p_max(n):
                    u = todo[n]
                    i = u[0]
                    L = (i + 1) * P
                    ve.wait_ge(sem("scored"), after("scored", (l, u)))
                    b = psk((l, u, "S"))
                    dg = pst[:, b:b + 2, L - P:L]
                    v(tt(dg, dg, cst[:, K_CAUS:K_CAUS + P].unsqueeze(1).broadcast_to([P, 2, P]), ALU.add))
                    if n >= 4:
                        for s, n_ in freed(("nm", l, n - 4)):
                            ve.wait_ge(s, n_)
                    m = 48 + 2 * (n % 4)
                    V.tensor_reduce(sm[:, m:m + 2], pst[:, b:b + 2, 0:L], AX.X, ALU.max, negate=True).then_inc(sem("neg_max"), up("neg_max", (l, u)))
                    ve.wait_ge(sem("neg_max"), now("neg_max"))

                sc3 = pc_s.rearrange("p (n c) -> p n c", n=8)
                pc3 = pc_p.rearrange("p (n c) -> p n c", n=8)

                def cmp_shift(i):
                    cm = cst[:, K_CMPM + i * NCP:K_CMPM + (i + 1) * NCP]
                    ve.wait_ge(sem("scored"), after("scored", (l, i, "c")))
                    b = psk((l, i, "Sc"))
                    x = pst[:, b:b + 2, 0:P].rearrange("p h (n c) -> p h n c", n=4)
                    tt(pc_s.rearrange("p (h n c) -> p h n c", h=2, n=4), x,
                         cm.unsqueeze(1).unsqueeze(1).broadcast_to([P, 2, 4, NCP]), ALU.add).then_inc(sem("vector_step"), up("vector_step", frees=[("psum", (l, i, "Sc"))]))
                    ve.wait_ge(sem("vector_step"), now("vector_step"))
                    v(V.tensor_reduce(sm[:, 100:108], sc3, AX.X, ALU.max))
                    v(tsc(sm[:, 100:108], sm[:, 100:108], -0.1 * BIG, None, ALU.max))
                    tt(sc3, sc3, sm[:, 100:108].unsqueeze(2).broadcast_to([P, 8, NCP]), ALU.subtract).then_inc(sem("cmp_shifted"), up("cmp_shifted", (l, i)))
                    ve.wait_ge(sem("cmp_shifted"), now("cmp_shifted"))

                def gated(i, br):
                    gt = gates[:, i, :].rearrange("p (h g c) -> p g h c", h=2, g=GR)
                    gh = lambda ap: ap.rearrange("p (g h) -> p g h", g=GR)
                    heads = lambda ap: ap.rearrange("p (n d) -> p n d", n=8)
                    if br == "c":
                        v(V.tensor_reduce(sm[:, 108:116], pc3, AX.X, ALU.add))
                        v(tsc(gh(sm[:, 124:132]), sm[:, 108:116].rearrange("p (h g) -> p g h", h=2), 1e-30, None, ALU.max))
                        lcol = sm[:, 124:132]
                        ve.wait_ge(sem("summed_values"), after("summed_values", (l, i, "c")))
                    else:
                        lc = 176 + 16 * (i % 2) + (0 if br == "s" else 8)
                        lcol = sm[:, lc:lc + 8]
                        ve.wait_ge(sem("summed_values"), after("summed_values", (l, (i, br, 3), 1)))
                    V.reciprocal(sm[:, 116:124], lcol).then_inc(sem("l_read" if br == "w" else "vector_step"), up("l_read" if br == "w" else "vector_step", (l, i) if br == "w" else None))
                    ve.wait_ge(sem("l_read" if br == "w" else "vector_step"), now("l_read" if br == "w" else "vector_step"))
                    v(tt(gh(sm[:, 116:124]), gh(sm[:, 116:124]), gt[:, :, :, "csw".index(br)], ALU.mult))
                    cf = sm[:, 116:124].unsqueeze(2).broadcast_to([P, 8, HD])
                    if br == "c" and i:
                        ve.wait_ge(sem("o_turned"), after("o_turned", (l, i - 1)))
                    tt(heads(o_sb if br == "c" else o_tmp), heads(pst[:, psk((l, i, br, "O")), :]), cf, ALU.mult).then_inc(sem("vector_step"), up("vector_step", frees=[("psum", (l, i, br, "O"))]))
                    ve.wait_ge(sem("vector_step"), now("vector_step"))
                    if br != "c":
                        tt(o_sb, o_sb, o_tmp, ALU.add).then_inc(sem("o_gated" if br == "w" else "vector_step"), up("o_gated" if br == "w" else "vector_step", (l, i) if br == "w" else None))
                        ve.wait_ge(sem("o_gated" if br == "w" else "vector_step"), now("o_gated" if br == "w" else "vector_step"))

                def copy_o(i):
                    ve.wait_ge(sem("o_turned"), after("o_turned", (l, i)))
                    b = psk((l, i, "oT"))
                    cp(hT[:, 0:4, i * P:(i + 1) * P], pst[:, b, :].rearrange("p (g q) -> p g q", g=4)).then_inc(sem("oT_copied"), up("oT_copied", (l, i), frees=[("psum", (l, i, "oT"))]))
                    ve.wait_ge(sem("oT_copied"), now("oT_copied"))

                def sample_part(part, k, G, e):
                    u = (l, "win", G) if e is None else (l, "slc", 4 * G + e)
                    nm = cst[:, K_NEWM + G * NS:K_NEWM + (G + 1) * NS]
                    pn = 10 * l + k

                    def copy_keys(x):
                        n = 4 * pn + x
                        ve.wait_ge(sem("turned"), after("turned", (u, "kt", x)))
                        if n >= NKS:
                            for s, n_ in freed(("ks", n - NKS)):
                                ve.wait_ge(s, n_)
                        cp(key_slot(n), bank(psk((u, "kt", x)))).then_inc(sem("copied_v"), up("copied_v", (u, "kt", x), frees=[("psum", (u, "kt", x))]))
                        ve.wait_ge(sem("copied_v"), now("copied_v"))

                    r = slice(0, P) if e is None else slice(32 * e, 32 * e + 32)
                    if part == "keys0":
                        copy_keys(0)
                    elif part == "keys1":
                        copy_keys(2)
                    elif part == "keys2" and e is not None:
                        if G:
                            ve.wait_ge(sem("turned"), after("turned", ((l, "slc", e), "ptn")))
                        masked(u, 0, r, G)
                    elif part == "keys3" and e is not None:
                        masked(u, 2, r, G)
                        ve.wait_ge(sem("scored"), after("scored", (u, "n")))
                        tt(sQ[r, 2048:2080], pst[r, psk((u, "Sn")), 0:NS], nm[r, :], ALU.add).then_inc(sem("vector_step"), up("vector_step", frees=[("psum", (u, "Sn"))]))
                        ve.wait_ge(sem("vector_step"), now("vector_step"))
                        V.tensor_reduce(sm[r, 89:90], sQ[r, :], AX.X, ALU.max, negate=True).then_inc(sem("neg_max"), up("neg_max", u))
                        ve.wait_ge(sem("neg_max"), now("neg_max"))
                    elif part == "keys3":
                        ve.wait_ge(sem("scored"), after("scored", (u, 3, "n")))
                        if G:
                            ve.wait_ge(sem("turned"), after("turned", ((l, "win", 0), "ptn")))
                        cp(sW[:, 0:512], bank(psk((u, "S", 0)))).then_inc(sem("vector_step"), up("vector_step", frees=[("psum", (u, "S", 0))]))
                        ve.wait_ge(sem("vector_step"), now("vector_step"))
                        w0 = sW[:, 0:512].rearrange("p (s c) -> p s c", s=4)[:, :, 0]
                        v(tt(w0, w0, cst[:, K_WINM:K_WINM + 4], ALU.add))
                        tt(sW[:, 512:544], pst[:, psk((u, "Sn")), 0:NS], nm, ALU.add).then_inc(sem("vector_step"), up("vector_step", frees=[("psum", (u, "Sn"))]))
                        ve.wait_ge(sem("vector_step"), now("vector_step"))
                        V.tensor_reduce(sm[:, 88:89], sW[:, :], AX.X, ALU.max, negate=True).then_inc(sem("neg_max"), up("neg_max", u))
                        ve.wait_ge(sem("neg_max"), now("neg_max"))
                    elif part == "turn":
                        if pn >= 2:
                            for s, n_ in freed(("pt", pn - 2)):
                                ve.wait_ge(s, n_)
                        ve.wait_ge(sem("turned"), after("turned", (u, "pt")))
                        cp(prob_slot(pn), bank(psk((u, "pt")))).then_inc(sem("copied_v"), up("copied_v", (u, "pt"), frees=[("psum", (u, "pt"))]))
                        ve.wait_ge(sem("copied_v"), now("copied_v"))
                        ve.wait_ge(sem("turned"), after("turned", (u, "ptn")))
                        m = P if e is None else 32
                        cp(new_slot(pn)[0:NS, 0:m], pst[0:NS, psk((u, "ptn")), 0:m]).then_inc(sem("copied_v"), up("copied_v", (u, "ptn"), frees=[("psum", (u, "ptn"))]))
                        ve.wait_ge(sem("copied_v"), now("copied_v"))
                    elif part == "values":
                        if e is None:
                            v(tt(sm[:, 96:97], sm[:, 90:91], sm[:, 91:92], ALU.add))
                            v(V.reciprocal(sm[:, 97:98], sm[:, 96:97]))
                        else:
                            v(V.reciprocal(sm[r, 97:98], sm[r, 92:93]))
                        br = 2 if e is None else 1
                        v(tt(sm[r, 97:98], sm[r, 97:98], gs[r, G, br:br + 1], ALU.mult))
                        ve.wait_ge(sem("summed_values"), after("summed_values", (u, 0)))
                        stt(comb[r, G, :], pst[r, psk((u, "O")), 0:P], sm[r, 97:98], comb[r, G, :], ALU.mult, ALU.add).then_inc(sem("vector_step"), up("vector_step", frees=[("psum", (u, "O"))]))
                        ve.wait_ge(sem("vector_step"), now("vector_step"))
                        if e == 3:
                            tt(comb[:, G, :], comb[:, G, :], cst[:, K_HM:K_HM + P], ALU.mult).then_inc(sem("comb_ready"), up("comb_ready", (l, G)))
                            ve.wait_ge(sem("comb_ready"), now("comb_ready"))
                    elif part == "output":
                        ve.wait_ge(sem("o_turned"), after("o_turned", (l, "s", G)))
                        b = psk((l, G, "oTs"))
                        for h in range(2):
                            hr = slice(h * HD, (h + 1) * HD)
                            for g in range(GR):
                                src = pst[hr, b, 0:P].rearrange("p (b h g t) -> p b h g t", b=4, h=2, g=4)[:, :, h, g, :]
                                dst = hT[hr, g, SEQ + 16 * G:SEQ + 16 * G + 16].rearrange("p (b t) -> p b t", b=4)
                                last = (h, g) == (1, 3)
                                cp(dst, src).then_inc(sem("oT_copied" if last else "vector_step"), up("oT_copied" if last else "vector_step", (l, "s", G) if last else None, frees=[("psum", (l, G, "oTs"))] if last else []))
                                ve.wait_ge(sem("oT_copied" if last else "vector_step"), now("oT_copied" if last else "vector_step"))

                ve.wait_ge(sem("gates_spread"), after("gates_spread", l))
                for who_, what, n in plan:
                    if who_ == "sample":
                        sample_part(what, *n)
                    elif who_ == "sample_cmp":
                        sample_cmp(what, n)
                    elif who_ == "tile":
                        if what == "scores":
                            cmp_shift(n)
                        elif what == "turn":
                            copy_ts((l, n, "c"), 256)
                        elif what == "values":
                            gated(n, "c")
                        elif what == "output":
                            copy_o(n)
                    elif what == "scores":
                        p_max(n)
                    elif what == "turn":
                        copy_ts((l, todo[n], 0), (todo[n][0] + 1) * P)
                    elif n % 4 == 3:
                        gated(*todo[n][0:2])
                post(l, 1, P_NORM + 8)
                pre(l, 2, P_NORM + 16)
                for r in range(RND):
                    for f in range(r * FR, (r + 1) * FR):
                        gp = gpad[f % 2]
                        ve.wait_ge(sem("g_copied"), after("g_copied", (l, f)))
                        ve.wait_ge(sem("prefix_copied"), after("prefix_copied", (l, f)))
                        if f:
                            ve.wait_ge(sem("gelu_done"), after("gelu_done", (l, f - 1)))
                        cw = lambda k: par[:, P_FCW + FT * k + f:P_FCW + FT * k + f + 1]
                        v(tsc(cF, gp[:, 0:560], cw(0), par[:, P_FCB + f:P_FCB + f + 1], ALU.mult, ALU.add))
                        v(stt(cF, gp[:, 1:561], cw(1), cF, ALU.mult, ALU.add))
                        stt(cF, gp[:, 2:562], cw(2), cF, ALU.mult, ALU.add).then_inc(sem("conv_done"), up("conv_done", (l, "f", f)))
                        ve.wait_ge(sem("conv_done"), now("conv_done"))
                        ve.wait_ge(sem("gelu_done"), after("gelu_done", (l, f)))
                        ve.wait_ge(sem("projected"), after("projected", (l, "u", f)))
                        if r:
                            ve.wait_ge(sem("projected"), after("projected", (l, "down", r - 1, KT - 1)))
                        b = psk((l, "u", f))
                        tt(halves(actT[:, f % FR, :]), pair(b), halves(gF), ALU.mult).then_inc(sem("act_ready"), up("act_ready", (l, f), frees=[("psum", (l, "u", f))]))
                        ve.wait_ge(sem("act_ready"), now("act_ready"))
                    if r:
                        for j in range(KT):
                            ve.wait_ge(sem("projected"), after("projected", (l, "down", r, j)))
                            b = psk((l, "down", r, j))
                            if r == 1 and j == 0:
                                ve.wait_ge(sem("m_copied"), after("m_copied", (l, KT - 1)))
                            tt(halves(mT[:, j, :]), pair(b), halves(mT[:, j, :]), ALU.add).then_inc(sem("m_summed"), up("m_summed", (l, r, j), frees=[("psum", (l, "down", r, j))]))
                            ve.wait_ge(sem("m_summed"), now("m_summed"))
                post(l, 3, P_NORM + 24)
            ve.wait_ge(sem("states_copied"), after("states_copied", (DEPTH - 1, 5)))
            for k in range(0, KT, 2):
                ve.wait_ge(sem("y_turned"), after("y_turned", k))
                b = psk(("y", k))
                v(cp(yout[:, :, k * P:(k + 1) * P], bank(b).rearrange("p (t c) -> p t c", t=4)))
                cp(youts[:, k * P:(k + 1) * P], pst[0:NS, b + 1, 0:P]).then_inc(sem("y_copied_v"), up("y_copied_v", k, frees=[("psum", ("y", k))]))
                ve.wait_ge(sem("y_copied_v"), now("y_copied_v"))
        return S

_INS = ["x_prompt", "x_sample", "cache_cmp_kv", "cache_slc_kv", "cache_win_kv", "state_rg_h", "state_rg_conv",
        "state_ffn_conv", "page_table", "norm_mix_pre", "norm_mix_post", "norm_ffn_pre", "norm_ffn_post", "w_in",
        "rg_conv_w", "rg_conv_b", "rg_wa", "rg_ba", "rg_wx", "rg_bx", "rg_lambda", "cmpk_pe", "cmpk_w1", "cmpk_b1",
        "cmpk_w2", "cmpv_pe", "cmpv_w1", "cmpv_b1", "cmpv_w2", "w_out", "ffn_w_in", "ffn_conv_w", "ffn_conv_b",
        "ffn_w_down"]
_KV = (2, NKV, HD)
_OUTS = {"y_p": (1, SEQ, D), "y_s": (DB, DT, D), "p_cmp": (DEPTH, 1, SEQ) + _KV, "s_cmp": (DEPTH, DB, DT) + _KV,
         "p_slc": (DEPTH, 1, SEQ) + _KV, "s_slc": (DEPTH, DB, DT) + _KV, "p_win": (DEPTH, 1, WIN) + _KV,
         "s_win": (DEPTH, DB, WIN) + _KV, "p_rgh": (DEPTH, 1, DR), "s_rgh": (DEPTH, DB, DR),
         "p_rgc": (DEPTH, 1, 3, DR), "s_rgc": (DEPTH, DB, 3, DR), "p_ffc": (DEPTH, 1, 2, DF), "s_ffc": (DEPTH, DB, 2, DF)}

def kernel(**inputs):
    import concourse.bacc as bacc
    from concourse.bass_utils import run_bass_kernel_spmd

    arrays = {f"in_{n}": np.ascontiguousarray(inputs[n]) for n in _INS}
    arrays["in_consts"] = constants()

    def build(known):
        nc = bacc.Bacc("TRN2", target_bir_lowering=False, num_devices=1)
        ins = {n[3:]: nc.dram_tensor(n, a.shape, mybir.dt.from_np(a.dtype), kind="ExternalInput").ap()
               for n, a in arrays.items()}
        outs = {n: nc.dram_tensor(f"out_{n}", shape, F32, kind="ExternalOutput").ap() for n, shape in _OUTS.items()}
        return nc, hybrid_step(nc, ins, outs, known)

    _, counts = build(None)
    nc, _ = build(counts)
    r = run_bass_kernel_spmd(nc, [arrays], core_ids=[0])
    return tuple(r.results[0][f"out_{n}"] for n in _OUTS)
```

```python
from contextlib import ExitStack

import numpy as np
import concourse.bass as bass
from concourse import mybir

F32 = mybir.dt.float32
I32 = mybir.dt.int32
U32 = mybir.dt.uint32
ALU = mybir.AluOpType
ACT = mybir.ActivationFunctionType
AX = mybir.AxisListType

P = 128
D = 1024
SEQ, DB, DT = 512, 8, 4
NS = DB * DT
T = SEQ + NS
TH = T // 2
DEPTH = 2
PAST, PAGE = 2048, 128
DR = 512
RJ = DR // P
NH, HD, NKV, GR = 8, 64, 2, 4
STRIDE = 16
CPP = PAGE // STRIDE
NCH = PAST // STRIDE
NCP = SEQ // STRIDE
SB = 64
NSB = PAST // SB + 1
WIN = 512
DF = 3072
FT = DF // P
KT = D // P
RND = 3
FR = FT // RND
NIN = 2328
C_GATE, C_Q, C_KVC, C_KVS, C_KVW, C_GL = 512, 1024, 1536, 1792, 2048, 2304
EPS = 1e-6
BIG = 1e30
THETA = 10000.0
TT = [(t * P, min(P, T - t * P)) for t in range(5)]
NPOOL = DB * (PAST // PAGE) * 5 // 4
NW, NA, NTS, NKS = 5, 3, 5, 4

K_ID, K_ROT, K_CH, K_CAUS, K_GSUM, K_HM, K_CMPM, K_NEWM, K_WINM, K_REP, K_PICK = \
    0, 128, 256, 260, 388, 516, 644, 772, 836, 840, 1096
K_COS, K_SIN, K_COSK, K_SINK, K_ALL = 1120, 1120 + T, 1120 + 2 * T, 1120 + 2 * T + 320, 1120 + 2 * T + 640

P_NORM, P_RCW, P_RCB, P_BA, P_BX, P_LAM, P_B1, P_PE, P_N0 = 0, 32, 48, 52, 56, 60, 64, 66, 98
P_FCW, P_FCB = 98, 170
P_H0, P_RC = 194, 226
P_FS = 322
P_ALL = 706

def constants():
    c = np.zeros((P, K_ALL), np.float32)
    c[:, K_ID:K_ID + P] = np.eye(P)
    for m in range(P):
        if m % 64 < 32:
            c[m + 32, K_ROT + m] = -1.0
        else:
            c[m - 32, K_ROT + m] = 1.0
    q = np.arange(P)
    c[:, K_CAUS:K_CAUS + P] = np.where(q[None, :] <= q[:, None], 0.0, -BIG)
    b, h, g, t = q // 32, q // 16 % 2, q // 4 % 4, q % 4
    same = (b[:, None] == b) & (h[:, None] == h) & (t[:, None] == t)
    c[:, K_GSUM:K_GSUM + P] = same
    c[:, K_HM:K_HM + P] = h[:, None] == (q // 64)[None, :]
    ch = np.arange(NCP)
    for i in range(4):
        ok = (ch[None, :] * STRIDE + 2 * STRIDE - 1 <= (i * P + q)[:, None]) & (ch < NCP - 1)[None, :]
        c[:, K_CMPM + i * NCP:K_CMPM + (i + 1) * NCP] = np.where(ok, 0.0, -BIG)
    n = np.arange(NS)
    for G in range(2):
        ok = ((n // DT)[None, :] == (4 * G + b)[:, None]) & ((n % DT)[None, :] <= t[:, None])
        c[:, K_NEWM + G * NS:K_NEWM + (G + 1) * NS] = np.where(ok, 0.0, -BIG)
        c[:NS, K_REP + G * P:K_REP + (G + 1) * P] = ((n // DT)[:, None] == (4 * G + b)[None, :]) & \
            ((n % DT)[:, None] == t[None, :])
    c[:, K_WINM:K_WINM + 4] = np.where(np.arange(4)[None, :] <= t[:, None], -BIG, 0.0)
    for j in range(3):
        c[:, K_PICK + j * 8:K_PICK + j * 8 + 8] = (h * GR + g)[:, None] == np.arange(8)[None, :]
    c[:, K_CH] = q % CPP
    pos = np.concatenate([np.arange(SEQ), PAST + np.arange(NS) % DT]).astype(np.float32)
    half = HD // 2
    freq = (np.float32(THETA) ** (-np.arange(half, dtype=np.float32) / np.float32(half))).astype(np.float32)
    ang = pos[:, None] * freq[None, :]
    cos, sin = np.cos(ang), np.sin(ang)
    c[:, K_COS:K_COS + T] = np.tile(cos.T, (4, 1))
    c[:, K_SIN:K_SIN + T] = np.tile(sin.T, (4, 1))
    for i, (t0, m) in enumerate(TT):
        c[:m, K_COSK + i * 64:K_COSK + i * 64 + 64] = np.tile(cos[t0:t0 + m], (1, 2))
        c[:m, K_SINK + i * 64:K_SINK + i * 64 + 32] = -sin[t0:t0 + m]
        c[:m, K_SINK + i * 64 + 32:K_SINK + i * 64 + 64] = sin[t0:t0 + m]
    return c

class Counts:

    def __init__(self, nc, ctx, known):
        self.nc, self.ctx, self.known = nc, ctx, known
        self.sems, self.count, self.table, self.read = {}, {}, {}, {}
        self.bank_of, self.last_use, self.slot_of, self.bank_key = {}, {}, {}, {}

    def sem(self, name):
        if name not in self.sems:
            self.sems[name] = self.ctx.enter_context(self.nc.semaphore(name))
            self.count[name] = 0
        return self.sems[name]

    def up(self, name, key=None, frees=(), by=1):
        self.count[name] += by
        if key is not None:
            self.table[name, key] = self.count[name]
        for buffer in frees:
            self.read.setdefault(buffer, {})[name] = self.count[name]
        return by

    def now(self, name):
        return self.count[name]

    def after(self, name, key):
        return self.known.table[name, key] if self.known else 1

    def freed(self, buffer):
        if not self.known:
            return []
        return [(self.sem(name), value) for name, value in self.known.read.get(buffer, {}).items()]

def hybrid_step(nc, I, O, known=None):
    ctx = ExitStack()
    with ctx:
        S = Counts(nc, ctx, known)
        sem, up, now, after, freed = S.sem, S.up, S.now, S.after, S.freed
        sb = lambda name, cols, dt=F32: ctx.enter_context(nc.sbuf_tensor(name, [P, cols], dt))
        xT = sb("xT", KT * T)[:].rearrange("p (k t) -> p k t", k=KT)
        hT = sb("hT", KT * T)[:].rearrange("p (k t) -> p k t", k=KT)
        ov = sb("ov", 12256)
        wr = sb("wr", NW * 1024)[:].rearrange("p (s k c) -> p s k c", s=NW, k=8)
        ar = sb("ar", NA * 4096)
        w1 = sb("w1", 4096)[:].rearrange("p (v s f) -> p v s f", v=2, s=16)
        ts = sb("ts", NTS * 512)
        kcT = sb("kcT", DB * 127)[:].rearrange("p (b c) -> p b c", b=DB)
        vc = sb("vc", DB * P)[:].rearrange("p (b c) -> p b c", b=DB)
        par = sb("par", P_ALL)
        cst = sb("cst", K_ALL)
        ov2 = sb("ov2", 1024)
        hid = sb("hid", 512)
        sm_row = hid[0:1, 0:2 * P]
        free1, freek, freev = (x.rearrange(r) for x, r in ((w1, "p v s f -> p (v s f)"), (kcT, "p b c -> p (b c)"),
                                                           (vc, "p b c -> p (b c)")))
        sQ, sW = free1[:, 0:2080], freek[:, 256:800]
        key_slot = lambda n: (free1[:, 2080:2592], free1[:, 2592:3104], free1[:, 3104:3616], hid[:, 0:512])[n % NKS]
        probs, probs_new = freev[:, 0:1024], freek[:, 0:P]
        w2 = sb("w2", 128)[:].rearrange("p (v d) -> p v d", v=2)
        WG = P + 24
        wvg = ts[:, 0:8 * WG].rearrange("p (k c) -> p k c", k=8)
        gates = sb("gates", 120)[:].rearrange("p (t c) -> p t c", t=5)
        gs = sb("gs", 6)[:].rearrange("p (g c) -> p g c", g=2)
        ones = sb("ones", P)
        sm = sb("sm", 288)
        outr = sb("outr", 144)
        idi = sb("idi", (1 + DEPTH) * DB, I32)
        pst = ctx.enter_context(nc.psum_tensor("ps", [P, 8, 512], F32))

        ident = cst[:, K_ID:K_ID + P]
        rot = cst[:, K_ROT:K_ROT + P]
        cosT, sinT = cst[:, K_COS:K_COS + T], cst[:, K_SIN:K_SIN + T]
        cosk = cst[:, K_COSK:K_COSK + 320].rearrange("p (t d) -> p t d", t=5)
        sink = cst[:, K_SINK:K_SINK + 320].rearrange("p (t d) -> p t d", t=5)

        o3 = lambda a, n: ov[:, a:a + n * T].rearrange("p (k t) -> p k t", k=n)
        yT = o3(0, 4)
        qcT, qrT = o3(2176, 4), o3(4352, 4)
        sS = ov[:, 6528:8608]
        kvt = {"c": ov[:, 6528:7808], "s": ov[:, 8608:9888], "w": ov[:, 9888:11168]}
        kvt = {n: v.rearrange("p (t c) -> p t c", t=5) for n, v in kvt.items()}
        kT = {"s": ov[:, 11168:11712], "w": ov[:, 11712:12256]}
        mT = o3(2176, 8)
        actT = o3(6528, 8)
        gpad = [ov[:, 10880 + 562 * i:10880 + 562 * (i + 1)] for i in range(2)]
        cF, gF, fcb = ov[:, 0:560], ov[:, 560:1104], ov[:, 1104:1536]
        R0 = 6825
        xrp = ov[:, R0:R0 + 571]
        cR = ov[:, R0 + 571:R0 + 1139]
        xc, rt, aR, tR, iR, hR, gR = (ov[:, R0 + 1139 + i * T:R0 + 1139 + (i + 1) * T] for i in range(7))
        recR = cR[:, 0:T]
        wbd = ov2[:, :].rearrange("p (v j c) -> p v j c", v=2, j=RJ)
        qbd = ov2[:, 0:512].rearrange("p (v b r) -> p v b r", v=2, b=DB)
        vbd = ov2[:, 512:1024].rearrange("p (h g d) -> p h g d", h=2, g=4)
        stage = lambda i: hid[:, 0:P] if i == 5 else ov[:, 1536 + i * P:1536 + (i + 1) * P]
        st_out = ov[:, 11424:12192]
        h4 = hT[:, 4:8, :].rearrange("p k t -> p (k t)")
        o_sb, o_tmp, pc_s, pc_p = h4[:, 0:512], h4[:, 512:1024], h4[:, 1024:1280], h4[:, 1280:1536]
        hidrep = h4[:, 512:768].rearrange("p (h c) -> p h c", h=2)
        comb = h4[:, 1536:1792].rearrange("p (g c) -> p g c", g=2)
        xs_slot = lambda n: h4[:, 768 * (n % 2):768 * (n % 2) + 512]
        pp, kcTp = h4[:, 1792:1928], h4[:, 1928:1960]
        cmp_p = h4[:, 1960:2087]
        idx = h4[:, 0:3 * DB]
        p_slot = lambda m: sS[:, (m % 4) * 512:(m % 4 + 1) * 512]
        mb = lambda G: sm[:, 208 + 36 * G:208 + 36 * G + 33]
        per7 = ov[:, R0 + 571 + 515:R0 + 571 + 515 + 56].rearrange("p (b c) -> p b c", b=DB)[:, :, 0:DT]
        per6 = ov[:, 514:562].rearrange("p (b c) -> p b c", b=DB)[:, :, 0:DT]

        def rearranged(u, v, s4, e, n):
            nch = NCH if u[1] == "cmp" else NCP
            r = 4 * s4 + 2 * e
            src = av(load_no[u]).rearrange("p (s c) -> p s c", s=STRIDE)[0:nch, r:r + 2, v * P:(v + 1) * P]
            dst = xs_slot(n)[0:nch, 256 * e:256 * e + 256]
            return dst.rearrange("p (h s d) -> p h s d", h=2, s=2), src.rearrange("p s (h d) -> p h s d", h=2)

        def hid_of(u, v):
            n = 127 if u[1] == "cmp" else NCP
            return hid[:, v * 254:v * 254 + 2 * n].rearrange("p (h c) -> p h c", h=2)

        OUTT = [("rg", 0, 48), ("rgc", 48, 144), ("pf", 0, 48), ("sf0", 48, 176), ("sf1", 176, 304), ("sf2", 304, 432)]
        xin = ov[:, 2176:2176 + 5 * D].rearrange("p (t d) -> p t d", t=5)
        yout = hT.rearrange("p k t -> p (k t)")[:, 0:4 * D].rearrange("p (t d) -> p t d", t=4)
        youts = ov[0:NS, 0:D]

        halves = lambda ap: ap.rearrange("p (h t) -> p h t", h=2)
        pair = lambda b: pst[:, b:b + 2, 0:TH]
        flat = lambda b, n: pst[:, b:b + 2, :].rearrange("p a c -> p (a c)")[:, 0:n]
        bank = lambda b: pst[:, b, :]
        wv = lambda n: wr[:, n % NW]
        av = lambda n: ar[:, (n % NA) * 4096:(n % NA + 1) * 4096]
        tv = lambda n: ts[:, (n % NTS) * 512:(n % NTS + 1) * 512]

        units = []
        for l in range(DEPTH):
            for j in range(RJ):
                units += [(l, "xr", j), (l, "gate", j)]
            units += [(l, "q", g) for g in range(4)]
            units += [(l, "kv", n) for n in ("s0", "s1", "w0", "c0", "c1")]
            units += [(l, "out", j) for j in range(KT)]
            for r in range(RND):
                for f in range(r * FR, (r + 1) * FR):
                    units += [(l, "g", f), (l, "u", f)]
                units += [(l, "down", (r, j)) for j in range(KT)]
        unit_no = {u: n for n, u in enumerate(units)}
        compressed_units = lambda l: [(l, "cmp", x) for x in range(DB - 1)] + [(l, "cmpp", 0), (l, "cmp", DB - 1)]
        loads = []
        for l in range(DEPTH):
            loads += compressed_units(l)
            for G in range(2):
                loads += [(l, "win", G)] + [(l, "slc", 4 * G + b) for b in range(4)]
        load_no = {u: n for n, u in enumerate(loads)}

        todo = [(i, br, g) for i in range(4) for br in "sw" for g in range(GR)]
        sample_units = [(G, e) for G in range(2) for e in (None, 0, 2)]
        WIN_PARTS = {"keys0": 0, "keys1": 1, "keys2": 2, "keys3": 3, "exp": 4, "turn": 8, "values": 10}
        SLC_PARTS = {"keys0": 0, "keys1": 1, "keys2": 2, "keys3": 7, "keys4": 8, "exp": 10, "turn": 13, "values": 15, "output": 17}
        START = (1, 4, 11, 17, 20, 28)
        FIRST_KEY = (0, 4, 12, 20, 24, 32, 40)
        CMP_PARTS = {4: ("scores", 0), 5: ("group", 0), 6: ("values", 0), 8: ("scores", 1)}
        plan = []
        for n in range(len(todo) + 3):
            for s, what in enumerate(("scores", "turn", "values")):
                if 0 <= n - s < len(todo):
                    plan.append(("prompt", what, n - s))
                for i in range(4):
                    for part, at in (("scores", (3, 1)), ("exp", (3, 2)), ("turn", (4, 1)), ("values", (4, 2)), ("output", (10, 1))):
                        if (n - 8 * i, s) == at:
                            plan.append(("tile", part, i))
                if 3 * n + s in (1, 4):
                    plan.append(("sample_cmp", "group" if n == 0 else "values", 1))
                for k, (G, e) in enumerate(sample_units):
                    for part, at in (WIN_PARTS if e is None else SLC_PARTS).items():
                        if 3 * n + s == 3 * START[k] + 2 + at and (part != "output" or e == 2):
                            plan.append(("sample", part, (k, G, e)))

        block = ctx.enter_context(nc.Block())

        @block.tensor
        def _(pe):
            
            cyc = {"pair": 0, "one": 0, "acc": 0, "quad": 0}

            def take(key, kind):
                banks, c, width = {"pair": ((0, 2), "pair", 2), "wide": ((0, 2), "pair", 2), "one": ((4, 5), "one", 1),
                                   "acc": ((6, 7), "acc", 1), "quad": ((0, 1, 2, 3), "quad", 1),
                                   "two": ((0, 1, 2, 3), "quad", 2)}[kind]
                if kind == "two":
                    cyc[c] += cyc[c] % 2
                b = banks[cyc[c] % len(banks)]
                cyc[c] += 2 if kind == "two" else 1
                for x in range(b, b + width):
                    if x in S.last_use:
                        for s, n_ in freed(("psum", S.last_use[x])):
                            pe.wait_ge(s, n_)
                    S.last_use[x] = key
                S.bank_of[key] = b
                return b

            mm = lambda o, a, b, st, sp: nc.tensor.matmul(o, a, b, start=st, stop=sp)

            def weights(u):
                n = unit_no[u]
                pe.wait_ge(sem(f"w_loaded{n % NW}"), after(f"w_loaded{n % NW}", n))
                return wv(n)

            def project(u, rhs, key, ready=None, by_half=False):
                w = weights(u)
                b = take(key, "pair")
                for k, h in [(k, h) for h in range(2) for k in range(KT)] if by_half else [(k, h) for k in range(KT) for h in range(2)]:
                    if ready:
                        ready(k, h)
                    i = mm(pst[:, b + h, 0:TH], w[:, k, :], rhs(k)[:, h * TH:(h + 1) * TH], k == 0, k == KT - 1)
                i.then_inc(sem("projected"), up("projected", key, frees=[("w", unit_no[u])]))

            def stats(l, n, sq):
                b = take((l, n, "rstd"), "pair")
                for k in range(KT):
                    pe.wait_ge(sem("squared"), after("squared", (l, n, k)))
                    for h in range(2):
                        i = mm(pst[:, b + h, 0:TH], ones[:, :], sq[:, k, h * TH:(h + 1) * TH], k == 0, k == KT - 1)
                i.then_inc(sem("summed"), up("summed", (l, n)))

            def turn_params(l, tiles):
                for i in tiles:
                    r = (98, 96, 128, 128, 128, 128)[i]
                    b = take((l, "par", i), ("one", "one", "acc", "acc", "one", "one")[i])
                    pe.wait_ge(sem("params_loaded"), after("params_loaded", l))
                    j = nc.tensor.transpose(pst[:, b, 0:r], stage(i)[0:r, :], ident[0:r, 0:r])
                    j.then_inc(sem("params_turned"), up("params_turned", (l, i)))

            pe.wait_ge(sem("const_loaded"), after("const_loaded", 0))
            pe.wait_ge(sem("ones_set"), after("ones_set", 0))
            pe.wait_ge(sem("x_loaded"), after("x_loaded", 0))
            for k in range(KT):
                b = take(("x", k), "wide")
                for t, (t0, m) in enumerate(TT):
                    i = nc.tensor.transpose(flat(b, T)[:, t0:t0 + m], xin[0:m, t, k * P:(k + 1) * P], ident[0:m, 0:m])
                i.then_inc(sem("x_turned"), up("x_turned", k))

            tsn, xsn = [0], [0]

            def slot(key, bank_key=None):
                S.slot_of[key], S.bank_key[key] = tsn[0], bank_key or key
                tsn[0] += 1
                return tsn[0] - 1

            def compress(l, us):
                quarters = [(u, v, s4) for u in us for v in range(2) for s4 in range(4)]

                def turn(u, v, s4):
                    nch = NCH if u[1] == "cmp" else NCP
                    b = take((u, "xt", v, s4), "one")
                    pe.wait_ge(sem("rearranged_v" if s4 == 3 else "rearranged"), after("rearranged_v" if s4 == 3 else "rearranged", (u, v, s4)))
                    x = xs_slot(xsn[0])
                    for c in range(4):
                        i = nc.tensor.transpose(pst[:, b, c * nch:(c + 1) * nch], x[0:nch, c * P:(c + 1) * P],
                                                ident[0:nch, 0:nch])
                    i.then_inc(sem("turned"), up("turned", (u, "xt", v, s4), frees=[("xs", xsn[0])]))
                    xsn[0] += 1
                    slot((u, "xt", v, s4))

                def product(u, v, s4):
                    nch = NCH if u[1] == "cmp" else NCP
                    if s4 == 0:
                        take((u, "hid", v), "acc")
                    hb = S.bank_of[u, "hid", v]
                    n = S.slot_of[u, "xt", v, s4]
                    pe.wait_ge(sem("copied_a" if s4 % 2 else "copied_v"), after("copied_a" if s4 % 2 else "copied_v", (u, "xt", v, s4)))
                    x = tv(n)[:, 0:4 * nch].rearrange("p (e h c) -> p e h c", e=2, h=2)
                    for e in range(2):
                        sp = 2 * s4 + e
                        o = pst[:, hb, 0:2 * (nch - 1)].rearrange("p (h c) -> p h c", h=2)
                        mm(o, w1[:, v, sp, :], x[:, e, :, 0:nch - 1], sp == 0, False)
                        i = mm(o, w1[:, v, 8 + sp, :], x[:, e, :, 1:nch], False, sp == 7)
                    i.then_inc(sem("compressed"), up("compressed", (u, v, s4), frees=[("ts", n)]))

                turn(*quarters[0])
                turn(*quarters[1])
                for q, (u, v, s4) in enumerate(quarters):
                    product(u, v, s4)
                    x = us.index(u)
                    if x and (v, s4) == (0, 0):
                        compress2(us[x - 1])
                    if u == us[-1] and (v, s4) == (1, 3):
                        compress2(u)
                    if q + 2 < len(quarters):
                        turn(*quarters[q + 2])
                    if (v, s4) == (1, 3) and x in CMP_PARTS:
                        sample_cmp(l, *CMP_PARTS[x])

            def compress2(u):
                nch = NCH if u[1] == "cmp" else NCP
                for v in range(2):
                    b = take((u, "c2", v), "quad")
                    pe.wait_ge(sem("hidden_rep" if u[1] == "cmpp" and v else "hidden"), after("hidden_rep" if u[1] == "cmpp" and v else "hidden", (u, v)))
                    for h in range(2):
                        if v == 0:
                            m = nch - 1 if u[1] == "cmp" else nch
                            i = mm(pst[h * HD:(h + 1) * HD, b, 0:m], w2[:, 0, :], hid_of(u, 0)[:, h, :], True, True)
                        elif u[1] == "cmp":
                            i = mm(pst[0:nch - 1, b, h * HD:(h + 1) * HD], hid_of(u, 1)[:, h, :], w2[:, 1, :], True, True)
                        else:
                            i = mm(pst[:, b, h * HD:(h + 1) * HD], hidrep[:, h, :], w2[:, 1, :], True, True)
                    i.then_inc(sem("compressed2"), up("compressed2", (u, v)))

            def prompt_attention(l):
                st = {}

                def scores(u):
                    i, br, g = u
                    L = (i + 1) * P
                    b = take((l, u, "S"), "two")
                    for h in range(2):
                        j = mm(pst[:, b + h, 0:L], qrT[h * HD:(h + 1) * HD, g, i * P:(i + 1) * P],
                               kT[br][h * HD:(h + 1) * HD, 0:L], True, True)
                    j.then_inc(sem("scored"), up("scored", (l, u)))

                def turn(u):
                    i, br, g = u
                    for h in range(2):
                        st[u] = st.get(u, []) + [slot((l, u, h), (l, u, "T", h))]
                        pe.wait_ge(sem("p_exp"), after("p_exp", (l, u, h)))
                        b = take((l, u, "T", h), "one")
                        for c in range(i + 1):
                            j = nc.tensor.transpose(pst[:, b, c * P:(c + 1) * P],
                                                    p_slot(todo.index(u) * 2 + h)[:, c * P:(c + 1) * P], ident)
                        j.then_inc(sem("turned"), up("turned", (l, u, h), frees=[("p", l, todo.index(u) * 2 + h)]))

                def values(u):
                    i, br, g = u
                    if g == 0:
                        take((l, i, br, "O"), "acc")
                    b = S.bank_of[l, i, br, "O"]
                    for h in range(2):
                        pe.wait_ge(sem("copied_a" if h else "copied_v"), after("copied_a" if h else "copied_v", (l, u, h)))
                        x = tv(st[u][h])
                        hd = g * 2 + h
                        for c in range(i + 1):
                            j = mm(pst[:, b, hd * HD:(hd + 1) * HD], x[:, c * P:(c + 1) * P],
                                   kvt[br][:, c, P + h * HD:P + (h + 1) * HD], c == 0, c == i)
                        j.then_inc(sem("summed_values"), up("summed_values", (l, u, h), frees=[("ts", st[u][h])]))

                def cmp_scores(i):
                    b = take((l, i, "Sc"), "two")
                    for h in range(2):
                        for g in range(GR):
                            j = mm(pst[:, b + h, g * NCP:(g + 1) * NCP],
                                   qcT[h * HD:(h + 1) * HD, g, i * P:(i + 1) * P],
                                   kcTp[h * HD:(h + 1) * HD, :], True, True)
                    j.then_inc(sem("scored"), up("scored", (l, i, "c")))

                def cmp_turn(i):
                    b = take((l, i, "Tc"), "one")
                    n = slot((l, i, "c"), (l, i, "Tc"))
                    pe.wait_ge(sem("cmp_exp"), after("cmp_exp", (l, i)))
                    for h in range(2):
                        j = nc.tensor.transpose(pst[:, b, h * P:(h + 1) * P], pc_p[:, h * P:(h + 1) * P], ident)
                    j.then_inc(sem("turned"), up("turned", (l, i, "c")))

                def cmp_values(i):
                    n = S.slot_of[l, i, "c"]
                    b = take((l, i, "c", "O"), "one")
                    pe.wait_ge(sem("copied_v"), after("copied_v", (l, i, "c")))
                    for h in range(2):
                        j = mm(pst[:, b, :].rearrange("p (g h d) -> p g h d", g=GR, h=2)[:, :, h, :], tv(n)[:, h * P:(h + 1) * P],
                               vbd[:, h].rearrange("p g d -> p (g d)"), True, True)
                    j.then_inc(sem("summed_values"), up("summed_values", (l, i, "c"), frees=[("ts", n)]))

                def turn_o(i):
                    b = take((l, i, "oT"), "one")
                    pe.wait_ge(sem("o_gated"), after("o_gated", (l, i)))
                    for g in range(GR):
                        j = nc.tensor.transpose(pst[:, b, g * P:(g + 1) * P], o_sb[:, g * P:(g + 1) * P], ident)
                    j.then_inc(sem("o_turned"), up("o_turned", (l, i)))

                for who_, what, n in plan:
                    if who_ == "sample":
                        sample_part(l, what, *n)
                    elif who_ == "sample_cmp":
                        sample_cmp(l, what, n)
                    elif who_ == "tile":
                        if what == "scores":
                            cmp_scores(n)
                        elif what == "turn":
                            cmp_turn(n)
                        elif what == "values":
                            cmp_values(n)
                        elif what == "output":
                            turn_o(n)
                    elif what == "scores":
                        scores(todo[n])
                    elif what == "turn":
                        turn(todo[n])
                    else:
                        values(todo[n])

            def sample_cmp(l, part, G):
                if part == "scores":
                    b = take((l, G, "Scs"), "quad")
                    for e in range(4):
                        pe.wait_ge(sem("copied_v"), after("copied_v", ((l, "cmp", 4 * G + e), "kc")))
                        pe.wait_ge(sem("qbd_built"), after("qbd_built", l))
                        i = mm(pst[32 * e:32 * e + 32, b, 0:127], qbd[:, 0, 4 * G + e, :], kcT[:, 4 * G + e, :], True, True)
                    i.then_inc(sem("scored"), up("scored", (l, G, "cs")))
                elif part == "group":
                    b = take((l, G, "gsum"), "quad")
                    pe.wait_ge(sem("pn_ready"), after("pn_ready", (l, G)))
                    i = mm(pst[:, b, 0:127], cst[:, K_GSUM:K_GSUM + P], cmp_p, True, True)
                    i.then_inc(sem("group_summed"), up("group_summed", (l, G)))
                else:
                    b = take((l, G, "Tcs"), "quad")
                    n = slot((l, G, "cs"), (l, G, "Tcs"))
                    i = nc.tensor.transpose(pst[0:127, b, 0:P], cmp_p, ident)
                    i.then_inc(sem("turned"), up("turned", (l, G, "cs")))
                    b = take((l, G, "Ocs"), "quad")
                    pe.wait_ge(sem("copied_v"), after("copied_v", (l, G, "cs")))
                    for e in range(4):
                        pe.wait_ge(sem("copied_v"), after("copied_v", ((l, "cmp", 4 * G + e), "vc")))
                        i = mm(pst[32 * e:32 * e + 32, b, 0:P], tv(n)[0:127, 32 * e:32 * e + 32], vc[0:127, 4 * G + e, :], True, True)
                    i.then_inc(sem("summed_values"), up("summed_values", (l, G, "cs"), frees=[("ts", n)]))

            def sample_part(l, part, k, G, e):
                kn = 40 * l + FIRST_KEY[k]
                if e is None:
                    u = (l, "win", G)
                    n = load_no[u]
                    a = av(n).rearrange("p (b s c) -> p b s c", b=4, s=4)
                else:
                    u = (l, "pair", G, e)
                    ns = [load_no[l, "slc", 4 * G + e + b] for b in range(2)]
                    ab = [av(n).rearrange("p (s c) -> p s c", s=STRIDE) for n in ns]

                def turn(x, b2=0):
                    b = take((u, "kt", x, b2), "one")
                    for s in range(4):
                        tile = a[:, x, s, 0:P] if e is None else ab[b2][:, 4 * x + s, 0:P]
                        i = nc.tensor.transpose(pst[:, b, s * P:(s + 1) * P], tile, ident)
                    i.then_inc(sem("turned"), up("turned", (u, "kt", x, b2)))

                def win_score(x):
                    q, r = qbd[:, 1, 4 * G + x, :], slice(32 * x, 32 * x + 32)
                    if x == 0:
                        take((u, "S", 0), "quad")
                        take((u, "Sn"), "quad")
                    pe.wait_ge(sem("copied_a" if x % 2 else "copied_v"), after("copied_a" if x % 2 else "copied_v", (u, "kt", x, 0)))
                    i = mm(pst[r, S.bank_of[u, "S", 0], :], q, key_slot(kn + x), True, True)
                    i.then_inc(sem("scored"), up("scored", (u, x), frees=[("ks", kn + x)]))
                    i = mm(pst[r, S.bank_of[u, "Sn"], 0:NS], q, kT["w"][:, SEQ:T], True, True)
                    i.then_inc(sem("scored"), up("scored", (u, x, "n")))

                def slc_score(x, b2):
                    q, r = qbd[:, 1, 4 * G + e + b2, :], slice(32 * (e + b2), 32 * (e + b2) + 32)
                    if (x % 2, b2) == (0, 0):
                        take((u, "S", x), "two")
                    pe.wait_ge(sem("copied_a" if b2 else "copied_v"), after("copied_a" if b2 else "copied_v", (u, "kt", x, b2)))
                    i = mm(pst[r, S.bank_of[u, "S", x - x % 2] + x % 2, :], q, key_slot(kn + 2 * x + b2), True, True)
                    i.then_inc(sem("scored"), up("scored", (u, x, b2), frees=[("ks", kn + 2 * x + b2)]))

                if part == "keys0":
                    if e is None:
                        pe.wait_ge(sem(f"a_loaded{n % NA}"), after(f"a_loaded{n % NA}", n))
                        turn(0)
                        turn(1)
                    else:
                        for b2 in range(2):
                            pe.wait_ge(sem(f"a_loaded{ns[b2] % NA}"), after(f"a_loaded{ns[b2] % NA}", ns[b2]))
                            turn(0, b2)
                elif part in ("keys1", "keys2", "keys3", "keys4") and e is not None:
                    x = int(part[4]) - 1
                    for b2 in range(2):
                        slc_score(x, b2)
                        if x < 3:
                            turn(x + 1, b2)
                    if x == 3:
                        sb2 = take((u, "Sn"), "one")
                        for b2 in range(2):
                            r = slice(32 * (e + b2), 32 * (e + b2) + 32)
                            i = mm(pst[r, sb2, 0:NS], qbd[:, 1, 4 * G + e + b2, :], kT["s"][:, SEQ:T], True, True)
                        i.then_inc(sem("scored"), up("scored", (u, "n")))
                elif part == "keys1":
                    win_score(0)
                    turn(2)
                elif part == "keys2":
                    win_score(1)
                    turn(3)
                elif part == "keys3":
                    win_score(2)
                    win_score(3)
                elif part == "turn" and e is None:
                    b = take((u, "pt", 0), "one")
                    pe.wait_ge(sem("p_exp"), after("p_exp", u))
                    for s in range(4):
                        i = nc.tensor.transpose(pst[:, b, s * P:(s + 1) * P], sW[:, s * P:(s + 1) * P], ident)
                    i.then_inc(sem("turned"), up("turned", (u, "pt", 0)))
                    b = take((u, "ptn"), "one")
                    i = nc.tensor.transpose(pst[0:NS, b, 0:P], sW[:, 512:512 + NS], ident)
                    i.then_inc(sem("turned"), up("turned", (u, "ptn")))
                elif part == "turn":
                    pe.wait_ge(sem("p_exp"), after("p_exp", u))
                    r = slice(32 * e, 32 * e + 64)
                    for x in range(2):
                        b = take((u, "pt", x), "one")
                        for s in range(8):
                            c = (8 * x + s) * P
                            i = nc.tensor.transpose(pst[:, b, 64 * s:64 * s + 64], sQ[r, c:c + P], ident[r, r])
                        i.then_inc(sem("turned"), up("turned", (u, "pt", x)))
                    b = take((u, "ptn"), "one")
                    i = nc.tensor.transpose(pst[0:NS, b, 0:64], sQ[r, 2048:2048 + NS], ident[r, r])
                    i.then_inc(sem("turned"), up("turned", (u, "ptn")))
                elif part == "values":
                    b = take((u, "O"), "one")
                    pe.wait_ge(sem("copied_v"), after("copied_v", (u, "ptn")))
                    if e is None:
                        for x in range(4):
                            o = pst[32 * x:32 * x + 32, b, 0:P]
                            for s in range(4):
                                mm(o, probs[:, s * P + 32 * x:s * P + 32 * x + 32], a[:, x, s, P:2 * P], s == 0, False)
                            i = mm(o, probs_new[0:NS, 32 * x:32 * x + 32], kvt["w"][0:NS, 4, P:2 * P], False, True)
                        i.then_inc(sem("summed_values"), up("summed_values", (u, 0), frees=[("pt", l, k), ("a", n)]))
                    else:
                        pe.wait_ge(sem("copied_a"), after("copied_a", (u, "pt", 1)))
                        for b2 in range(2):
                            o = pst[32 * (e + b2):32 * (e + b2) + 32, b, 0:P]
                            for s in range(16):
                                mm(o, probs[:, 64 * s + 32 * b2:64 * s + 32 * b2 + 32], ab[b2][:, s, P:2 * P], s == 0, False)
                            i = mm(o, probs_new[0:NS, 32 * b2:32 * b2 + 32], kvt["s"][0:NS, 4, P:2 * P], False, True)
                        i.then_inc(sem("summed_values"), up("summed_values", (u, 0), frees=[("pt", l, k), ("a", ns[0]), ("a", ns[1])]))
                elif part == "output":
                    b = take((l, G, "oTs"), "one")
                    pe.wait_ge(sem("comb_ready"), after("comb_ready", (l, G)))
                    i = nc.tensor.transpose(pst[:, b, 0:P], comb[:, G, :], ident)
                    i.then_inc(sem("o_turned"), up("o_turned", (l, "s", G)))

            for l in range(DEPTH):
                turn_params(l, range(4))
                stats(l, 0, actT)
                for j in range(RJ):
                    rd = (lambda k, h: pe.wait_ge(sem("h_ready"), after("h_ready", (l, 0, k, h)))) if j == 0 else None
                    project((l, "xr", j), lambda k: hT[:, k, :], (l, "xr", j), rd, j == 0)
                    project((l, "gate", j), lambda k: hT[:, k, :], (l, "gate", j))
                    if j == 0:
                        turn_params(l, (4, 5))
                    pe.wait_ge(sem("wbd_loaded"), after("wbd_loaded", l))
                    pe.wait_ge(sem("conv_done"), after("conv_done", (l, j)))
                    for v in range(2):
                        b = take((l, "rg", j, v), "pair")
                        for h in range(2):
                            i = mm(pst[:, b + h, 0:TH], wbd[:, v, j, :], xc[:, h * TH:(h + 1) * TH], True, True)
                        i.then_inc(sem("projected"), up("projected", (l, "rg", j, v)))
                for g in range(GR):
                    project((l, "q", g), lambda k: hT[:, k, :], (l, "q", g))
                b = take((l, "pe"), "one")
                pe.wait_ge(sem("w1_loaded"), after("w1_loaded", l))
                for v in range(2):
                    for s in range(16):
                        i = mm(pst[0:1, b, v * P:(v + 1) * P], par[:, P_PE + 16 * v + s:P_PE + 16 * v + s + 1], w1[:, v, s, :], s == 0, s == 15)
                i.then_inc(sem("pe_row"), up("pe_row", l))
                for g in range(GR):
                    b = take((l, "rot", g), "pair")
                    pe.wait_ge(sem("q_copied"), after("q_copied", (l, g)))
                    for h in range(2):
                        i = mm(pst[:, b + h, 0:TH], rot, qcT[:, g, h * TH:(h + 1) * TH], True, True)
                    i.then_inc(sem("projected"), up("projected", (l, "rot", g)))
                b = take((l, "pec"), "one")
                pe.wait_ge(sem("pe_row_copied"), after("pe_row_copied", l))
                for v in range(2):
                    i = mm(pst[:, b, v:v + 1], sm_row[:, v * P:(v + 1) * P], ones[0:1, 0:1], True, True)
                i.then_inc(sem("pe_summed"), up("pe_summed", l))
                for n in ("s0", "s1", "w0", "w1", "c0", "c1"):
                    b = take((l, "kv", n), "wide")
                    if n == "w1":
                        pe.wait_ge(sem("wvg_loaded"), after("wvg_loaded", l))
                        for t, (t0, m) in enumerate(TT):
                            o = pst[0:m, b + t // 3, t % 3 * WG:(t % 3 + 1) * WG]
                            for k in range(KT):
                                i = mm(o, hT[:, k, t0:t0 + m], wvg[:, k, :], k == 0, k == KT - 1)
                        i.then_inc(sem("projected"), up("projected", (l, "kv", n)))
                        continue
                    w = weights((l, "kv", n))
                    for t, (t0, m) in enumerate(TT):
                        for k in range(KT):
                            i = mm(flat(b, 640)[0:m, t * P:(t + 1) * P], hT[:, k, t0:t0 + m], w[:, k, :], k == 0, k == KT - 1)
                    i.then_inc(sem("projected"), up("projected", (l, "kv", n), frees=[("w", unit_no[l, "kv", n])]))
                for n in "sw":
                    b = take((l, "kT", n), "wide")
                    pe.wait_ge(sem("k_roped"), after("k_roped", (l, n)))
                    for t, (t0, m) in enumerate(TT):
                        i = nc.tensor.transpose(flat(b, T)[:, t0:t0 + m], kvt[n][0:m, t, 0:P], ident[0:m, 0:m])
                    i.then_inc(sem("k_turned"), up("k_turned", (l, n)))
                b = take((l, "gsel"), "one")
                pe.wait_ge(sem("gates_ready"), after("gates_ready", l))
                for G in range(2):
                    i = mm(pst[:, b, 24 * G:24 * G + 24], cst[0:NS, K_REP + G * P:K_REP + (G + 1) * P], gates[0:NS, 4, :], True, True)
                i.then_inc(sem("gates_spread"), up("gates_spread", l))
                compress(l, compressed_units(l))
                pe.wait_ge(sem("kT_copied"), after("kT_copied", (l, "w")))
                pe.wait_ge(sem("q_roped"), after("q_roped", (l, 3)))
                pe.wait_ge(sem("vbd_built"), after("vbd_built", l))
                prompt_attention(l)
                pe.wait_ge(sem("y_ready"), after("y_ready", (l, RJ - 1)))
                pe.wait_ge(sem("oT_copied"), after("oT_copied", (l, "s", 1)))
                pe.wait_ge(sem("oT_copied"), after("oT_copied", (l, 3)))
                for j in range(KT):
                    project((l, "out", j), lambda k: yT[:, k, :] if k < 4 else hT[:, k - 4, :], (l, "out", j))
                stats(l, 1, actT)
                stats(l, 2, actT)
                for r in range(RND):
                    for f in range(r * FR, (r + 1) * FR):
                        rd = (lambda k, h: pe.wait_ge(sem("h_ready"), after("h_ready", (l, 2, k, h)))) if f == 0 else None
                        project((l, "g", f), lambda k: hT[:, k, :], (l, "g", f), rd, f == 0)
                        project((l, "u", f), lambda k: hT[:, k, :], (l, "u", f))
                    for j in range(KT):
                        rd = (lambda k, h: pe.wait_ge(sem("act_ready"), after("act_ready", (l, r * FR + k)))) if j == 0 else None
                        project((l, "down", (r, j)), lambda k: actT[:, k, :], (l, "down", r, j), rd)
                stats(l, 3, hT)
                pe.wait_ge(sem("states_ready"), after("states_ready", (l, "ffn")))
                for i in range(6):
                    r0, r1 = OUTT[i][1:3]
                    src = outr[:, r0:r1] if i < 2 else fcb[:, r0:r1]
                    b = take((l, "st", i), "one")
                    j = nc.tensor.transpose(pst[0:r1 - r0, b, 0:P], src, ident)
                    j.then_inc(sem("states_turned"), up("states_turned", (l, i)))
            for k in range(KT):
                pe.wait_ge(sem("x_added_p" if k % 2 else "x_added_v"), after("x_added_p" if k % 2 else "x_added_v", (DEPTH - 1, 3, k)))
                b = take(("y", k), "wide")
                for t, (t0, m) in enumerate(TT):
                    i = nc.tensor.transpose(flat(b, 640)[0:m, t * P:(t + 1) * P], xT[:, k, t0:t0 + m], ident)
                i.then_inc(sem("y_turned"), up("y_turned", k))

        @block.sync
        def _(sp):

            n_ld = [0]

            sp.dma_start(cst[:, 0:K_CAUS], I["consts"][:, 0:K_CAUS])\
                .then_inc(sem("const_loaded"), up("const_loaded", 0, by=16))
            xp, xs = I["x_prompt"], I["x_sample"]
            sp.dma_start(xin[:, 0:4, :], xp.rearrange("a (t p) d -> p (a t) d", p=P))\
                .then_inc(sem("x_loaded"), up("x_loaded", 0, by=16))
            sp.dma_start(xin[0:NS, 4, :], xs.rearrange("b t d -> (b t) d"))\
                .then_inc(sem("x_loaded"), up("x_loaded", 0, by=16))
            sp.dma_start(cst[:, K_CAUS:], I["consts"][:, K_CAUS:])\
                .then_inc(sem("tables_loaded"), up("tables_loaded", 0, by=16))

            def small(l):
                if l:
                    sp.wait_ge(sem("summed_values"), after("summed_values", ((l - 1, "pair", 1, 2), 0)))
                    sp.wait_ge(sem("summed_values"), after("summed_values", (l - 1, todo[-1], 1)))
                sp.dma_start(wvg, I["w_in"][l][:, C_KVW + P:NIN].rearrange("(k p) c -> p k c", p=P))\
                    .then_inc(sem("wvg_loaded"), up("wvg_loaded", l, by=16))
                sp.wait_ge(sem("wbd_zeroed"), after("wbd_zeroed", l))
                for v, name in enumerate(("rg_wa", "rg_wx")):
                    for e in range(2):
                        src = I[name][l].rearrange("(j e) c d -> e c j d", e=2)[e]
                        sp.dma_start(wbd[64 * e:64 * e + 64, v, :, 64 * e:64 * e + 64], src)\
                            .then_inc(sem("wbd_loaded"), up("wbd_loaded", l, by=16))
                if l:
                    sp.wait_ge(sem("summed_values"), after("summed_values", ((l - 1, "pair", 1, 2), 0)))
                for v, name in enumerate(("cmpk", "cmpv")):
                    sp.dma_start(w1[:, v], I[name + "_w1"][l].rearrange("(s e) d f -> (e d) s f", e=2))\
                        .then_inc(sem("w1_loaded"), up("w1_loaded", l, by=16))
                    sp.dma_start(w2[:, v, :], I[name + "_w2"][l])\
                        .then_inc(sem("w1_loaded"), up("w1_loaded", l, by=16))

            def params(l):
                if l:
                    sp.wait_ge(sem("projected"), after("projected", (l - 1, "out", KT - 1)))
                r = lambda name: I[name][l]
                row = [0]

                def put(src, n, tile):
                    sp.dma_start(stage(tile)[row[0]:row[0] + n, :], src)\
                        .then_inc(sem("params_loaded"), up("params_loaded", l, by=16))
                    row[0] += n

                for name in ("norm_mix_pre", "norm_mix_post", "norm_ffn_pre", "norm_ffn_post"):
                    put(r(name).rearrange("(k p) -> k p", p=P), KT, 0)
                put(r("rg_conv_w").rearrange("w (k p) -> (w k) p", p=P), 16, 0)
                for name in ("rg_conv_b", "rg_ba", "rg_bx", "rg_lambda"):
                    put(r(name).rearrange("(k p) -> k p", p=P), RJ, 0)
                for name in ("cmpk_b1", "cmpv_b1"):
                    put(r(name).rearrange("(k p) -> k p", p=P), 1, 0)
                for name in ("cmpk_pe", "cmpv_pe"):
                    put(r(name).rearrange("(s e) d -> s (e d)", e=2), 16, 0)
                row[0] = 0
                put(r("ffn_conv_w").rearrange("w (k p) -> (w k) p", p=P), 72, 1)
                put(r("ffn_conv_b").rearrange("(k p) -> k p", p=P), FT, 1)
                row[0] = 0
                put(r("state_rg_h").rearrange("b (k p) -> (b k) p", p=P), 32, 2)
                put(r("state_rg_conv").rearrange("b w (k p) -> (b w k) p", p=P), 96, 2)
                fs = r("state_ffn_conv").rearrange("b w (k p) -> (b w k) p", p=P)
                for t in range(3):
                    sp.dma_start(stage(3 + t), fs[t * P:(t + 1) * P])\
                        .then_inc(sem("params_loaded"), up("params_loaded", l, by=16))

            def new_rows(l):
                for n, out in (("s", "slc"), ("w", "win"), ("c", "cmp")):
                    if n != "c":
                        sp.wait_ge(sem("k_roped"), after("k_roped", (l, n)))
                    sp.wait_ge(sem("kv_copied"), after("kv_copied", (l, n)))
                    kv4 = lambda ap: ap.rearrange("(t p) v h d -> p t (v h d)", p=P)
                    name = f"kv_stored_{n}"
                    sp.dma_start(kv4(O["p_" + out][l, 0]), kvt[n][:, 0:4, :])\
                        .then_inc(sem(name), up(name, l, by=16))
                    if n == "w":
                        for b in range(DB):
                            sp.dma_start(O["s_win"][l, b, WIN - DT:WIN].rearrange("t v h d -> t (v h d)"), kvt[n][b * DT:(b + 1) * DT, 4, :])\
                                .then_inc(sem(name), up(name, l, by=16))
                        for b in range(DB):
                            sp.dma_start(O["s_win"][l, b, 0:WIN - DT].rearrange("(n t) v h d -> n (t v h d)", t=4), I["cache_win_kv"][l, b, DT:WIN].rearrange("(n t) v h d -> n (t v h d)", t=4))\
                                .then_inc(sem("window_moved"), up("window_moved", 0, by=16))
                    else:
                        sp.dma_start(O["s_" + out][l].rearrange("b t v h d -> (b t) (v h d)"), kvt[n][0:NS, 4, :])\
                            .then_inc(sem(name), up(name, l, by=16))

            params(0)
            for n, (l, kind, x) in enumerate(units):
                if (kind, x) == ("xr", 1):
                    small(l)
                if (kind, x) == ("out", 0):
                    new_rows(l)
                if l < DEPTH - 1 and n == unit_no[l, "out", KT - 1] + NW:
                    params(l + 1)
                if n >= NW:
                    for s, n_ in freed(("w", n - NW)):
                        sp.wait_ge(s, n_)
                w, name = wv(n), f"w_loaded{n % NW}"
                win = I["w_in"][l].rearrange("(k p) c -> p k c", p=P)
                if kind in ("xr", "gate", "kv"):
                    c = {"xr": 0, "gate": C_GATE}.get(kind)
                    c = c + x * P if c is not None else {"c": C_KVC, "s": C_KVS, "w": C_KVW}[x[0]] + int(x[1]) * P
                    sp.dma_start(w, win[:, :, c:c + P])\
                        .then_inc(sem(name), up(name, n, by=16))
                elif kind == "q":
                    for h in range(2):
                        c = C_Q + h * 256 + x * HD
                        sp.dma_start(w[:, :, h * HD:(h + 1) * HD], win[:, :, c:c + HD])\
                            .then_inc(sem(name), up(name, n, by=16))
                elif kind == "out":
                    c = slice(x * P, (x + 1) * P)
                    sp.dma_start(w[:, 0:4, :], I["w_out"][l][0:DR, c].rearrange("(k p) c -> p k c", p=P))\
                        .then_inc(sem(name), up(name, n, by=16))
                    for h in range(2):
                        src = I["w_out"][l][DR + h * 256:DR + (h + 1) * 256, c].rearrange("(g d) c -> d g c", d=HD)
                        sp.dma_start(w[h * HD:(h + 1) * HD, 4:8, :], src)\
                            .then_inc(sem(name), up(name, n, by=16))
                elif kind in ("g", "u"):
                    c = (DF if kind == "g" else 0) + x * P
                    sp.dma_start(w, I["ffn_w_in"][l].rearrange("(k p) c -> p k c", p=P)[:, :, c:c + P])\
                        .then_inc(sem(name), up(name, n, by=16))
                else:
                    r, j = x
                    src = I["ffn_w_down"][l][r * D:(r + 1) * D, j * P:(j + 1) * P]
                    sp.dma_start(w, src.rearrange("(k p) c -> p k c", p=P))\
                        .then_inc(sem(name), up(name, n, by=16))
            for n in "swc":
                sp.wait_ge(sem("kv_stored_" + n), after("kv_stored_" + n, DEPTH - 1))
            sp.wait_ge(sem("window_moved"), after("window_moved", 0))

        @block.gpsimd
        def _(po):

            def p(ins):
                ins.then_inc(sem("pool_step"), up("pool_step"))
                po.wait_ge(sem("pool_step"), now("pool_step"))

            nc.gpsimd.memset(ones[:, :], 1.0).then_inc(sem("ones_set"), up("ones_set", 0))
            po.wait_ge(sem("ones_set"), now("ones_set"))
            for c in range(CPP):
                po.dma_start(idi[c:P:CPP, 0:DB], I["page_table"].rearrange("b j -> j b"),
                                      allow_slow_non_contiguous=True).then_inc(sem("pages_loaded"), up("pages_loaded", 0, by=16))
            nload, xsn = [0], [0]

            def cache(upto):
                while nload[0] <= upto:
                    n = nload[0]
                    nload[0] += 1
                    l, kind, x = loads[n]
                    if n >= NA:
                        for s, n_ in freed(("a", n - NA)):
                            po.wait_ge(s, n_)
                    name = f"a_loaded{n % NA}"
                    if kind in ("cmp", "slc"):
                        po.wait_ge(sem("index_ready"), after("index_ready", 0))
                        pool = I["cache_cmp_kv" if kind == "cmp" else "cache_slc_kv"]
                        src = pool.rearrange("l n (c s) v h d -> (l n c) (s v h d)", c=CPP)
                        ixc = idi[:, (1 + l) * DB + x:(1 + l) * DB + x + 1].bitcast(U32)
                        po.indirect_dma_start(av(n), None, src, bass.IndirectOffsetOnAxis(ap=ixc, axis=0)).then_inc(sem(name), up(name, n, by=16))
                    elif kind == "cmpp":
                        po.wait_ge(sem("kv_stored_c"), after("kv_stored_c", l))
                        src = O["p_cmp"][l, 0].rearrange("(n s) v h d -> n (s v h d)", s=STRIDE)
                        po.dma_start(av(n)[0:NCP, :], src).then_inc(sem(name), up(name, n, by=16))
                    else:
                        src = I["cache_win_kv"][l, 4 * x:4 * x + 4].rearrange("b (p s) v h d -> p b (s v h d)", s=4)
                        po.dma_start(av(n).rearrange("p (b c) -> p b c", b=4), src).then_inc(sem(name), up(name, n, by=16))

            A0 = len(loads) // DEPTH
            for l in range(DEPTH):
                if l:
                    po.wait_ge(sem("projected"), after("projected", (l - 1, "rg", RJ - 1, 1)))
                    po.wait_ge(sem("comb_ready"), after("comb_ready", (l - 1, 1)))
                    po.wait_ge(sem("summed_values"), after("summed_values", ((l - 1, "pair", 1, 2), 0)))
                nc.gpsimd.memset(ov2[:, :], 0.0).then_inc(sem("wbd_zeroed"), up("wbd_zeroed", l))
                po.wait_ge(sem("wbd_zeroed"), now("wbd_zeroed"))
                if l == 0:
                    cache(2)
                po.wait_ge(sem("projected"), after("projected", (l, "rg", RJ - 1, 1)))
                nc.gpsimd.memset(ov2[:, :], 0.0).then_inc(sem("ov2_zeroed"), up("ov2_zeroed", l))
                po.wait_ge(sem("ov2_zeroed"), now("ov2_zeroed"))
                po.wait_ge(sem("projected"), after("projected", (l, "kv", "c1")))
                for u in compressed_units(l):
                    n = load_no[u]
                    cache(n)
                    po.wait_ge(sem(f"a_loaded{n % NA}"), after(f"a_loaded{n % NA}", n))
                    for vv in range(2):
                        for s4 in range(3):
                            for s, n_ in freed(("xs", xsn[0] - 2)):
                                po.wait_ge(s, n_)
                            for e in range(2):
                                dst, src = rearranged(u, vv, s4, e, xsn[0])
                                nc.gpsimd.tensor_copy(dst, src).then_inc(sem("rearranged" if e else "pool_step"), up("rearranged" if e else "pool_step", (u, vv, s4) if e else None, frees=[("a", n)] if e and vv and s4 == 2 else []))
                                po.wait_ge(sem("rearranged" if e else "pool_step"), now("rearranged" if e else "pool_step"))
                            xsn[0] += 1
                        xsn[0] += 1
                    cache(min(n + NA, l * A0 + A0 - 1))
                cache(l * A0 + A0 - 1)
                if l < DEPTH - 1:
                    cache((l + 1) * A0 + 2)
                for k in range(1, KT, 2):
                    po.wait_ge(sem("m_scaled"), after("m_scaled", (l, 1, k)))
                    nc.gpsimd.tensor_tensor(xT[:, k, :], xT[:, k, :], mT[:, k, :], ALU.add).then_inc(sem("x_added_p"), up("x_added_p", (l, 1, k)))
                    po.wait_ge(sem("x_added_p"), now("x_added_p"))
                fs = par[:, P_FS:P_FS + 384].rearrange("p (b w f) -> p b w f", b=DB, w=2)
                fo = fcb.rearrange("p (r f) -> p r f", f=FT)
                for f in range(FT):
                    gp = gpad[f % 2]
                    if f < 2:
                        p(nc.gpsimd.memset(gp[:, 0:2], 0.0))
                    else:
                        po.wait_ge(sem("conv_done"), after("conv_done", (l, "f", f - 2)))
                    gps = gp[:, 2 + SEQ:].rearrange("p (b c) -> p b c", b=DB)
                    nc.gpsimd.tensor_copy(gps[:, :, 0:2], fs[:, :, :, f]).then_inc(sem("prefix_copied"), up("prefix_copied", (l, f)))
                    po.wait_ge(sem("prefix_copied"), now("prefix_copied"))
                    po.wait_ge(sem("g_copied"), after("g_copied", (l, f)))
                    p(nc.gpsimd.tensor_copy(fo[:, 0:2, f], gp[:, SEQ:SEQ + 2]))
                    nc.gpsimd.tensor_copy(fo[:, 2:18, f].rearrange("p (b w) -> p b w", b=DB), gps[:, :, 4:6]).then_inc(sem("states_ready"), up("states_ready", (l, f if f < FT - 1 else "ffn"), frees=[("gpad", l, f)]))
                    po.wait_ge(sem("states_ready"), now("states_ready"))
                for k in range(1, KT, 2):
                    po.wait_ge(sem("m_scaled"), after("m_scaled", (l, 3, k)))
                    nc.gpsimd.tensor_tensor(xT[:, k, :], xT[:, k, :], mT[:, k, :], ALU.add).then_inc(sem("x_added_p"), up("x_added_p", (l, 3, k)))
                    po.wait_ge(sem("x_added_p"), now("x_added_p"))
                for i, (name, r0, r1) in enumerate(OUTT):
                    po.wait_ge(sem("states_copied"), after("states_copied", (l, i)))
                    src = st_out[0:r1 - r0, i * P:(i + 1) * P]
                    if i == 0:
                        po.dma_start(O["p_rgc"][l].rearrange("b w (k p) -> (b w k) p", p=P), src[0:12])\
                            .then_inc(sem("states_stored"), up("states_stored", l, by=16))
                        po.dma_start(O["p_rgh"][l].rearrange("b (k p) -> (b k) p", p=P), src[12:16])\
                            .then_inc(sem("states_stored"), up("states_stored", l, by=16))
                        po.dma_start(O["s_rgh"][l].rearrange("b (k p) -> (b k) p", p=P), src[16:48])\
                            .then_inc(sem("states_stored"), up("states_stored", l, by=16))
                    elif i == 1:
                        po.dma_start(O["s_rgc"][l].rearrange("b w (k p) -> (b w k) p", p=P), src)\
                            .then_inc(sem("states_stored"), up("states_stored", l, by=16))
                    elif i == 2:
                        po.dma_start(O["p_ffc"][l].rearrange("b w (k p) -> (b w k) p", p=P), src)\
                            .then_inc(sem("states_stored"), up("states_stored", l, by=16))
                    else:
                        dst = O["s_ffc"][l].rearrange("b w (k p) -> (b w k) p", p=P)
                        po.dma_start(dst[(i - 3) * P:(i - 2) * P], src)\
                            .then_inc(sem("states_stored"), up("states_stored", l, by=16))
            for k in (3, 7):
                po.wait_ge(sem("y_copied_v"), after("y_copied_v", k - 1))
                po.wait_ge(sem("y_copied_a"), after("y_copied_a", k))
                c = slice((k - 3) * P, (k + 1) * P)
                po.dma_start(O["y_p"][0].rearrange("(t p) d -> p t d", p=P)[:, :, c], yout[:, :, c])\
                    .then_inc(sem("y_stored"), up("y_stored", 0, by=16))
                po.dma_start(O["y_s"].rearrange("b t d -> (b t) d")[:, c], youts[:, c])\
                    .then_inc(sem("y_stored"), up("y_stored", 0, by=16))
            po.wait_ge(sem("y_stored"), after("y_stored", 0))
            po.wait_ge(sem("states_stored"), after("states_stored", DEPTH - 1))

        @block.scalar
        def _(ac):

            def a(ins):
                ins.then_inc(sem("scalar_step"), up("scalar_step"))
                ac.wait_ge(sem("scalar_step"), now("scalar_step"))

            act = nc.scalar.activation
            psk = lambda key: S.bank_of[key]

            def sqrt_table():
                a(act(sm[:, 151:152], sm[:, 150:151], ACT.Sqrt))

            def squares(l, n, src, sq, ready):
                sqrt_table()
                for k in range(KT):
                    ready(k)
                    act(sq[:, k, :], src[:, k, :], ACT.Square).then_inc(sem("squared"), up("squared", (l, n, k)))
                    ac.wait_ge(sem("squared"), now("squared"))

            def root(l, n):
                b = psk((l, n, "rstd"))
                ac.wait_ge(sem("summed"), after("summed", (l, n)))
                act(pair(b), pair(b), ACT.Sqrt, scale=1.0 / D, bias=sm[:, 150:151]).then_inc(sem("rms_ready"), up("rms_ready", (l, n)))
                ac.wait_ge(sem("rms_ready"), now("rms_ready"))

            for k in range(KT):
                ac.wait_ge(sem("x_turned"), after("x_turned", k))
                b = psk(("x", k))
                act(xT[:, k, :], flat(b, T), ACT.Copy).then_inc(sem("x_copied"), up("x_copied", k, frees=[("psum", ("x", k))]))
                ac.wait_ge(sem("x_copied"), now("x_copied"))

            def compress(u, prev):
                nch = NCH if u[1] == "cmp" else NCP
                for v in range(2):
                    for s4 in (1, 3):
                        ac.wait_ge(sem("turned"), after("turned", (u, "xt", v, s4)))
                        sl = S.slot_of[u, "xt", v, s4]
                        for s, n_ in freed(("ts", sl - NTS)):
                            ac.wait_ge(s, n_)
                        b = psk((u, "xt", v, s4))
                        act(tv(sl)[:, 0:4 * nch], pst[:, b, 0:4 * nch], ACT.Copy).then_inc(sem("copied_a"), up("copied_a", (u, "xt", v, s4), frees=[("psum", (u, "xt", v, s4))]))
                        ac.wait_ge(sem("copied_a"), now("copied_a"))
                    ac.wait_ge(sem("compressed"), after("compressed", (u, v, 3)))
                    ac.wait_ge(sem("b1_ready"), after("b1_ready", u[0]))
                    b = psk((u, "hid", v))
                    if prev:
                        ac.wait_ge(sem("compressed2"), after("compressed2", (prev, v)))
                    if u[1] == "cmp":
                        act(hid_of(u, v), pst[:, b, 0:2 * (nch - 1)].rearrange("p (h c) -> p h c", h=2),
                              ACT.Gelu_apprx_tanh, bias=sm[:, 140 + v:141 + v]).then_inc(sem("hidden"), up("hidden", (u, v), frees=[("psum", (u, "hid", v))]))
                        ac.wait_ge(sem("hidden"), now("hidden"))
                    else:
                        hv = hid_of(u, v)
                        a(act(hv[:, :, 31:32], cst[:, K_ROT:K_ROT + 2].rearrange("p (h c) -> p h c", h=2), ACT.Copy, scale=0.0))
                        act(hv[:, :, 0:31], pst[:, b, 0:62].rearrange("p (h c) -> p h c", h=2),
                              ACT.Gelu_apprx_tanh, bias=sm[:, 140 + v:141 + v]).then_inc(sem("hidden"), up("hidden", (u, v), frees=[("psum", (u, "hid", v))]))
                        ac.wait_ge(sem("hidden"), now("hidden"))

            for l in range(DEPTH):
                if l == 0:
                    ac.wait_ge(sem("eps_set"), after("eps_set", 0))
                    squares(l, 0, xT, actT, lambda k: None)
                else:
                    squares(l, 0, xT, actT, lambda k: ac.wait_ge(sem("x_added_p" if k % 2 else "x_added_v"), after("x_added_p" if k % 2 else "x_added_v", (l - 1, 3, k))))
                root(l, 0)
                ac.wait_ge(sem("lam_abs"), after("lam_abs", l))
                a(act(sm[:, 108:112], sm[:, 104:108], ACT.Exp))
                act(sm[:, 112:116], sm[:, 108:112], ACT.Ln, bias=1.0).then_inc(sem("lam_exp"), up("lam_exp", l))
                ac.wait_ge(sem("lam_exp"), now("lam_exp"))
                for j in range(RJ):
                    ac.wait_ge(sem("projected"), after("projected", (l, "xr", j)))
                    b = psk((l, "xr", j))
                    if j == 0:
                        ac.wait_ge(sem("h_ready"), after("h_ready", (l, 0, KT - 1, 1)))
                    else:
                        ac.wait_ge(sem("y_ready"), after("y_ready", (l, j - 1)))
                    a(act(xrp[:, 3:3 + TH], pst[:, b, 0:TH], ACT.Copy))
                    a(act(xrp[:, 3 + TH:3 + SEQ], pst[:, b + 1, 0:SEQ - TH], ACT.Copy))
                    xs = xrp[:, 3 + SEQ:].rearrange("p (b c) -> p b c", b=DB)
                    act(xs[:, :, 3:7], pst[:, b + 1, SEQ - TH:TH].rearrange("p (b c) -> p b c", b=DB), ACT.Copy).then_inc(sem("xr_copied"), up("xr_copied", (l, j), frees=[("psum", (l, "xr", j))]))
                    ac.wait_ge(sem("xr_copied"), now("xr_copied"))
                    ac.wait_ge(sem("projected"), after("projected", (l, "gate", j)))
                    b = psk((l, "gate", j))
                    if l:
                        ac.wait_ge(sem("states_stored"), after("states_stored", l - 1))
                    act(halves(gR), pair(b), ACT.Gelu_apprx_tanh).then_inc(sem("gate_ready"), up("gate_ready", (l, j), frees=[("psum", (l, "gate", j))]))
                    ac.wait_ge(sem("gate_ready"), now("gate_ready"))
                    ac.wait_ge(sem("lambda_ready"), after("lambda_ready", l))
                    ac.wait_ge(sem("projected"), after("projected", (l, "rg", j, 0)))
                    b = psk((l, "rg", j, 0))
                    act(halves(rt), pair(b), ACT.Tanh, scale=0.5, bias=sm[:, 20 + j:21 + j]).then_inc(sem("scalar_step"), up("scalar_step", frees=[("psum", (l, "rg", j, 0))]))
                    ac.wait_ge(sem("scalar_step"), now("scalar_step"))
                    ac.wait_ge(sem("projected"), after("projected", (l, "rg", j, 1)))
                    b = psk((l, "rg", j, 1))
                    act(halves(iR), pair(b), ACT.Tanh, scale=0.5, bias=sm[:, 24 + j:25 + j]).then_inc(sem("i_ready"), up("i_ready", (l, j), frees=[("psum", (l, "rg", j, 1))]))
                    ac.wait_ge(sem("i_ready"), now("i_ready"))
                    act(tR, rt, ACT.Tanh, scale=sm[:, 28 + j:29 + j], bias=sm[:, 28 + j:29 + j]).then_inc(sem("t_ready"), up("t_ready", (l, j)))
                    ac.wait_ge(sem("t_ready"), now("t_ready"))
                    act(aR, rt, ACT.Exp, scale=sm[:, 28 + j:29 + j], bias=sm[:, 28 + j:29 + j]).then_inc(sem("a_ready"), up("a_ready", (l, j)))
                    ac.wait_ge(sem("a_ready"), now("a_ready"))
                    ac.wait_ge(sem("f_ready"), after("f_ready", (l, j)))
                    act(rt, tR, ACT.Sqrt, scale=-0.5).then_inc(sem("s_ready"), up("s_ready", (l, j)))
                    ac.wait_ge(sem("s_ready"), now("s_ready"))
                for g in range(GR):
                    ac.wait_ge(sem("projected"), after("projected", (l, "q", g)))
                    b = psk((l, "q", g))
                    act(halves(qcT[:, g, :]), pair(b), ACT.Copy, scale=HD ** -0.5).then_inc(sem("q_copied"), up("q_copied", (l, g), frees=[("psum", (l, "q", g))]))
                    ac.wait_ge(sem("q_copied"), now("q_copied"))
                for n in ("s1", "w1", "c0", "c1"):
                    ac.wait_ge(sem("projected"), after("projected", (l, "kv", n)))
                    b = psk((l, "kv", n))
                    ac.wait_ge(sem("y_ready"), after("y_ready", (l, RJ - 1)))
                    if n[0] == "c":
                        ac.wait_ge(sem("k_roped"), after("k_roped", (l, "w")))
                    v = int(n[1])
                    dst = kvt[n[0]][:, :, v * P:(v + 1) * P]
                    if n == "w1":
                        x = pst[:, b, 0:3 * WG].rearrange("p (t c) -> p t c", t=3)
                        y = pst[:, b + 1, 0:2 * WG].rearrange("p (t c) -> p t c", t=2)
                        a(act(dst[:, 0:3, :], x[:, :, 0:P], ACT.Copy))
                        a(act(dst[:, 3, :], y[:, 0, 0:P], ACT.Copy))
                        act(dst[0:NS, 4, :], y[0:NS, 1, 0:P], ACT.Copy).then_inc(sem("kv_copied"), up("kv_copied", (l, n[0])))
                        ac.wait_ge(sem("kv_copied"), now("kv_copied"))
                        a(act(gates[:, 0:3, :], x[:, :, P:WG], ACT.Tanh, scale=0.5))
                        a(act(gates[:, 3, :], y[:, 0, P:WG], ACT.Tanh, scale=0.5))
                        act(gates[0:NS, 4, :], y[0:NS, 1, P:WG], ACT.Tanh, scale=0.5).then_inc(sem("gates_tanh"), up("gates_tanh", l, frees=[("psum", (l, "kv", n))]))
                        ac.wait_ge(sem("gates_tanh"), now("gates_tanh"))
                        continue
                    a(act(dst[:, 0:4, :], pst[:, b, :].rearrange("p (t c) -> p t c", t=4), ACT.Copy))
                    act(dst[0:NS, 4, :], pst[0:NS, b + 1, 0:P], ACT.Copy).then_inc(sem("kv_copied"), up("kv_copied", (l, n[0]) if v else None, frees=[("psum", (l, "kv", n))]))
                    ac.wait_ge(sem("kv_copied"), now("kv_copied"))
                for n in "sw":
                    ac.wait_ge(sem("k_turned"), after("k_turned", (l, n)))
                    b = psk((l, "kT", n))
                    act(kT[n], flat(b, T), ACT.Copy).then_inc(sem("kT_copied"), up("kT_copied", (l, n), frees=[("psum", (l, "kT", n))]))
                    ac.wait_ge(sem("kT_copied"), now("kT_copied"))
                us = compressed_units(l)
                for i, u in enumerate(us):
                    compress(u, us[i - 1] if i else (l - 1, "cmp", DB - 1) if l else None)
                    if CMP_PARTS.get(i, ("", 0))[0] != "scores":
                        continue
                    G = CMP_PARTS[i][1]
                    ac.wait_ge(sem("neg_max"), after("neg_max", (l, G, "cs")))
                    if G:
                        ac.wait_ge(sem("turned"), after("turned", (l, 0, "cs")))
                    b = psk((l, G, "Scs"))
                    act(cmp_p, pst[:, b, 0:127], ACT.Exp, bias=sm[:, 40 + G:41 + G], accum_out=sm[:, 42 + G:43 + G]).then_inc(sem("p_exp"), up("p_exp", (l, G, "cs"), frees=[("psum", (l, G, "Scs"))]))
                    ac.wait_ge(sem("p_exp"), now("p_exp"))
                def p_exp(n):
                    u = todo[n]
                    i, br, g = u
                    for h in range(2):
                        m = 2 * n + h
                        if h == 0:
                            ac.wait_ge(sem("neg_max"), after("neg_max", (l, u)))
                        if m >= 4:
                            for s, n_ in freed(("p", l, m - 4)):
                                ac.wait_ge(s, n_)
                        b = psk((l, u, "S")) + h
                        L = (i + 1) * P
                        col = 176 + 16 * (i % 2) + (0 if br == "s" else 8) + g * 2 + h
                        act(p_slot(m)[:, 0:L], pst[:, b, 0:L], ACT.Exp, bias=sm[:, 48 + m % 8:49 + m % 8],
                              accum_out=sm[:, col:col + 1]).then_inc(sem("p_exp"), up("p_exp", (l, u, h), frees=[("psum", (l, u, "S")), ("nm", l, n)]))
                        ac.wait_ge(sem("p_exp"), now("p_exp"))

                def p_copy(n):
                    u = todo[n]
                    sl = S.slot_of[l, u, 1]
                    ac.wait_ge(sem("turned"), after("turned", (l, u, 1)))
                    for s, n_ in freed(("ts", sl - NTS)):
                        ac.wait_ge(s, n_)
                    L = (u[0] + 1) * P
                    b = psk((l, u, "T", 1))
                    act(tv(sl)[:, 0:L], pst[:, b, 0:L], ACT.Copy).then_inc(sem("copied_a"), up("copied_a", (l, u, 1), frees=[("psum", (l, u, "T", 1))]))
                    ac.wait_ge(sem("copied_a"), now("copied_a"))

                def sample_part(part, k, G, e):
                    u = (l, "win", G) if e is None else (l, "pair", G, e)

                    def copy_keys(x, b2, n):
                        n += 40 * l + FIRST_KEY[k]
                        ac.wait_ge(sem("turned"), after("turned", (u, "kt", x, b2)))
                        if n >= NKS:
                            for s, n_ in freed(("ks", n - NKS)):
                                ac.wait_ge(s, n_)
                        act(key_slot(n), bank(psk((u, "kt", x, b2))), ACT.Copy).then_inc(sem("copied_a"), up("copied_a", (u, "kt", x, b2), frees=[("psum", (u, "kt", x, b2))]))
                        ac.wait_ge(sem("copied_a"), now("copied_a"))

                    if e is None and part in ("keys0", "keys2"):
                        x = 1 if part == "keys0" else 3
                        copy_keys(x, 0, x)
                    elif e is not None and part in ("keys0", "keys1", "keys2", "keys3"):
                        x = int(part[4])
                        copy_keys(x, 1, 2 * x + 1)
                    elif part == "turn" and e is not None:
                        for s, n_ in freed(("pt", l, k - 1)):
                            ac.wait_ge(s, n_)
                        ac.wait_ge(sem("turned"), after("turned", (u, "pt", 1)))
                        act(probs[:, 512:1024], bank(psk((u, "pt", 1))), ACT.Copy).then_inc(sem("copied_a"), up("copied_a", (u, "pt", 1), frees=[("psum", (u, "pt", 1))]))
                        ac.wait_ge(sem("copied_a"), now("copied_a"))
                    elif part == "exp":
                        ac.wait_ge(sem("neg_max"), after("neg_max", u))
                        if e is None:
                            a(act(sW[:, 0:512], sW[:, 0:512], ACT.Exp, bias=sm[:, 88:89], accum_out=sm[:, 90:91]))
                            act(sW[:, 512:544], sW[:, 512:544], ACT.Exp, bias=sm[:, 88:89], accum_out=sm[:, 91:92]).then_inc(sem("p_exp"), up("p_exp", u))
                            ac.wait_ge(sem("p_exp"), now("p_exp"))
                        else:
                            r = slice(32 * e, 32 * e + 64)
                            act(sQ[r, :], sQ[r, :], ACT.Exp, bias=sm[r, 89:90], accum_out=sm[r, 92:93]).then_inc(sem("p_exp"), up("p_exp", u))
                            ac.wait_ge(sem("p_exp"), now("p_exp"))

                ac.wait_ge(sem("kv_stored_c"), after("kv_stored_c", l))
                for who_, what, n in plan:
                    if who_ == "sample":
                        if what == "keys0":
                            ac.wait_ge(sem("summed_values"), after("summed_values", (l, 1, "cs")))
                        sample_part(what, *n)
                    elif (who_, what) == ("tile", "exp"):
                        ac.wait_ge(sem("cmp_shifted"), after("cmp_shifted", (l, n)))
                        act(pc_p, pc_s, ACT.Exp).then_inc(sem("cmp_exp"), up("cmp_exp", (l, n)))
                        ac.wait_ge(sem("cmp_exp"), now("cmp_exp"))
                    elif who_ != "prompt":
                        continue
                    elif what == "scores":
                        if n % 8 == 0 and n >= 16:
                            ac.wait_ge(sem("l_read"), after("l_read", (l, todo[n][0] - 2)))
                        p_exp(n)
                    elif what == "turn":
                        p_copy(n)
                ac.wait_ge(sem("kv_stored_s"), after("kv_stored_s", l))
                ac.wait_ge(sem("kv_stored_w"), after("kv_stored_w", l))
                sqrt_table()
                for j in range(KT):
                    ac.wait_ge(sem("projected"), after("projected", (l, "out", j)))
                    b = psk((l, "out", j))
                    ac.wait_ge(sem("summed_values"), after("summed_values", ((l, "pair", 1, 2), 0)))
                    a(act(halves(mT[:, j, :]), pair(b), ACT.Copy))
                    act(halves(actT[:, j, :]), pair(b), ACT.Square).then_inc(sem("squared"), up("squared", (l, 1, j), frees=[("psum", (l, "out", j))]))
                    ac.wait_ge(sem("squared"), now("squared"))
                root(l, 1)
                squares(l, 2, xT, actT, lambda k: ac.wait_ge(sem("x_added_p" if k % 2 else "x_added_v"), after("x_added_p" if k % 2 else "x_added_v", (l, 1, k))))
                root(l, 2)
                for r in range(RND):
                    for f in range(r * FR, (r + 1) * FR):
                        ac.wait_ge(sem("projected"), after("projected", (l, "g", f)))
                        b = psk((l, "g", f))
                        gp = gpad[f % 2]
                        if f >= 2:
                            ac.wait_ge(sem("conv_done"), after("conv_done", (l, "f", f - 2)))
                            for s, n_ in freed(("gpad", l, f - 2)):
                                ac.wait_ge(s, n_)
                        a(act(gp[:, 2:2 + TH], pst[:, b, 0:TH], ACT.Copy))
                        a(act(gp[:, 2 + TH:2 + SEQ], pst[:, b + 1, 0:SEQ - TH], ACT.Copy))
                        gps = gp[:, 2 + SEQ:].rearrange("p (b c) -> p b c", b=DB)
                        act(gps[:, :, 2:6], pst[:, b + 1, SEQ - TH:TH].rearrange("p (b c) -> p b c", b=DB), ACT.Copy).then_inc(sem("g_copied"), up("g_copied", (l, f), frees=[("psum", (l, "g", f))]))
                        ac.wait_ge(sem("g_copied"), now("g_copied"))
                        ac.wait_ge(sem("conv_done"), after("conv_done", (l, "f", f)))
                        if f:
                            ac.wait_ge(sem("act_ready"), after("act_ready", (l, f - 1)))
                        a(act(gF[:, 0:SEQ], cF[:, 0:SEQ], ACT.Gelu_apprx_tanh))
                        act(gF[:, SEQ:T].rearrange("p (b c) -> p b c", b=DB), per6, ACT.Gelu_apprx_tanh).then_inc(sem("gelu_done"), up("gelu_done", (l, f)))
                        ac.wait_ge(sem("gelu_done"), now("gelu_done"))
                    for j in range(KT):
                        ac.wait_ge(sem("projected"), after("projected", (l, "down", r, j)))
                        b = psk((l, "down", r, j))
                        if r == 0:
                            act(halves(mT[:, j, :]), pair(b), ACT.Copy).then_inc(sem("m_copied"), up("m_copied", (l, j), frees=[("psum", (l, "down", r, j))]))
                            ac.wait_ge(sem("m_copied"), now("m_copied"))
                        if r == RND - 1:
                            if j == 0:
                                sqrt_table()
                            ac.wait_ge(sem("m_summed"), after("m_summed", (l, r, j)))
                            act(hT[:, j, :], mT[:, j, :], ACT.Square).then_inc(sem("squared"), up("squared", (l, 3, j)))
                            ac.wait_ge(sem("squared"), now("squared"))
                root(l, 3)
                for i, (name, r0, r1) in enumerate(OUTT):
                    ac.wait_ge(sem("states_turned"), after("states_turned", (l, i)))
                    b = psk((l, "st", i))
                    act(st_out[0:r1 - r0, i * P:(i + 1) * P], pst[0:r1 - r0, b, 0:P], ACT.Copy).then_inc(sem("states_copied"), up("states_copied", (l, i), frees=[("psum", (l, "st", i))]))
                    ac.wait_ge(sem("states_copied"), now("states_copied"))
            ac.wait_ge(sem("x_added_v"), after("x_added_v", (DEPTH - 1, 3, KT - 2)))
            for k in range(1, KT, 2):
                ac.wait_ge(sem("y_turned"), after("y_turned", k))
                b = psk(("y", k))
                a(act(yout[:, :, k * P:(k + 1) * P], bank(b).rearrange("p (t c) -> p t c", t=4), ACT.Copy))
                act(youts[:, k * P:(k + 1) * P], pst[0:NS, b + 1, 0:P], ACT.Copy).then_inc(sem("y_copied_a"), up("y_copied_a", k, frees=[("psum", ("y", k))]))
                ac.wait_ge(sem("y_copied_a"), now("y_copied_a"))

        @block.vector
        def _(ve):

            def v(ins):
                ins.then_inc(sem("vector_step"), up("vector_step"))
                ve.wait_ge(sem("vector_step"), now("vector_step"))

            V = nc.vector
            tt, tsc, stt, cp = V.tensor_tensor, V.tensor_scalar, V.scalar_tensor_tensor, V.tensor_copy
            psk = lambda key: S.bank_of[key]

            def copy_ts(key, cols, rows=P):
                ve.wait_ge(sem("turned"), after("turned", key))
                sl = S.slot_of[key]
                for s, n_ in freed(("ts", sl - NTS)):
                    ve.wait_ge(s, n_)
                b = S.bank_of[S.bank_key[key]]
                cp(tv(sl)[0:rows, 0:cols], pst[0:rows, b, 0:cols]).then_inc(sem("copied_v"), up("copied_v", key, frees=[("psum", S.bank_key[key])]))
                ve.wait_ge(sem("copied_v"), now("copied_v"))

            def masked(u, x, r, G):
                ve.wait_ge(sem("scored"), after("scored", (u, x + 1, 1)))
                b = S.bank_of[u, "S", x]
                y = lambda ap: ap.rearrange("p (s n c) -> p s n c", n=32, c=4)
                m = mb(G)[r, 0:32].unsqueeze(1).unsqueeze(3).broadcast_to([64, 8, 32, 4])
                tt(y(sQ[r, x * 512:(x + 2) * 512]), y(pst[r, b:b + 2, :].rearrange("p b c -> p (b c)")), m, ALU.add).then_inc(sem("vector_step"), up("vector_step", frees=[("psum", (u, "S", x))]))
                ve.wait_ge(sem("vector_step"), now("vector_step"))

            def norm(l, n):
                ve.wait_ge(sem("rms_ready"), after("rms_ready", (l, n)))
                b = psk((l, n, "rstd"))
                v(V.reciprocal(pair(b), pair(b)))

            def pre(l, n, gain):
                ve.wait_ge(sem("rms_ready"), after("rms_ready", (l, n)))
                b = psk((l, n, "rstd"))
                for h in range(2):
                    x = slice(h * TH, (h + 1) * TH)
                    v(V.reciprocal(pst[:, b + h, 0:TH], pst[:, b + h, 0:TH]))
                    for k in range(KT):
                        stt(hT[:, k, x], xT[:, k, x], par[:, gain + k:gain + k + 1], pst[:, b + h, 0:TH], ALU.mult, ALU.mult).then_inc(sem("h_ready"), up("h_ready", (l, n, k, h), frees=[("psum", (l, n, "rstd"))]))
                        ve.wait_ge(sem("h_ready"), now("h_ready"))

            def post(l, n, gain):
                norm(l, n)
                b = psk((l, n, "rstd"))
                for k in range(KT):
                    stt(halves(mT[:, k, :]), halves(mT[:, k, :]), par[:, gain + k:gain + k + 1], pair(b), ALU.mult, ALU.mult).then_inc(sem("m_scaled"), up("m_scaled", (l, n, k), frees=[("psum", (l, n, "rstd"))]))
                    ve.wait_ge(sem("m_scaled"), now("m_scaled"))
                    if k % 2 == 0:
                        tt(xT[:, k, :], xT[:, k, :], mT[:, k, :], ALU.add).then_inc(sem("x_added_v"), up("x_added_v", (l, n, k)))
                        ve.wait_ge(sem("x_added_v"), now("x_added_v"))

            v(V.memset(sm[:, :], 0.0))
            V.memset(sm[:, 150:151], EPS).then_inc(sem("eps_set"), up("eps_set", 0))
            ve.wait_ge(sem("eps_set"), now("eps_set"))
            ve.wait_ge(sem("pages_loaded"), after("pages_loaded", 0))
            ve.wait_ge(sem("const_loaded"), after("const_loaded", 0))
            v(cp(idx[:, 0:DB], idi[:, 0:DB]))
            v(tsc(idx[:, DB:2 * DB], idx[:, 0:DB], float(CPP), cst[:, K_CH:K_CH + 1], ALU.mult, ALU.add))

            for l in range(DEPTH):
                v(tsc(idx[:, 2 * DB:3 * DB], idx[:, DB:2 * DB], float(l * NPOOL * CPP), None, ALU.add))
                cp(idi[:, (1 + l) * DB:(2 + l) * DB], idx[:, 2 * DB:3 * DB]).then_inc(sem("index_ready"), up("index_ready", 0))
                ve.wait_ge(sem("index_ready"), now("index_ready"))
            for l in range(DEPTH):
                offs = [0, 98, 194, 322, 450, 578, 706]

                def copy_params(tiles):
                    for i in tiles:
                        ve.wait_ge(sem("params_turned"), after("params_turned", (l, i)))
                        b = psk((l, "par", i))
                        cp(par[:, offs[i]:offs[i + 1]], pst[:, b, 0:offs[i + 1] - offs[i]]).then_inc(sem("params_ready"), up("params_ready", (l, i), frees=[("psum", (l, "par", i))]))
                        ve.wait_ge(sem("params_ready"), now("params_ready"))

                copy_params(range(4))
                pre(l, 0, P_NORM)
                v(tsc(sm[:, 20:28], par[:, P_BA:P_BA + 8], 0.5, None, ALU.mult))
                lam = par[:, P_LAM:P_LAM + 4]
                v(tsc(sm[:, 100:104], lam, -1.0, None, ALU.mult))
                tt(sm[:, 104:108], lam, sm[:, 100:104], ALU.min).then_inc(sem("lam_abs"), up("lam_abs", l))
                ve.wait_ge(sem("lam_abs"), now("lam_abs"))
                ve.wait_ge(sem("lam_exp"), after("lam_exp", l))
                y, w = sm[:, 108:112], sm[:, 112:116]
                v(tsc(sm[:, 116:120], y, 1.0, None, ALU.add))
                v(tsc(sm[:, 120:124], sm[:, 116:120], -1.0, None, ALU.add))
                v(tsc(sm[:, 124:128], sm[:, 120:124], 1e-30, None, ALU.max))
                v(V.reciprocal(sm[:, 128:132], sm[:, 124:128]))
                v(tt(sm[:, 132:136], w, y, ALU.mult))
                v(tt(sm[:, 132:136], sm[:, 132:136], sm[:, 128:132], ALU.mult))
                v(stt(sm[:, 120:124], sm[:, 120:124], 0.0, y, ALU.is_equal, ALU.mult))
                v(tt(sm[:, 132:136], sm[:, 132:136], sm[:, 120:124], ALU.add))
                v(tsc(sm[:, 116:120], lam, 0.0, None, ALU.min))
                v(tt(sm[:, 116:120], sm[:, 116:120], sm[:, 132:136], ALU.subtract))
                tsc(sm[:, 28:32], sm[:, 116:120], 4.0, None, ALU.mult).then_inc(sem("lambda_ready"), up("lambda_ready", l))
                ve.wait_ge(sem("lambda_ready"), now("lambda_ready"))
                rc = par[:, P_RC:P_RC + 96].rearrange("p (b w j) -> p b w j", b=DB, w=3)
                h0 = par[:, P_H0:P_H0 + 32].rearrange("p (b j) -> p b j", b=DB)
                for j in range(RJ):
                    xs = xrp[:, 3 + SEQ:].rearrange("p (b c) -> p b c", b=DB)
                    v(V.memset(xrp[:, 0:3], 0.0))
                    v(cp(xs[:, :, 0:3], rc[:, :, :, j]))
                    ve.wait_ge(sem("xr_copied"), after("xr_copied", (l, j)))
                    cw = lambda k: par[:, P_RCW + 4 * k + j:P_RCW + 4 * k + j + 1]
                    v(tsc(cR, xrp[:, 0:568], cw(0), par[:, P_RCB + j:P_RCB + j + 1], ALU.mult, ALU.add))
                    v(stt(cR, xrp[:, 1:569], cw(1), cR, ALU.mult, ALU.add))
                    v(stt(cR, xrp[:, 2:570], cw(2), cR, ALU.mult, ALU.add))
                    v(stt(xc[:, 0:SEQ], xrp[:, 3:3 + SEQ], cw(3), cR[:, 0:SEQ], ALU.mult, ALU.add))
                    stt(xc[:, SEQ:T].rearrange("p (b c) -> p b c", b=DB), xs[:, :, 3:7], cw(3), per7,
                          ALU.mult, ALU.add).then_inc(sem("conv_done"), up("conv_done", (l, j)))
                    ve.wait_ge(sem("conv_done"), now("conv_done"))
                    if j == 0:
                        copy_params((4, 5))
                    oc = outr[:, 0:12].rearrange("p (w j) -> p w j", w=3)
                    if j == 0 and l:
                        ve.wait_ge(sem("states_turned"), after("states_turned", (l - 1, 5)))
                    v(cp(oc[:, :, j], xrp[:, SEQ:SEQ + 3]))
                    oc = outr[:, 48:144].rearrange("p (b w j) -> p b w j", b=DB, w=3)
                    v(cp(oc[:, :, :, j], xs[:, :, 4:7]))
                    ve.wait_ge(sem("t_ready"), after("t_ready", (l, j)))
                    v(tsc(recR, tR, -1.0, 1.0, ALU.mult, ALU.add))
                    v(V.reciprocal(recR, recR))
                    tt(tR, tR, recR, ALU.mult).then_inc(sem("f_ready"), up("f_ready", (l, j)))
                    ve.wait_ge(sem("f_ready"), now("f_ready"))
                    v(stt(iR, iR, 1.0, xc, ALU.add, ALU.mult))
                    ve.wait_ge(sem("s_ready"), after("s_ready", (l, j)))
                    v(tt(iR, iR, rt, ALU.mult))
                    a0 = aR[:, SEQ:T].rearrange("p (b c) -> p b c", b=DB)[:, :, 0]
                    b0 = iR[:, SEQ:T].rearrange("p (b c) -> p b c", b=DB)[:, :, 0]
                    v(tt(sm[:, 100:108], a0, h0[:, :, j], ALU.mult))
                    v(tt(b0, b0, sm[:, 100:108], ALU.add))
                    v(V.memset(a0, 0.0))
                    v(V.tensor_tensor_scan(hR, aR, iR, 0.0, ALU.mult, ALU.add))
                    v(cp(outr[:, 12 + j:13 + j], hR[:, SEQ - 1:SEQ]))
                    oh = outr[:, 16:48].rearrange("p (b j) -> p b j", b=DB)
                    v(cp(oh[:, :, j], hR[:, SEQ:T].rearrange("p (b c) -> p b c", b=DB)[:, :, 3]))
                    ve.wait_ge(sem("gate_ready"), after("gate_ready", (l, j)))
                    tt(yT[:, j, :], hR, gR, ALU.mult).then_inc(sem("y_ready"), up("y_ready", (l, j)))
                    ve.wait_ge(sem("y_ready"), now("y_ready"))
                ve.wait_ge(sem("pe_row"), after("pe_row", l))
                cp(sm_row[:, 0:2 * P], pst[0:1, psk((l, "pe")), 0:2 * P]).then_inc(sem("pe_row_copied"), up("pe_row_copied", l, frees=[("psum", (l, "pe"))]))
                ve.wait_ge(sem("pe_row_copied"), now("pe_row_copied"))
                ve.wait_ge(sem("tables_loaded"), after("tables_loaded", 0))
                t1, t2 = sS[:, 0:T], sS[:, T:2 * T]
                for g in range(GR):
                    ve.wait_ge(sem("projected"), after("projected", (l, "rot", g)))
                    b = psk((l, "rot", g))
                    v(tt(t1, qcT[:, g, :], cosT, ALU.mult))
                    tt(halves(t2), pair(b), halves(sinT), ALU.mult).then_inc(sem("vector_step"), up("vector_step", frees=[("psum", (l, "rot", g))]))
                    ve.wait_ge(sem("vector_step"), now("vector_step"))
                    tt(qrT[:, g, :], t1, t2, ALU.add).then_inc(sem("q_roped"), up("q_roped", (l, g)))
                    ve.wait_ge(sem("q_roped"), now("q_roped"))
                ve.wait_ge(sem("pe_summed"), after("pe_summed", l))
                b = psk((l, "pec"))
                tt(sm[:, 140:142], pst[:, b, 0:2], par[:, P_B1:P_B1 + 2], ALU.add).then_inc(sem("b1_ready"), up("b1_ready", l, frees=[("psum", (l, "pec"))]))
                ve.wait_ge(sem("b1_ready"), now("b1_ready"))
                ve.wait_ge(sem("ov2_zeroed"), after("ov2_zeroed", l))
                for h in range(2):
                    for c, q in ((0, qcT), (1, qrT)):
                        hr = slice(h * HD, (h + 1) * HD)
                        for g in range(GR):
                            dst = qbd[hr, c, :, h * 16 + 4 * g:h * 16 + 4 * g + 4]
                            cp(dst, q[hr, g, SEQ:T].rearrange("p (b t) -> p b t", b=DB)).then_inc(sem("qbd_built" if (h, c, g) == (1, 1, 3) else "vector_step"), up("qbd_built" if (h, c, g) == (1, 1, 3) else "vector_step", l if (h, c, g) == (1, 1, 3) else None))
                            ve.wait_ge(sem("qbd_built" if (h, c, g) == (1, 1, 3) else "vector_step"), now("qbd_built" if (h, c, g) == (1, 1, 3) else "vector_step"))
                for n in "sw":
                    ve.wait_ge(sem("projected"), after("projected", (l, "kv", n + "0")))
                    b = psk((l, "kv", n + "0"))
                    for m, t0, t1_ in ((P, 0, 4), (NS, 4, 5)):
                        nt = t1_ - t0
                        x = flat(b, 640)[0:m, t0 * P:t1_ * P].rearrange("p (t h d) -> p t h d", t=nt, h=2)
                        A = sS[0:m, 0:nt * P].rearrange("p (t h d) -> p t h d", t=nt, h=2)
                        Bb = sS[0:m, 512:512 + nt * P].rearrange("p (t h d) -> p t h d", t=nt, h=2)
                        for h in range(2):
                            v(tt(A[:, :, h], x[:, :, h], cosk[0:m, t0:t1_, :], ALU.mult))
                            v(tt(Bb[:, :, h, 0:32], x[:, :, h, 32:64], sink[0:m, t0:t1_, 0:32], ALU.mult))
                            v(tt(Bb[:, :, h, 32:64], x[:, :, h, 0:32], sink[0:m, t0:t1_, 32:64], ALU.mult))
                        dst = kvt[n][0:m, t0:t1_, 0:P]
                        A2 = sS[0:m, 0:nt * P].rearrange("p (t c) -> p t c", t=nt)
                        B2 = sS[0:m, 512:512 + nt * P].rearrange("p (t c) -> p t c", t=nt)
                        tt(dst, A2, B2, ALU.add).then_inc(sem("k_roped" if nt == 1 else "vector_step"), up("k_roped" if nt == 1 else "vector_step", (l, n) if nt == 1 else None, frees=[("psum", (l, "kv", n + "0"))] if nt == 1 else []))
                        ve.wait_ge(sem("k_roped" if nt == 1 else "vector_step"), now("k_roped" if nt == 1 else "vector_step"))
                ve.wait_ge(sem("gates_tanh"), after("gates_tanh", l))
                v(tsc(gates[:, 0:4, :], gates[:, 0:4, :], 0.5, 0.5, ALU.mult, ALU.add))
                tsc(gates[0:NS, 4, :], gates[0:NS, 4, :], 0.5, 0.5, ALU.mult, ALU.add).then_inc(sem("gates_ready"), up("gates_ready", l))
                ve.wait_ge(sem("gates_ready"), now("gates_ready"))
                ve.wait_ge(sem("gates_spread"), after("gates_spread", l))
                b = psk((l, "gsel"))
                for G in range(2):
                    x = pst[:, b, 24 * G:24 * G + 24].rearrange("p (n c) -> p c n", c=3)
                    tmp = sm[:, 100:124].rearrange("p (c n) -> p c n", c=3)
                    tt(tmp, x, cst[:, K_PICK:K_PICK + 24].rearrange("p (c n) -> p c n", c=3), ALU.mult).then_inc(sem("vector_step"), up("vector_step", frees=[("psum", (l, "gsel"))]))
                    ve.wait_ge(sem("vector_step"), now("vector_step"))
                    v(V.tensor_reduce(gs[:, G, :], tmp, AX.X, ALU.add))

                def sample_cmp(part, G):
                    if part == "scores":
                        ve.wait_ge(sem("scored"), after("scored", (l, G, "cs")))
                        b = psk((l, G, "Scs"))
                        V.tensor_reduce(sm[:, 40 + G:41 + G], pst[:, b, 0:127], AX.X, ALU.max, negate=True).then_inc(sem("neg_max"), up("neg_max", (l, G, "cs")))
                        ve.wait_ge(sem("neg_max"), now("neg_max"))
                    elif part == "group":
                        ve.wait_ge(sem("p_exp"), after("p_exp", (l, G, "cs")))
                        v(tsc(sm[:, 44:45], sm[:, 42 + G:43 + G], 1e-30, None, ALU.max))
                        v(V.reciprocal(sm[:, 45:46], sm[:, 44:45]))
                        tsc(cmp_p, cmp_p, sm[:, 45:46], None, ALU.mult).then_inc(sem("pn_ready"), up("pn_ready", (l, G)))
                        ve.wait_ge(sem("pn_ready"), now("pn_ready"))
                        ve.wait_ge(sem("group_summed"), after("group_summed", (l, G)))
                        b = psk((l, G, "gsum"))
                        cp(pp[:, 1:128], pst[:, b, 0:127]).then_inc(sem("vector_step"), up("vector_step", frees=[("psum", (l, G, "gsum"))]))
                        ve.wait_ge(sem("vector_step"), now("vector_step"))
                        sc = sm[:, 100:133]
                        v(V.tensor_reduce(sc, pp[:, 0:132].rearrange("p (n r) -> p n r", r=4), AX.X, ALU.add))
                        v(tt(sc, sc, pp[:, 4:136].rearrange("p (n r) -> p n r", r=4)[:, :, 0], ALU.add))
                        v(V.memset(sm[:, 100:101], BIG))
                        v(V.memset(sm[:, 131:133], BIG))
                        for r in range(2):
                            v(V.max(sm[:, 80:88], sc))
                            v(V.match_replace(sc, sm[:, 80:88], sc, -1.0))
                        tsc(mb(G), sc, 0.0, -BIG, ALU.is_ge, ALU.mult).then_inc(sem("selected"), up("selected", (l, G)))
                        ve.wait_ge(sem("selected"), now("selected"))
                    else:
                        copy_ts((l, G, "cs"), P, 127)
                        ve.wait_ge(sem("summed_values"), after("summed_values", (l, G, "cs")))
                        b = psk((l, G, "Ocs"))
                        tsc(comb[:, G, :], pst[:, b, 0:P], gs[:, G, 0:1], None, ALU.mult).then_inc(sem("vector_step"), up("vector_step", frees=[("psum", (l, G, "Ocs"))]))
                        ve.wait_ge(sem("vector_step"), now("vector_step"))

                def second_layer(u):
                    if u[1] == "cmpp":
                        ve.wait_ge(sem("hidden"), after("hidden", (u, 1)))
                        cp(hidrep[:, :, :].rearrange("p h (r c) -> p h r c", r=4),
                             hid_of(u, 1).unsqueeze(2).broadcast_to([P, 2, 4, NCP])).then_inc(sem("hidden_rep"), up("hidden_rep", (u, 1)))
                        ve.wait_ge(sem("hidden_rep"), now("hidden_rep"))
                    for vv in range(2):
                        ve.wait_ge(sem("compressed2"), after("compressed2", (u, vv)))
                        b = psk((u, "c2", vv))
                        fr = [("psum", (u, "c2", vv))]
                        if u[1] == "cmp":
                            if vv == 0:
                                cp(kcT[:, u[2], :], pst[:, b, 0:127]).then_inc(sem("copied_v"), up("copied_v", (u, "kc"), frees=fr))
                                ve.wait_ge(sem("copied_v"), now("copied_v"))
                            else:
                                cp(vc[0:127, u[2], :], pst[0:127, b, 0:P]).then_inc(sem("copied_v"), up("copied_v", (u, "vc"), frees=fr))
                                ve.wait_ge(sem("copied_v"), now("copied_v"))
                        elif vv == 0:
                            cp(kcTp[:, :], pst[:, b, 0:32]).then_inc(sem("vector_step"), up("vector_step", frees=fr))
                            ve.wait_ge(sem("vector_step"), now("vector_step"))
                        else:
                            for g in range(4):
                                cp(vbd[32 * g:32 * g + 32, :, g, :], pst[32 * g:32 * g + 32, b, 0:P].rearrange("p (h d) -> p h d", h=2)).then_inc(sem("vbd_built" if g == 3 else "vector_step"), up("vbd_built" if g == 3 else "vector_step", l if g == 3 else None, frees=fr if g == 3 else []))
                                ve.wait_ge(sem("vbd_built" if g == 3 else "vector_step"), now("vbd_built" if g == 3 else "vector_step"))

                v(V.memset(pp[:, :], 0.0))
                us = compressed_units(l)
                for x, u in enumerate(us):
                    nch = NCH if u[1] == "cmp" else NCP
                    for vv in range(2):
                        for s4 in (0, 2):
                            copy_ts((u, "xt", vv, s4), 4 * nch)
                            if (vv, s4) == (0, 0) and x:
                                second_layer(us[x - 1])
                            if s4 == 0:
                                n = load_no[u]
                                xn = 8 * (l * len(us) + x) + 4 * vv + 3
                                ve.wait_ge(sem(f"a_loaded{n % NA}"), after(f"a_loaded{n % NA}", n))
                                for s, n_ in freed(("xs", xn - 2)):
                                    ve.wait_ge(s, n_)
                                for e in range(2):
                                    dst, src = rearranged(u, vv, 3, e, xn)
                                    cp(dst, src).then_inc(sem("rearranged_v" if e else "vector_step"), up("rearranged_v" if e else "vector_step", (u, vv, 3) if e else None, frees=[("a", n)] if e and vv else []))
                                    ve.wait_ge(sem("rearranged_v" if e else "vector_step"), now("rearranged_v" if e else "vector_step"))
                    if x == len(us) - 1:
                        second_layer(u)
                    if x in CMP_PARTS:
                        sample_cmp(*CMP_PARTS[x])

                def p_max(n):
                    u = todo[n]
                    i = u[0]
                    L = (i + 1) * P
                    ve.wait_ge(sem("scored"), after("scored", (l, u)))
                    b = psk((l, u, "S"))
                    dg = pst[:, b:b + 2, L - P:L]
                    v(tt(dg, dg, cst[:, K_CAUS:K_CAUS + P].unsqueeze(1).broadcast_to([P, 2, P]), ALU.add))
                    if n >= 4:
                        for s, n_ in freed(("nm", l, n - 4)):
                            ve.wait_ge(s, n_)
                    m = 48 + 2 * (n % 4)
                    V.tensor_reduce(sm[:, m:m + 2], pst[:, b:b + 2, 0:L], AX.X, ALU.max, negate=True).then_inc(sem("neg_max"), up("neg_max", (l, u)))
                    ve.wait_ge(sem("neg_max"), now("neg_max"))

                sc3 = pc_s.rearrange("p (n c) -> p n c", n=8)
                pc3 = pc_p.rearrange("p (n c) -> p n c", n=8)

                def cmp_shift(i):
                    cm = cst[:, K_CMPM + i * NCP:K_CMPM + (i + 1) * NCP]
                    ve.wait_ge(sem("scored"), after("scored", (l, i, "c")))
                    b = psk((l, i, "Sc"))
                    x = pst[:, b:b + 2, 0:P].rearrange("p h (n c) -> p h n c", n=4)
                    tt(pc_s.rearrange("p (h n c) -> p h n c", h=2, n=4), x,
                         cm.unsqueeze(1).unsqueeze(1).broadcast_to([P, 2, 4, NCP]), ALU.add).then_inc(sem("vector_step"), up("vector_step", frees=[("psum", (l, i, "Sc"))]))
                    ve.wait_ge(sem("vector_step"), now("vector_step"))
                    v(V.tensor_reduce(sm[:, 100:108], sc3, AX.X, ALU.max))
                    v(tsc(sm[:, 100:108], sm[:, 100:108], -0.1 * BIG, None, ALU.max))
                    tt(sc3, sc3, sm[:, 100:108].unsqueeze(2).broadcast_to([P, 8, NCP]), ALU.subtract).then_inc(sem("cmp_shifted"), up("cmp_shifted", (l, i)))
                    ve.wait_ge(sem("cmp_shifted"), now("cmp_shifted"))

                def gated(i, br):
                    gt = gates[:, i, :].rearrange("p (h g c) -> p g h c", h=2, g=GR)
                    gh = lambda ap: ap.rearrange("p (g h) -> p g h", g=GR)
                    heads = lambda ap: ap.rearrange("p (n d) -> p n d", n=8)
                    if br == "c":
                        v(V.tensor_reduce(sm[:, 108:116], pc3, AX.X, ALU.add))
                        v(tsc(gh(sm[:, 124:132]), sm[:, 108:116].rearrange("p (h g) -> p g h", h=2), 1e-30, None, ALU.max))
                        lcol = sm[:, 124:132]
                        ve.wait_ge(sem("summed_values"), after("summed_values", (l, i, "c")))
                    else:
                        lc = 176 + 16 * (i % 2) + (0 if br == "s" else 8)
                        lcol = sm[:, lc:lc + 8]
                        ve.wait_ge(sem("summed_values"), after("summed_values", (l, (i, br, 3), 1)))
                    V.reciprocal(sm[:, 116:124], lcol).then_inc(sem("l_read" if br == "w" else "vector_step"), up("l_read" if br == "w" else "vector_step", (l, i) if br == "w" else None))
                    ve.wait_ge(sem("l_read" if br == "w" else "vector_step"), now("l_read" if br == "w" else "vector_step"))
                    v(tt(gh(sm[:, 116:124]), gh(sm[:, 116:124]), gt[:, :, :, "csw".index(br)], ALU.mult))
                    cf = sm[:, 116:124].unsqueeze(2).broadcast_to([P, 8, HD])
                    if br == "c" and i:
                        ve.wait_ge(sem("o_turned"), after("o_turned", (l, i - 1)))
                    tt(heads(o_sb if br == "c" else o_tmp), heads(pst[:, psk((l, i, br, "O")), :]), cf, ALU.mult).then_inc(sem("vector_step"), up("vector_step", frees=[("psum", (l, i, br, "O"))]))
                    ve.wait_ge(sem("vector_step"), now("vector_step"))
                    if br != "c":
                        tt(o_sb, o_sb, o_tmp, ALU.add).then_inc(sem("o_gated" if br == "w" else "vector_step"), up("o_gated" if br == "w" else "vector_step", (l, i) if br == "w" else None))
                        ve.wait_ge(sem("o_gated" if br == "w" else "vector_step"), now("o_gated" if br == "w" else "vector_step"))

                def copy_o(i):
                    ve.wait_ge(sem("o_turned"), after("o_turned", (l, i)))
                    b = psk((l, i, "oT"))
                    cp(hT[:, 0:4, i * P:(i + 1) * P], pst[:, b, :].rearrange("p (g q) -> p g q", g=4)).then_inc(sem("oT_copied"), up("oT_copied", (l, i), frees=[("psum", (l, i, "oT"))]))
                    ve.wait_ge(sem("oT_copied"), now("oT_copied"))

                def sample_part(part, k, G, e):
                    u = (l, "win", G) if e is None else (l, "pair", G, e)
                    nm = cst[:, K_NEWM + G * NS:K_NEWM + (G + 1) * NS]

                    def copy_keys(x, n):
                        n += 40 * l + FIRST_KEY[k]
                        ve.wait_ge(sem("turned"), after("turned", (u, "kt", x, 0)))
                        if n >= NKS:
                            for s, n_ in freed(("ks", n - NKS)):
                                ve.wait_ge(s, n_)
                        cp(key_slot(n), bank(psk((u, "kt", x, 0)))).then_inc(sem("copied_v"), up("copied_v", (u, "kt", x, 0), frees=[("psum", (u, "kt", x, 0))]))
                        ve.wait_ge(sem("copied_v"), now("copied_v"))

                    r = slice(0, P) if e is None else slice(32 * e, 32 * e + 64)
                    if e is None and part in ("keys0", "keys1"):
                        x = 0 if part == "keys0" else 2
                        copy_keys(x, x)
                    elif e is not None and part in ("keys0", "keys1", "keys2", "keys3"):
                        x = int(part[4])
                        copy_keys(x, 2 * x)
                        if x == 2:
                            if G:
                                ve.wait_ge(sem("turned"), after("turned", ((l, "pair", 0, e), "ptn")))
                            masked(u, 0, r, G)
                    elif part == "keys4":
                        masked(u, 2, r, G)
                        ve.wait_ge(sem("scored"), after("scored", (u, "n")))
                        tt(sQ[r, 2048:2080], pst[r, psk((u, "Sn")), 0:NS], nm[r, :], ALU.add).then_inc(sem("vector_step"), up("vector_step", frees=[("psum", (u, "Sn"))]))
                        ve.wait_ge(sem("vector_step"), now("vector_step"))
                        V.tensor_reduce(sm[r, 89:90], sQ[r, :], AX.X, ALU.max, negate=True).then_inc(sem("neg_max"), up("neg_max", u))
                        ve.wait_ge(sem("neg_max"), now("neg_max"))
                    elif part == "keys3":
                        ve.wait_ge(sem("scored"), after("scored", (u, 3, "n")))
                        if G:
                            ve.wait_ge(sem("turned"), after("turned", ((l, "win", 0), "ptn")))
                        cp(sW[:, 0:512], bank(psk((u, "S", 0)))).then_inc(sem("vector_step"), up("vector_step", frees=[("psum", (u, "S", 0))]))
                        ve.wait_ge(sem("vector_step"), now("vector_step"))
                        w0 = sW[:, 0:512].rearrange("p (s c) -> p s c", s=4)[:, :, 0]
                        v(tt(w0, w0, cst[:, K_WINM:K_WINM + 4], ALU.add))
                        tt(sW[:, 512:544], pst[:, psk((u, "Sn")), 0:NS], nm, ALU.add).then_inc(sem("vector_step"), up("vector_step", frees=[("psum", (u, "Sn"))]))
                        ve.wait_ge(sem("vector_step"), now("vector_step"))
                        V.tensor_reduce(sm[:, 88:89], sW[:, :], AX.X, ALU.max, negate=True).then_inc(sem("neg_max"), up("neg_max", u))
                        ve.wait_ge(sem("neg_max"), now("neg_max"))
                    elif part == "turn":
                        if k:
                            for s, n_ in freed(("pt", l, k - 1)):
                                ve.wait_ge(s, n_)
                        ve.wait_ge(sem("turned"), after("turned", (u, "pt", 0)))
                        cp(probs[:, 0:512], bank(psk((u, "pt", 0)))).then_inc(sem("copied_v"), up("copied_v", (u, "pt", 0), frees=[("psum", (u, "pt", 0))]))
                        ve.wait_ge(sem("copied_v"), now("copied_v"))
                        ve.wait_ge(sem("turned"), after("turned", (u, "ptn")))
                        m = P if e is None else 64
                        cp(probs_new[0:NS, 0:m], pst[0:NS, psk((u, "ptn")), 0:m]).then_inc(sem("copied_v"), up("copied_v", (u, "ptn"), frees=[("psum", (u, "ptn"))]))
                        ve.wait_ge(sem("copied_v"), now("copied_v"))
                    elif part == "values":
                        if e is None:
                            v(tt(sm[:, 96:97], sm[:, 90:91], sm[:, 91:92], ALU.add))
                            v(V.reciprocal(sm[:, 97:98], sm[:, 96:97]))
                        else:
                            v(V.reciprocal(sm[r, 97:98], sm[r, 92:93]))
                        br = 2 if e is None else 1
                        v(tt(sm[r, 97:98], sm[r, 97:98], gs[r, G, br:br + 1], ALU.mult))
                        ve.wait_ge(sem("summed_values"), after("summed_values", (u, 0)))
                        stt(comb[r, G, :], pst[r, psk((u, "O")), 0:P], sm[r, 97:98], comb[r, G, :], ALU.mult, ALU.add).then_inc(sem("vector_step"), up("vector_step", frees=[("psum", (u, "O"))]))
                        ve.wait_ge(sem("vector_step"), now("vector_step"))
                        if e == 2:
                            tt(comb[:, G, :], comb[:, G, :], cst[:, K_HM:K_HM + P], ALU.mult).then_inc(sem("comb_ready"), up("comb_ready", (l, G)))
                            ve.wait_ge(sem("comb_ready"), now("comb_ready"))
                    elif part == "output":
                        ve.wait_ge(sem("o_turned"), after("o_turned", (l, "s", G)))
                        b = psk((l, G, "oTs"))
                        for h in range(2):
                            hr = slice(h * HD, (h + 1) * HD)
                            for g in range(GR):
                                src = pst[hr, b, 0:P].rearrange("p (b h g t) -> p b h g t", b=4, h=2, g=4)[:, :, h, g, :]
                                dst = hT[hr, g, SEQ + 16 * G:SEQ + 16 * G + 16].rearrange("p (b t) -> p b t", b=4)
                                last = (h, g) == (1, 3)
                                cp(dst, src).then_inc(sem("oT_copied" if last else "vector_step"), up("oT_copied" if last else "vector_step", (l, "s", G) if last else None, frees=[("psum", (l, G, "oTs"))] if last else []))
                                ve.wait_ge(sem("oT_copied" if last else "vector_step"), now("oT_copied" if last else "vector_step"))

                ve.wait_ge(sem("gates_spread"), after("gates_spread", l))
                for who_, what, n in plan:
                    if who_ == "sample":
                        sample_part(what, *n)
                    elif who_ == "sample_cmp":
                        sample_cmp(what, n)
                    elif who_ == "tile":
                        if what == "scores":
                            cmp_shift(n)
                        elif what == "turn":
                            copy_ts((l, n, "c"), 256)
                        elif what == "values":
                            gated(n, "c")
                        elif what == "output":
                            copy_o(n)
                    elif what == "scores":
                        p_max(n)
                    elif what == "turn":
                        copy_ts((l, todo[n], 0), (todo[n][0] + 1) * P)
                    elif n % 4 == 3:
                        gated(*todo[n][0:2])
                post(l, 1, P_NORM + 8)
                pre(l, 2, P_NORM + 16)
                for r in range(RND):
                    for f in range(r * FR, (r + 1) * FR):
                        gp = gpad[f % 2]
                        ve.wait_ge(sem("g_copied"), after("g_copied", (l, f)))
                        ve.wait_ge(sem("prefix_copied"), after("prefix_copied", (l, f)))
                        if f:
                            ve.wait_ge(sem("gelu_done"), after("gelu_done", (l, f - 1)))
                        cw = lambda k: par[:, P_FCW + FT * k + f:P_FCW + FT * k + f + 1]
                        v(tsc(cF, gp[:, 0:560], cw(0), par[:, P_FCB + f:P_FCB + f + 1], ALU.mult, ALU.add))
                        v(stt(cF, gp[:, 1:561], cw(1), cF, ALU.mult, ALU.add))
                        stt(cF, gp[:, 2:562], cw(2), cF, ALU.mult, ALU.add).then_inc(sem("conv_done"), up("conv_done", (l, "f", f)))
                        ve.wait_ge(sem("conv_done"), now("conv_done"))
                        ve.wait_ge(sem("gelu_done"), after("gelu_done", (l, f)))
                        ve.wait_ge(sem("projected"), after("projected", (l, "u", f)))
                        if r:
                            ve.wait_ge(sem("projected"), after("projected", (l, "down", r - 1, KT - 1)))
                        b = psk((l, "u", f))
                        tt(halves(actT[:, f % FR, :]), pair(b), halves(gF), ALU.mult).then_inc(sem("act_ready"), up("act_ready", (l, f), frees=[("psum", (l, "u", f))]))
                        ve.wait_ge(sem("act_ready"), now("act_ready"))
                    if r:
                        for j in range(KT):
                            ve.wait_ge(sem("projected"), after("projected", (l, "down", r, j)))
                            b = psk((l, "down", r, j))
                            if r == 1 and j == 0:
                                ve.wait_ge(sem("m_copied"), after("m_copied", (l, KT - 1)))
                            tt(halves(mT[:, j, :]), pair(b), halves(mT[:, j, :]), ALU.add).then_inc(sem("m_summed"), up("m_summed", (l, r, j), frees=[("psum", (l, "down", r, j))]))
                            ve.wait_ge(sem("m_summed"), now("m_summed"))
                post(l, 3, P_NORM + 24)
            ve.wait_ge(sem("states_copied"), after("states_copied", (DEPTH - 1, 5)))
            for k in range(0, KT, 2):
                ve.wait_ge(sem("y_turned"), after("y_turned", k))
                b = psk(("y", k))
                v(cp(yout[:, :, k * P:(k + 1) * P], bank(b).rearrange("p (t c) -> p t c", t=4)))
                cp(youts[:, k * P:(k + 1) * P], pst[0:NS, b + 1, 0:P]).then_inc(sem("y_copied_v"), up("y_copied_v", k, frees=[("psum", ("y", k))]))
                ve.wait_ge(sem("y_copied_v"), now("y_copied_v"))
        return S

_INS = ["x_prompt", "x_sample", "cache_cmp_kv", "cache_slc_kv", "cache_win_kv", "state_rg_h", "state_rg_conv",
        "state_ffn_conv", "page_table", "norm_mix_pre", "norm_mix_post", "norm_ffn_pre", "norm_ffn_post", "w_in",
        "rg_conv_w", "rg_conv_b", "rg_wa", "rg_ba", "rg_wx", "rg_bx", "rg_lambda", "cmpk_pe", "cmpk_w1", "cmpk_b1",
        "cmpk_w2", "cmpv_pe", "cmpv_w1", "cmpv_b1", "cmpv_w2", "w_out", "ffn_w_in", "ffn_conv_w", "ffn_conv_b",
        "ffn_w_down"]
_KV = (2, NKV, HD)
_OUTS = {"y_p": (1, SEQ, D), "y_s": (DB, DT, D), "p_cmp": (DEPTH, 1, SEQ) + _KV, "s_cmp": (DEPTH, DB, DT) + _KV,
         "p_slc": (DEPTH, 1, SEQ) + _KV, "s_slc": (DEPTH, DB, DT) + _KV, "p_win": (DEPTH, 1, WIN) + _KV,
         "s_win": (DEPTH, DB, WIN) + _KV, "p_rgh": (DEPTH, 1, DR), "s_rgh": (DEPTH, DB, DR),
         "p_rgc": (DEPTH, 1, 3, DR), "s_rgc": (DEPTH, DB, 3, DR), "p_ffc": (DEPTH, 1, 2, DF), "s_ffc": (DEPTH, DB, 2, DF)}

def kernel(**inputs):
    import concourse.bacc as bacc
    from concourse.bass_utils import run_bass_kernel_spmd

    arrays = {f"in_{n}": np.ascontiguousarray(inputs[n]) for n in _INS}
    arrays["in_consts"] = constants()

    def build(known):
        nc = bacc.Bacc("TRN2", target_bir_lowering=False, num_devices=1)
        ins = {n[3:]: nc.dram_tensor(n, a.shape, mybir.dt.from_np(a.dtype), kind="ExternalInput").ap()
               for n, a in arrays.items()}
        outs = {n: nc.dram_tensor(f"out_{n}", shape, F32, kind="ExternalOutput").ap() for n, shape in _OUTS.items()}
        return nc, hybrid_step(nc, ins, outs, known)

    _, counts = build(None)
    nc, _ = build(counts)
    r = run_bass_kernel_spmd(nc, [arrays], core_ids=[0])
    return tuple(r.results[0][f"out_{n}"] for n in _OUTS)
```
